# Optimizing a Trainium2 kernel written in Bass

```python
import jax, jax.numpy as jnp
from jax import lax
import numpy as np

D_MODEL = 1024
BATCH = 1
SEQ = 512
DEPTH = 1

LRU_WIDTH = D_MODEL
LRU_BLOCKS = 8
LRU_BLOCK_W = LRU_WIDTH // LRU_BLOCKS
LRU_CONV = 4
LRU_C = 8.0
HG_EXPAND = 128
HG_HEADS = D_MODEL // HG_EXPAND
HG_KDIM = HG_HEADS * HG_EXPAND
HG_VHEAD = D_MODEL // HG_HEADS
HG_VDIM = HG_HEADS * HG_VHEAD
HG_CHUNK = 32
D_FF = 2816
FFN_CONV = 3
EPS = 1e-6
IN_SPLITS = (LRU_WIDTH, LRU_WIDTH, HG_KDIM, HG_KDIM, HG_VDIM, HG_VDIM, D_MODEL, D_MODEL)
D_IN = LRU_WIDTH * 2 + HG_KDIM * 2 + HG_VDIM * 2 + D_MODEL * 2

kernel_name = "hybrid_rglru_hgrn2_convffn"

def rmsnorm(x, g):
    xf = x.astype(jnp.float32)
    y = xf * lax.rsqrt(jnp.mean(xf * xf, axis=-1, keepdims=True) + EPS)
    return (y * g.astype(jnp.float32)).astype(x.dtype)

def causal_dwconv(x, w, b):
    k = w.shape[0]
    y = lax.conv_general_dilated(
        x, w[:, None, :].astype(x.dtype), window_strides=(1,), padding=[(k - 1, 0)],
        dimension_numbers=("NWC", "WIO", "NWC"), feature_group_count=x.shape[-1])
    return y + b.astype(x.dtype)

def rg_lru(x, w_a, b_a, w_x, b_x, lam):
    bsz, t, _ = x.shape
    xb = x.astype(jnp.float32).reshape(bsz, t, LRU_BLOCKS, LRU_BLOCK_W)
    r = jax.nn.sigmoid(jnp.einsum("btnd,nde->btne", xb, w_a.astype(jnp.float32))
                       + b_a.astype(jnp.float32).reshape(LRU_BLOCKS, LRU_BLOCK_W))
    i = jax.nn.sigmoid(jnp.einsum("btnd,nde->btne", xb, w_x.astype(jnp.float32))
                       + b_x.astype(jnp.float32).reshape(LRU_BLOCKS, LRU_BLOCK_W))
    log_a = -LRU_C * r * jax.nn.softplus(-lam.astype(jnp.float32)).reshape(LRU_BLOCKS, LRU_BLOCK_W)
    a = jnp.exp(log_a).reshape(bsz, t, LRU_WIDTH)
    u = (jnp.sqrt(-jnp.expm1(2.0 * log_a)) * i * xb).reshape(bsz, t, LRU_WIDTH)

    def combine(left, right):
        a_l, h_l = left
        a_r, h_r = right
        return a_l * a_r, a_r * h_l + h_r

    _, h = lax.associative_scan(combine, (a, u), axis=1)
    return h

def hgrn2(q, fz, v, lb):
    bsz, t, _ = q.shape
    n = t // HG_CHUNK
    q = q.astype(jnp.float32)
    fz = fz.astype(jnp.float32)
    v = v.astype(jnp.float32)
    f = lb + (1.0 - lb) * jax.nn.sigmoid(fz)
    log_f = jnp.log(f)
    k = (1.0 - lb) * jax.nn.sigmoid(-fz)

    def chunks(z, d):
        return z.reshape(bsz, n, HG_CHUNK, HG_HEADS, d).transpose(0, 1, 3, 2, 4)

    qc, kc, gc = chunks(q, HG_EXPAND), chunks(k, HG_EXPAND), chunks(log_f, HG_EXPAND)
    vc = chunks(v, HG_VHEAD)
    g_cum = jnp.cumsum(gc, axis=3)
    g_last = g_cum[:, :, :, -1:, :]
    q_t = qc * jnp.exp(g_cum)
    k_t = kc * jnp.exp(-g_cum)
    k_dec = kc * jnp.exp(g_last - g_cum)
    dec = jnp.exp(g_last[:, :, :, 0, :])

    causal = jnp.tril(jnp.ones((HG_CHUNK, HG_CHUNK), dtype=bool))
    att = jnp.where(causal, jnp.einsum("bnhcd,bnhsd->bnhcs", q_t, k_t), 0.0)
    o_intra = jnp.einsum("bnhcs,bnhse->bnhce", att, vc)

    def step(s, xs):
        q_c, kd_c, v_c, d_c = xs
        o = jnp.einsum("bhcd,bhde->bhce", q_c, s)
        s = s * d_c[..., None] + jnp.einsum("bhcd,bhce->bhde", kd_c, v_c)
        return s, o

    s0 = jnp.zeros((bsz, HG_HEADS, HG_EXPAND, HG_VHEAD), jnp.float32)
    _, o_inter = lax.scan(step, s0, (jnp.moveaxis(q_t, 1, 0), jnp.moveaxis(k_dec, 1, 0),
                                     jnp.moveaxis(vc, 1, 0), jnp.moveaxis(dec, 1, 0)))
    o = o_intra + jnp.moveaxis(o_inter, 0, 1)
    return o.transpose(0, 1, 3, 2, 4).reshape(bsz, t, HG_HEADS, HG_VHEAD)

def setup_inputs(seed: int = 0) -> dict:
    key = jax.random.key(seed)
    ks = jax.random.split(key, 24)
    f32 = jnp.float32

    def nrm(k, shape, fan_in):
        return jax.random.normal(k, shape, f32) * (fan_in ** -0.5)

    def gain(k, shape):
        return 1.0 + 0.02 * jax.random.normal(k, shape, f32)

    def bias(k, shape):
        return 0.02 * jax.random.normal(k, shape, f32)

    u = jax.random.uniform(ks[9], (DEPTH, LRU_WIDTH), f32, 0.9, 0.999)
    s = u ** (1.0 / LRU_C)
    lru_lambda = jnp.log(s) - jnp.log1p(-s)
    return {
        "x": jax.random.normal(ks[0], (BATCH, SEQ, D_MODEL), f32),
        "norm_pre_mix": gain(ks[1], (DEPTH, D_MODEL)),
        "w_in": nrm(ks[2], (DEPTH, D_MODEL, D_IN), D_MODEL),
        "conv_a_w": nrm(ks[3], (DEPTH, LRU_CONV, LRU_WIDTH), LRU_CONV),
        "conv_a_b": bias(ks[4], (DEPTH, LRU_WIDTH)),
        "lru_wa": nrm(ks[5], (DEPTH, LRU_BLOCKS, LRU_BLOCK_W, LRU_BLOCK_W), LRU_BLOCK_W),
        "lru_ba": bias(ks[6], (DEPTH, LRU_WIDTH)),
        "lru_wx": nrm(ks[7], (DEPTH, LRU_BLOCKS, LRU_BLOCK_W, LRU_BLOCK_W), LRU_BLOCK_W),
        "lru_bx": bias(ks[8], (DEPTH, LRU_WIDTH)),
        "lru_lambda": lru_lambda,
        "hg_lb_logits": 0.1 * jax.random.normal(ks[10], (DEPTH + 1, HG_KDIM), f32),
        "hg_norm_g": gain(ks[11], (DEPTH, HG_VDIM)),
        "w_branch_a": nrm(ks[12], (DEPTH, LRU_WIDTH, D_MODEL), LRU_WIDTH),
        "w_branch_b": nrm(ks[13], (DEPTH, HG_VDIM, D_MODEL), HG_VDIM),
        "w_out": nrm(ks[14], (DEPTH, D_MODEL, D_MODEL), D_MODEL),
        "norm_post_mix": gain(ks[15], (DEPTH, D_MODEL)),
        "norm_pre_ffn": gain(ks[16], (DEPTH, D_MODEL)),
        "w_up": nrm(ks[17], (DEPTH, D_MODEL, 2 * D_FF), D_MODEL),
        "conv_f_w": nrm(ks[18], (DEPTH, FFN_CONV, 2 * D_FF), FFN_CONV),
        "conv_f_b": bias(ks[19], (DEPTH, 2 * D_FF)),
        "w_down": nrm(ks[20], (DEPTH, D_FF, D_MODEL), D_FF),
        "norm_post_ffn": gain(ks[21], (DEPTH, D_MODEL)),
    }

def reference(x, norm_pre_mix, w_in, conv_a_w, conv_a_b, lru_wa, lru_ba, lru_wx, lru_bx,
              lru_lambda, hg_lb_logits, hg_norm_g, w_branch_a, w_branch_b, w_out,
              norm_post_mix, norm_pre_ffn, w_up, conv_f_w, conv_f_b, w_down, norm_post_ffn):
    bsz, t, _ = x.shape
    lb_all = jnp.cumsum(jax.nn.softmax(hg_lb_logits.astype(jnp.float32), axis=0), axis=0)
    split_idx = [int(v) for v in np.cumsum(IN_SPLITS)[:-1]]
    for l in range(DEPTH):
        h = rmsnorm(x, norm_pre_mix[l])
        p = h @ w_in[l].astype(h.dtype)
        xa, ga, q, fz, vi, og, gate_a, gate_b = jnp.split(p, split_idx, axis=-1)

        xa = causal_dwconv(xa, conv_a_w[l], conv_a_b[l])
        ya = rg_lru(xa, lru_wa[l], lru_ba[l], lru_wx[l], lru_bx[l], lru_lambda[l])
        ya = (ya * jax.nn.gelu(ga.astype(jnp.float32), approximate=True)).astype(x.dtype)

        ob = hgrn2(q, fz, vi, lb_all[l])
        ob = ob * lax.rsqrt(jnp.mean(ob * ob, axis=-1, keepdims=True) + EPS)
        ob = ob * hg_norm_g[l].astype(jnp.float32).reshape(HG_HEADS, HG_VHEAD)
        yb = (ob.reshape(bsz, t, HG_VDIM) * jax.nn.silu(og.astype(jnp.float32))).astype(x.dtype)

        za = ya @ w_branch_a[l].astype(ya.dtype)
        zb = yb @ w_branch_b[l].astype(yb.dtype)
        mix = jax.nn.sigmoid(gate_a) * za + jax.nn.sigmoid(gate_b) * zb
        x = x + rmsnorm(mix @ w_out[l].astype(mix.dtype), norm_post_mix[l])

        h2 = rmsnorm(x, norm_pre_ffn[l])
        up = causal_dwconv(h2 @ w_up[l].astype(h2.dtype), conv_f_w[l], conv_f_b[l])
        u_gate, u_val = jnp.split(up, 2, axis=-1)
        y = jax.nn.gelu(u_gate, approximate=True) * u_val
        x = x + rmsnorm(y @ w_down[l].astype(y.dtype), norm_post_ffn[l])
    return x


_drawn_inputs = setup_inputs


def setup_inputs(seed=0):
    import zlib

    import numpy as np

    out = dict(_drawn_inputs(seed))
    spreads = {}
    factors = {'lru_ba': 64.0,
     'lru_bx': 44.114,
     'hg_norm_g': 4.029,
     'norm_post_mix': 3.454,
     'norm_pre_ffn': 3.422,
     'conv_f_b': 3.471,
     'norm_post_ffn': 16.291}
    for name, (base, spread) in spreads.items():
        noise = np.random.default_rng([zlib.crc32(name.encode()), seed]).standard_normal(out[name].shape)
        drawn = base * np.exp(spread * noise) if base else spread * noise
        out[name] = __import__('jax').numpy.asarray(drawn.astype(out[name].dtype))
    for name, factor in factors.items():
        out[name] = (out[name] * factor).astype(out[name].dtype)
    return out
```

```python
from contextlib import ExitStack

import concourse.bass as bass
from concourse import mybir

F32 = mybir.dt.float32
F32R = mybir.dt.float32r
U32 = mybir.dt.uint32
ALU = mybir.AluOpType
ACT = mybir.ActivationFunctionType

P = 128
D = 1024
T = 512
KD = D // P
HEADS = KD
CH = 32
NCH = T // CH
NT = T // P
CPT = P // CH
FF = 2816
KF = FF // P
EPS = 1e-6
RING = 4
LEAD = 2

SECT = 6
N_HEAD = SECT * HEADS
N_MERGE = 4 * KD
N_OUT = KD
N_UP = 2 * KF
N_DOWN = KF
Q_MERGE = N_HEAD // RING
Q_OUT = Q_MERGE + N_MERGE // RING
Q_UP = Q_OUT + N_OUT // RING
Q_DOWN = Q_UP + N_UP // RING
N_TILES = N_HEAD + N_MERGE + N_OUT + N_UP + N_DOWN

HPC = 11
C_BA, C_BX, C_LAM, C_L0, C_L1, C_HG = 5, 6, 7, 8, 9, 10
O_PRE = HEADS * HPC
O_POST = O_PRE + KD
O_PREF = O_POST + KD
O_POSTF = O_PREF + KD
O_FFN = O_POSTF + KD
N_PAR = O_FFN + 4 * 2 * KF
C_C8, C_NC8, C_LB, C_OMLB = 0, 1, 2, 3

SET_SIG = "sigmoid_and_others"
SET_EXP = "natural_log_exp_and_others"
GELU_C = 0.044715
GELU_S = 0.7978845608028654


def layer(nc, xT, wts, par, lru, outT):
    ctx = ExitStack()
    with ctx:
        base = (nc.sbuf_base + 63) // 64 * 64
        top = [base]

        def at(name, shape, dt, offset):
            return nc.alloc_sbuf_tensor_at(name, shape, dt, offset=offset)

        def size(shape):
            n = 4
            for s in shape[1:]:
                n *= s
            return (n + 31) // 32 * 32

        def new(name, shape, dt=F32):
            t = at(name, shape, dt, top[0])
            top[0] += size(shape)
            return t

        def sem(name):
            return ctx.enter_context(nc.semaphore(name))

        w_raw = [new(f"w_raw{s}", [P, KD, P]) for s in range(RING)]
        w_hi = [new(f"w_hi{s}", [P, KD, P], F32R) for s in range(RING)]
        w_lo = [new(f"w_lo{s}", [P, KD, P], F32R) for s in range(RING)]
        pv = new("pv", [P, N_PAR])
        hc = new("hc", [P, HEADS, 4])
        hp_now = [new(f"hp_now{s}", [P, HPC]) for s in range(2)]
        hc_now = [new(f"hc_now{s}", [P, 4]) for s in range(2)]
        fp_now = [new(f"fp_now{s}", [P, 8]) for s in range(2)]
        eps_col = new("eps_col", [P, 2])
        ones = new("ones", [P, P])
        ident = new("ident", [P, P])
        amask = new("amask", [P, P])
        lru_w = [new(f"lru_w{s}", [P, 2, P]) for s in range(2)]
        dec = new("dec", [P, NCH])
        sp_t = new("sp_t", [P, 8, HEADS])
        off_h = top[0]
        h_hi = new("h_hi", [P, KD, T], F32R)
        h_lo = new("h_lo", [P, KD, T], F32R)
        g_hi = at("g_hi", [P, KD, T], F32R, off_h)
        g_lo = at("g_lo", [P, KD, T], F32R, off_h + KD * T * 4)
        d_out = at("d_out", [P, KD, T], F32, off_h)
        off_y = top[0]
        yy_hi = new("yy_hi", [P, 2 * KD, T], F32R)
        yy_lo = new("yy_lo", [P, 2 * KD, T], F32R)
        x_in = at("x_in", [P, KD, T], F32, off_y)
        x_sq = at("x_sq", [P, KD, T], F32, off_y + KD * T * 4)
        h_tmp = [at(f"h_tmp{s}", [P, T], F32, off_y + (2 * KD + s) * T * 4) for s in range(2)]
        o_out = at("o_out", [P, KD, T], F32, off_y)
        yf_hi = at("yf_hi", [P, KF, T], F32R, off_y)
        yf_lo = at("yf_lo", [P, KF, T], F32R, off_y + KF * T * 4)
        off_t = top[0]
        rmask = new("rmask", [P, T])
        f_a = new("f_a", [P, T])
        f_b = new("f_b", [P, T])
        gcum = new("gcum", [P, T])
        e_g = new("e_g", [P, T])
        q_t = new("q_t", [P, T])
        k_d = new("k_d", [P, T])
        v_fm = new("v_fm", [P, T])
        v_tm = new("v_tm", [P, NT, P])
        kd_tm = new("kd_tm", [P, NT, P])
        att = new("att", [P, NT, P])
        o_sq = v_fm
        rs_o = new("rs_o", [P, T])
        sil = new("sil", [P, T])
        xpad = new("xpad", [P, T + 8])
        xc = new("xc", [P, T])
        l_r = new("l_r", [P, T])
        l_i = new("l_i", [P, T])
        l_th = new("l_th", [P, T])
        l_2 = new("l_2", [P, T])
        l_h = new("l_h", [P, T])
        g_t = new("g_t", [P, T])
        v_bd = new("v_bd", [P, NT, CPT, P])
        s_all = new("s_all", [P, NCH, P])
        mix_hi = at("mix_hi", [P, KD, T], F32R, off_t)
        mix_lo = at("mix_lo", [P, KD, T], F32R, off_t + KD * T * 4)
        x1 = at("x1", [P, KD, T], F32, off_t + 2 * KD * T * 4)
        tmp0 = off_t + 3 * KD * T * 4
        m_a, m_b, m_ga, m_gb, o_acc = [at(f"m_tmp{s}", [P, T], F32, tmp0 + s * T * 4) for s in range(5)]
        m_sq = [m_a, m_b]
        rs_t = m_ga
        t_tmp = m_gb
        fin0 = off_y + 2 * KF * T * 4
        pads = 2 * (T + 8) * 4
        u_pad = at("u_pad", [P, 2, T + 8], F32, fin0)
        fin1 = fin0 + pads
        assert fin1 + T * 4 <= off_t + 2 * KD * T * 4
        u_c0 = at("u_c0", [P, T], F32, fin1)
        u_c1 = m_b
        u_y = t_tmp
        rs_2 = o_acc
        u_c = [u_c0, u_c1]
        assert tmp0 + 5 * T * 4 <= top[0]
        assert top[0] <= nc.sbuf_usable_end, (top[0], nc.sbuf_usable_end)

        bank = [ctx.enter_context(nc.psum_tensor(f"bank{b}", [P, T], F32)) for b in range(8)]
        B_FZ, B_Q, B_V, B_XA, B_GA, B_OG = 0, 1, 2, 0, 1, 2
        B_TR, B_KV, B_ATT, B_O = 3, (4, 5), 6, 7

        w_landed = [sem(f"w_landed{s}") for s in range(RING)]
        hi_ready = sem("hi_ready")
        lo_ready = sem("lo_ready")
        product_done = sem("product_done")
        x_landed = [sem(f"x_landed{s}") for s in range(4)]
        par_landed = sem("par_landed")
        lru_landed = [sem(f"lru_landed{s}") for s in range(2)]
        consts_made = sem("consts_made")
        setup_v = sem("setup_v")
        setup_a = sem("setup_a")
        x_squared = sem("x_squared")
        ss_done = sem("ss_done")
        rs_ready = sem("rs_ready")
        rs_ln = sem("rs_ln")
        h_scaled = sem("h_scaled")
        h_hi_ready = sem("h_hi_ready")
        h_ready = sem("h_ready")
        hp_ready = sem("hp_ready")
        fz_read = sem("fz_read")
        fa_ready = sem("fa_ready")
        logf_ready = sem("logf_ready")
        g_ready = sem("g_ready")
        eg_ready = sem("eg_ready")
        eng_ready = sem("eng_ready")
        dec_ready = sem("dec_ready")
        qt_ready = sem("qt_ready")
        kt_ready = sem("kt_ready")
        kd_ready = sem("kd_ready")
        v_read = sem("v_read")
        tv_done = sem("tv_done")
        vtm_ready = sem("vtm_ready")
        vbd_ready = sem("vbd_ready")
        tkd_done = sem("tkd_done")
        kdtm_ready = sem("kdtm_ready")
        att_done = sem("att_done")
        att_ready = sem("att_ready")
        kv_done = sem("kv_done")
        s_ready = sem("s_ready")
        o_done = sem("o_done")
        osq_ready = sem("osq_ready")
        osum_done = sem("osum_done")
        rso_ln = sem("rso_ln")
        rso_ready = sem("rso_ready")
        og_sig = sem("og_sig")
        sil_ready = sem("sil_ready")
        yb_scaled = sem("yb_scaled")
        yb_made = sem("yb_made")
        y_hi_ready = sem("y_hi_ready")
        y_ready = sem("y_ready")
        xa_read = sem("xa_read")
        conv_step = sem("conv_step")
        gate_r = sem("gate_r")
        gate_i = sem("gate_i")
        r_ready = sem("r_ready")
        i_ready = sem("i_ready")
        th_ready = sem("th_ready")
        th_clamped = sem("th_clamped")
        a_ready = sem("a_ready")
        l1_ready = sem("l1_ready")
        l2_ready = sem("l2_ready")
        ix_ready = sem("ix_ready")
        ld_ready = sem("ld_ready")
        w_sqrt = sem("w_sqrt")
        u_ready = sem("u_ready")
        lru_h = sem("lru_h")
        ga_sq = sem("ga_sq")
        ga_1 = sem("ga_1")
        ga_2 = sem("ga_2")
        ga_th = sem("ga_th")
        ga_read = sem("ga_read")
        ya_made = sem("ya_made")
        sig_a = sem("sig_a")
        sig_b = sem("sig_b")
        za_read = sem("za_read")
        zb_read = sem("zb_read")
        mix_sum = sem("mix_sum")
        mix_hi_ready = sem("mix_hi_ready")
        mix_ready = sem("mix_ready")
        x_again = sem("x_again")
        acc_zero = sem("acc_zero")
        o_squared = sem("o_squared")
        o_copied = sem("o_copied")
        o_summed = sem("o_summed")
        osc_ready = sem("osc_ready")
        x1_ready = sem("x1_ready")
        x1_sq = sem("x1_sq")
        g_hi_ready = sem("g_hi_ready")
        g_ready2 = sem("g_ready2")
        pad_zero = sem("pad_zero")
        fp_ready = sem("fp_ready")
        up_read = sem("up_read")
        tap2 = sem("tap2")
        tap1 = sem("tap1")
        tap0 = sem("tap0")
        gelu_done = sem("gelu_done")
        y_made = sem("y_made")
        yf_hi_ready = sem("yf_hi_ready")
        yf_ready = sem("yf_ready")
        down_done = sem("down_done")
        d_squared = sem("d_squared")
        d_copied = sem("d_copied")
        d_summed = sem("d_summed")
        d_scaled = sem("d_scaled")
        x2_ready = sem("x2_ready")
        stored = sem("stored")

        block = ctx.enter_context(nc.Block())

        def col(t, c):
            return t[:, c:c + 1]

        @block.sync
        def _(sp):
            def tile(q, c, reuse):
                if reuse:
                    sp.wait_ge(lo_ready, 4 * q + c - RING + 1)
                src = wts[4 * q + c] if isinstance(q, int) else \
                    wts[bass.ds(4 * q + c, 1)].rearrange("o p n -> (o p) n")
                sp.dma_start(w_raw[c][:, :, :].rearrange("p a b -> p (a b)"), src).then_inc(w_landed[c], 16)

            sp.dma_start(pv[:, :], par).then_inc(par_landed, 16)
            for s in range(4):
                sp.dma_start(x_in[:, 2 * s:2 * s + 2, :], xT[:, 2 * s:2 * s + 2, :]).then_inc(x_landed[s], 16)
                if s == 1:
                    tile(0, 0, False)
            for c in range(1, RING):
                tile(0, c, False)
            with sp.Fori(1, Q_MERGE + 3) as q:
                for c in range(RING):
                    tile(q, c, True)
            sp.wait_ge(y_ready, 2 * HEADS)
            sp.dma_start(x1[:, :, :], xT).then_inc(x_again, 16)
            with sp.Fori(Q_MERGE + 3, N_TILES // RING) as q:
                for c in range(RING):
                    tile(q, c, True)
            for c in range(N_TILES % RING):
                tile(N_TILES // RING, c, True)
            for m in range(KD):
                sp.wait_ge(x2_ready, m + 1)
                sp.dma_start(outT[:, m, :], x1[:, m, :]).then_inc(stored, 16)
            sp.wait_ge(stored, 16 * KD)

        @block.gpsimd
        def _(pool):
            nc.gpsimd.memset(eps_col[:, 0:1], EPS).then_inc(consts_made, 1)
            nc.gpsimd.memset(eps_col[:, 1:2], 1.0).then_inc(consts_made, 1)
            nc.gpsimd.memset(ones[:, :], 1.0).then_inc(consts_made, 1)
            nc.gpsimd.memset(ident[:, :], 0.0).then_inc(consts_made, 1)
            nc.gpsimd.memset(amask[:, :], 1.0).then_inc(consts_made, 1)
            nc.gpsimd.memset(rmask[:, :], 1.0).then_inc(consts_made, 1)
            nc.gpsimd.memset(att[:, :, :], 0.0).then_inc(consts_made, 1)
            nc.gpsimd.memset(v_bd[:, :, :, :], 0.0).then_inc(consts_made, 1)
            nc.gpsimd.memset(xpad[:, 0:8], 0.0).then_inc(consts_made, 1)
            pool.wait_ge(consts_made, 9)
            nc.gpsimd.memset(rmask[:, :].rearrange("p (n c) -> p n c", c=CH)[:, :, 0:1], 0.0)\
                .then_inc(consts_made, 1)
            nc.gpsimd.affine_select(out=ident[:, :], in_=ident[:, :], compare_op=ALU.not_equal, fill=1.0,
                                    base=0, pattern=[[-1, P]], channel_multiplier=1).then_inc(consts_made, 1)
            nc.gpsimd.affine_select(out=amask[:, :], in_=amask[:, :], compare_op=ALU.is_ge, fill=0.0,
                                    base=0, pattern=[[1, P]], channel_multiplier=-1).then_inc(consts_made, 1)
            pool.wait_ge(consts_made, 12)
            am = amask[:, :].rearrange("p (b c) -> p b c", c=CH)
            nc.gpsimd.affine_select(out=am, in_=am, compare_op=ALU.is_ge, fill=0.0,
                                    base=0, pattern=[[-CH, CPT], [0, CH]], channel_multiplier=1)\
                .then_inc(consts_made, 1)

            def spread_v(j, first):
                pool.wait_ge(consts_made, 13)
                pool.wait_ge(vtm_ready, j + 1)
                if not first:
                    pool.wait_ge(kv_done, 4 * j)
                for b in range(CPT):
                    rows = slice(CH * b, CH * b + CH)
                    nc.gpsimd.tensor_copy(v_bd[rows, :, b, :], v_tm[rows, :, :]).then_inc(vbd_ready, 1)

            pool.wait_ge(consts_made, 13)
            for j in range(HEADS):
                spread_v(j, j == 0)

        CONSTS = 13

        @block.scalar
        def _(act):
            A = nc.scalar.activation

            def split_hi(q, c):
                act.wait_ge(w_landed[c % RING], 16 * (q + c // RING + 1))
                if not (isinstance(q, int) and 4 * q + c < RING):
                    act.wait_ge(product_done, 4 * q + c - RING + 1)
                A(w_hi[c % RING][:, :, :], w_raw[c % RING][:, :, :], ACT.Copy).then_inc(hi_ready, 1)

            def split_at(q, c):
                if not (isinstance(q, int) and 4 * q + c + LEAD >= N_TILES):
                    split_hi(q, c + LEAD)

            act.wait_ge(consts_made, CONSTS)
            nc.scalar.preload_act_table_set(SET_EXP)
            act.wait_ge(setup_v, 5)
            A(sp_t[:, 0:3, :], sp_t[:, 0:3, :], ACT.Exp).then_inc(setup_a, 1)
            for k in range(KD):
                act.wait_ge(x_landed[k // 2], 16)
                A(x_sq[:, k, :], x_in[:, k, :], ACT.Square).then_inc(x_squared, 1)
                if k == 5:
                    split_hi(0, 0)
            act.wait_ge(ss_done, 1)
            A(rs_o[:, :], bank[B_TR][:, :], ACT.Ln, bias=col(eps_col, 0), scale=1.0 / D).then_inc(rs_ln, 1)
            act.wait_ge(rs_ln, 1)
            A(rs_o[:, :], rs_o[:, :], ACT.Exp, scale=-0.5).then_inc(rs_ready, 1)
            for k in range(KD):
                act.wait_ge(h_scaled, k + 1)
                A(h_hi[:, k, :], h_tmp[k % 2][:, :], ACT.Copy).then_inc(h_hi_ready, 1)
            split_hi(0, 1)

            def lru_gates(j, pj):
                act.wait_ge(product_done, SECT * j + 6)
                act.wait_ge(yb_made, j) if not is0(j) else None
                A(sil[:, :], bank[B_OG][:, :], ACT.Sigmoid).then_inc(og_sig, 1)
                act.wait_ge(gate_r, j + 1)
                if not is0(j):
                    act.wait_ge(lru_h, j)
                A(l_r[:, :], bank[B_ATT][:, :], ACT.Sigmoid, bias=col(hp_now[pj], C_BA)).then_inc(r_ready, 1)
                act.wait_ge(gate_i, j + 1)
                A(l_i[:, :], bank[B_TR][:, :], ACT.Sigmoid, bias=col(hp_now[pj], C_BX)).then_inc(i_ready, 1)
                act.wait_ge(r_ready, j + 1)
                if not is0(j):
                    act.wait_ge(u_ready, j)
                A(l_th[:, :], l_r[:, :], ACT.Tanh, scale=col(hc_now[pj], C_C8)).then_inc(th_ready, 1)

            def is0(j):
                return isinstance(j, int) and j == 0

            def front_sig(j):
                act.wait_ge(product_done, SECT * j + 1)
                if not is0(j):
                    act.wait_ge(att_done, j)
                    act.wait_ge(kd_ready, j)
                A(f_a[:, :], bank[B_FZ][:, :], ACT.Sigmoid).then_inc(fa_ready, 1)
                A(f_b[:, :], bank[B_FZ][:, :], ACT.Sigmoid, scale=-1.0).then_inc(fz_read, 1)

            def front_log(j, pj):
                act.wait_ge(fa_ready, j + 1)
                act.wait_ge(hp_ready, 2 * j + 2)
                A(f_a[:, :], f_a[:, :], ACT.Ln, bias=col(hc_now[pj], C_LB), scale=col(hc_now[pj], C_OMLB))\
                    .then_inc(logf_ready, 1)

            def front_exp(j):
                act.wait_ge(g_ready, j + 1)
                if not is0(j):
                    act.wait_ge(dec_ready, j)
                    act.wait_ge(qt_ready, j)
                A(e_g[:, :], gcum[:, :], ACT.Exp).then_inc(eg_ready, 1)
                act.wait_ge(eg_ready, j + 1)
                A(gcum[:, :], gcum[:, :], ACT.Exp, scale=-1.0).then_inc(eng_ready, 1)

            def lru_logs(j, pj):
                act.wait_ge(th_ready, j + 1)
                A(l_r[:, :], l_r[:, :], ACT.Exp, scale=col(hc_now[pj], C_NC8)).then_inc(a_ready, 1)
                act.wait_ge(th_clamped, j + 1)
                act.wait_ge(ga_th, j + 1)
                A(l_2[:, :], l_th[:, :], ACT.Ln, bias=col(eps_col, 1)).then_inc(l2_ready, 1)
                act.wait_ge(l2_ready, j + 1)
                A(l_th[:, :], l_th[:, :], ACT.Ln, scale=2.0).then_inc(l1_ready, 1)

            def lru_root(j):
                act.wait_ge(ld_ready, j + 1)
                A(l_th[:, :], l_th[:, :], ACT.Exp, scale=0.5).then_inc(w_sqrt, 1)

            def o_square(j):
                act.wait_ge(o_done, j + 1)
                if not is0(j):
                    act.wait_ge(osum_done, j)
                A(o_sq[:, :], bank[B_O][:, :], ACT.Square).then_inc(osq_ready, 1)

            def o_rms(j):
                act.wait_ge(osum_done, j + 1)
                if is0(j):
                    act.wait_ge(h_scaled, KD)
                else:
                    act.wait_ge(yb_scaled, j)
                A(rs_o[:, :], bank[B_TR][:, :], ACT.Ln, bias=col(eps_col, 0), scale=1.0 / P).then_inc(rso_ln, 1)
                act.wait_ge(rso_ln, j + 1)
                A(rs_o[:, :], rs_o[:, :], ACT.Exp, scale=-0.5).then_inc(rso_ready, 1)

            def finish_a(j, pj):
                lru_logs(j, pj)
                o_square(j)
                lru_root(j)

            def head(i, pj, first):
                j = 2 * i + pj
                q, c = 3 * i, SECT * pj
                pp = 1 - pj
                split_at(q, c)
                if not first:
                    nc.scalar.preload_act_table_set(SET_SIG)
                    lru_gates(j - 1, pp)
                split_at(q, c + 1)
                if first:
                    nc.scalar.preload_act_table_set(SET_SIG)
                front_sig(j)
                nc.scalar.preload_act_table_set(SET_EXP)
                front_log(j, pj)
                if not first:
                    lru_logs(j - 1, pp)
                front_exp(j)
                if not first:
                    o_square(j - 1)
                    lru_root(j - 1)
                if not is0(i):
                    act.wait_ge(gate_i, j - 1)
                act.dma_start(lru_w[pj][:, :, :].rearrange("p a b -> p (a b)"),
                              lru[bass.ds(j, 1), :, :].rearrange("o p n -> (o p) n")).then_inc(lru_landed[pj], 16)
                split_at(q, c + 2)
                if not first:
                    o_rms(j - 1)
                split_at(q, c + 3)
                act.wait_ge(product_done, SECT * j + 3)
                if not first:
                    act.wait_ge(osum_done, j)
                A(v_fm[:, :], bank[B_V][:, :], ACT.Copy).then_inc(v_read, 1)
                act.wait_ge(tv_done, j + 1)
                if not first:
                    act.wait_ge(o_done, j)
                    act.wait_ge(vbd_ready, CPT * j)
                A(v_tm[:, :, :].rearrange("p a b -> p (a b)"), bank[B_TR][:, :], ACT.Copy).then_inc(vtm_ready, 1)
                split_at(q, c + 4)
                act.wait_ge(product_done, SECT * j + 4)
                if not first:
                    act.wait_ge(conv_step, 4 * j)
                A(xpad[:, 3:3 + T], bank[B_XA][:, :], ACT.Copy).then_inc(xa_read, 1)
                split_at(q, c + 5)
                act.wait_ge(product_done, SECT * j + 5)
                if not first:
                    act.wait_ge(ld_ready, j)
                A(l_2[:, :], bank[B_GA][:, :], ACT.Square).then_inc(ga_sq, 1)
                nc.scalar.preload_act_table_set(SET_SIG)
                act.wait_ge(ga_2, j + 1)
                A(g_t[:, :], l_2[:, :], ACT.Tanh, scale=GELU_S).then_inc(ga_th, 1)

            head(0, 0, True)
            head(0, 1, False)
            with act.Fori(1, HEADS // 2) as i:
                head(i, 0, False)
                head(i, 1, False)

            def merge(m, first):
                q = Q_MERGE + m
                split_at(q, 0)
                if first:
                    lru_gates(HEADS - 1, 1)
                    nc.scalar.preload_act_table_set(SET_EXP)
                    lru_logs(HEADS - 1, 1)
                    o_square(HEADS - 1)
                    lru_root(HEADS - 1)
                split_at(q, 1)
                if first:
                    o_rms(HEADS - 1)
                    act.wait_ge(y_ready, 2 * HEADS)
                    nc.scalar.preload_act_table_set(SET_SIG)
                else:
                    act.wait_ge(mix_sum, m)
                act.wait_ge(product_done, 4 * q + 1)
                A(m_ga[:, :], bank[0][:, :], ACT.Sigmoid).then_inc(sig_a, 1)
                act.wait_ge(product_done, 4 * q + 2)
                A(m_gb[:, :], bank[2][:, :], ACT.Sigmoid).then_inc(sig_b, 1)
                split_at(q, 2)
                split_at(q, 3)

            merge(0, True)
            with act.Fori(1, KD) as m:
                merge(m, False)

            def out_block(it, c, first):
                q = Q_OUT + it
                m = 4 * it + c
                split_at(q, c)
                act.wait_ge(product_done, 4 * q + c + 1)
                if first and c < 2:
                    act.wait_ge(mix_sum, KD)
                else:
                    act.wait_ge(o_summed, m - 1)
                A(m_sq[c % 2][:, :], bank[c][:, :], ACT.Square).then_inc(o_squared, 1)
                A(o_out[:, bass.ds(m, 1), :].rearrange("p a b -> p (a b)"), bank[c][:, :], ACT.Copy)\
                    .then_inc(o_copied, 1)

            for c in range(RING):
                out_block(0, c, True)
            with act.Fori(1, 2) as it:
                for c in range(RING):
                    out_block(it, c, False)
            nc.scalar.preload_act_table_set(SET_EXP)
            act.wait_ge(ss_done, 2)
            act.wait_ge(mix_ready, KD)
            A(rs_t[:, :], bank[B_O][:, :], ACT.Ln, bias=col(eps_col, 0), scale=1.0 / D).then_inc(rs_ln, 1)
            act.wait_ge(rs_ln, 2)
            A(rs_t[:, :], rs_t[:, :], ACT.Exp, scale=-0.5).then_inc(rs_ready, 1)
            for k in range(KD):
                act.wait_ge(x1_ready, k + 1)
                A(g_hi[:, k, :], x1[:, k, :], ACT.Copy, scale=col(pv, O_PREF + k)).then_inc(g_hi_ready, 1)
                act.wait_ge(o_summed, KD)
                if k >= 2:
                    act.wait_ge(x1_sq, 0 + k - 1)
                    act.wait_ge(ss_done, 2 + k - 1)
                A(m_sq[k % 2][:, :], x1[:, k, :], ACT.Square).then_inc(x1_sq, 1)
            act.wait_ge(ss_done, 2 + KD)
            A(rs_2[:, :], bank[B_ATT][:, :], ACT.Ln, bias=col(eps_col, 0), scale=1.0 / D).then_inc(rs_ln, 1)
            act.wait_ge(rs_ln, 3)
            A(rs_2[:, :], rs_2[:, :], ACT.Exp, scale=-0.5).then_inc(rs_ready, 1)
            nc.scalar.preload_act_table(ACT.Gelu_apprx_tanh)

            def pair(it, e, first):
                q = Q_UP + it
                n = 2 * it + e
                for v in range(2):
                    c = 2 * e + v
                    split_at(q, c)
                    act.wait_ge(up_read, 2 * n + v + 1)
                    act.wait_ge(fp_ready, n + 1)
                    if not first:
                        act.wait_ge(y_made, n)
                    A(u_c[v][:, :], u_pad[:, v, 2:2 + T], ACT.Identity, bias=col(fp_now[e], 4 * v + 3),
                      scale=col(fp_now[e], 4 * v + 2)).then_inc(tap2, 1)
                act.wait_ge(tap0, 2 * n + 1)
                A(u_c[0][:, :], u_c[0][:, :], ACT.Gelu_apprx_tanh).then_inc(gelu_done, 1)

            pair(0, 0, True)
            pair(0, 1, False)
            with act.Fori(1, KF // 2) as it:
                pair(it, 0, False)
                pair(it, 1, False)

            with act.Fori(0, (N_DOWN - LEAD) // RING) as it:
                for c in range(RING):
                    split_at(Q_DOWN + it, c)
            for m in range(KD):
                act.wait_ge(down_done, m + 1)
                if m >= 2:
                    act.wait_ge(d_summed, m - 1)
                A(m_sq[m % 2][:, :], bank[m][:, :], ACT.Square).then_inc(d_squared, 1)
                A(d_out[:, m, :], bank[m][:, :], ACT.Copy, scale=col(pv, O_POSTF + m)).then_inc(d_copied, 1)
            nc.scalar.preload_act_table_set(SET_EXP)
            act.wait_ge(ss_done, 3 + KD)
            A(rs_t[:, :], bank[0][:, :], ACT.Ln, bias=col(eps_col, 0), scale=1.0 / D).then_inc(rs_ln, 1)
            act.wait_ge(rs_ln, 4)
            A(rs_t[:, :], rs_t[:, :], ACT.Exp, scale=-0.5).then_inc(rs_ready, 1)

        @block.vector
        def _(dve):
            V = nc.vector

            def is0(j):
                return isinstance(j, int) and j == 0

            def split_lo(q, c):
                s = c % RING
                dve.wait_ge(hi_ready, 4 * q + c + 1)
                V.tensor_tensor(w_lo[s][:, :, :], w_raw[s][:, :, :], w_hi[s][:, :, :].bitcast(F32),
                                ALU.subtract).then_inc(lo_ready, 1)

            def split_at(q, c):
                if not (isinstance(q, int) and 4 * q + c + LEAD >= N_TILES):
                    split_lo(q, c + LEAD)

            def at_j(t, j):
                return t[:, bass.ds(j, 1), :].rearrange("p a b -> p (a b)")

            steps = [0]

            def link(ins):
                steps[0] += 1
                ins.then_inc(setup_v, 1)
                dve.wait_ge(setup_v, steps[0])

            hpv = pv[:, 0:O_PRE].rearrange("p (h c) -> p c h", c=HPC)
            lam, l0, l1 = hpv[:, C_LAM, :], hpv[:, C_L0, :], hpv[:, C_L1, :]
            s = [sp_t[:, a, :] for a in range(8)]
            dve.wait_ge(par_landed, 16)
            link(V.tensor_tensor(s[3], l0, l1, ALU.max))
            link(V.tensor_tensor(s[0], l0, s[3], ALU.subtract))
            link(V.tensor_tensor(s[1], l1, s[3], ALU.subtract))
            link(V.tensor_scalar(s[4], lam, -1.0, None, ALU.mult))
            link(V.tensor_tensor(s[2], lam, s[4], ALU.min))
            dve.wait_ge(setup_a, 1)
            link(V.tensor_tensor(s[3], s[0], s[1], ALU.add))
            link(V.reciprocal(s[3], s[3]))
            link(V.tensor_tensor(hc[:, :, C_LB], s[0], s[3], ALU.mult))
            link(V.tensor_scalar(hc[:, :, C_OMLB], hc[:, :, C_LB], -1.0, 1.0, ALU.mult, ALU.add))
            link(V.tensor_scalar(s[5], s[2], 2.0, None, ALU.add))
            link(V.reciprocal(s[5], s[5]))
            link(V.tensor_tensor(s[5], s[2], s[5], ALU.mult))
            link(V.tensor_tensor(s[6], s[5], s[5], ALU.mult))
            link(V.tensor_scalar(s[7], s[6], 1.0 / 15, None, ALU.mult))
            for odd in (13, 11, 9, 7, 5, 3):
                link(V.scalar_tensor_tensor(out=s[7], in0=s[7], scalar=1.0 / odd, in1=s[6],
                                            op0=ALU.add, op1=ALU.mult))
            link(V.scalar_tensor_tensor(out=s[7], in0=s[7], scalar=1.0, in1=s[5], op0=ALU.add, op1=ALU.mult))
            link(V.tensor_scalar(s[4], s[4], 0.0, 8.0, ALU.max, ALU.mult))
            link(V.scalar_tensor_tensor(out=hc[:, :, C_C8], in0=s[7], scalar=16.0, in1=s[4],
                                        op0=ALU.mult, op1=ALU.add))
            link(V.tensor_scalar(hc[:, :, C_NC8], hc[:, :, C_C8], -1.0, None, ALU.mult))

            split_lo(0, 0)
            dve.wait_ge(rs_ready, 1)
            for k in range(KD + 1):
                if k < KD:
                    if k >= 2:
                        dve.wait_ge(h_ready, k - 1)
                    V.scalar_tensor_tensor(out=h_tmp[k % 2][:, :], in0=x_in[:, k, :], scalar=col(pv, O_PRE + k),
                                           in1=rs_o[:, :], op0=ALU.mult, op1=ALU.mult).then_inc(h_scaled, 1)
                if k >= 1:
                    dve.wait_ge(h_hi_ready, k)
                    V.tensor_tensor(h_lo[:, k - 1, :], h_tmp[(k - 1) % 2][:, :],
                                    h_hi[:, k - 1, :].bitcast(F32), ALU.subtract).then_inc(h_ready, 1)
            split_lo(0, 1)

            def params(j, pj, first):
                if not first:
                    dve.wait_ge(y_ready, 2 * j - 2)
                V.tensor_copy(hp_now[pj][:, :], pv[:, bass.ds(j * HPC, HPC)]).then_inc(hp_ready, 1)
                V.tensor_copy(hc_now[pj][:, :], at_j(hc, j)).then_inc(hp_ready, 1)

            def lru_1(j):
                dve.wait_ge(og_sig, j + 1)
                V.tensor_tensor(sil[:, :], bank[B_OG][:, :], sil[:, :], ALU.mult).then_inc(sil_ready, 1)
                dve.wait_ge(th_ready, j + 1)
                V.tensor_scalar(l_th[:, :], l_th[:, :], 2.0 ** -63, None, ALU.max).then_inc(th_clamped, 1)
                dve.wait_ge(i_ready, j + 1)
                V.tensor_tensor(l_i[:, :], l_i[:, :], xc[:, :], ALU.mult).then_inc(ix_ready, 1)

            def scan_g(j):
                dve.wait_ge(logf_ready, j + 1)
                if not is0(j):
                    dve.wait_ge(kt_ready, j)
                V.tensor_tensor_scan(out=gcum[:, :], data0=rmask[:, :], data1=f_a[:, :], initial=0.0,
                                     op0=ALU.mult, op1=ALU.add).then_inc(g_ready, 1)

            def lru_2(j):
                dve.wait_ge(l1_ready, j + 1)
                V.tensor_tensor(l_th[:, :], l_th[:, :], l_2[:, :], ALU.subtract).then_inc(ld_ready, 1)

            def lru_3(j):
                dve.wait_ge(w_sqrt, j + 1)
                dve.wait_ge(ix_ready, j + 1)
                V.tensor_tensor(l_i[:, :], l_i[:, :], l_th[:, :], ALU.mult).then_inc(u_ready, 1)
                dve.wait_ge(u_ready, j + 1)
                dve.wait_ge(a_ready, j + 1)
                if not is0(j):
                    dve.wait_ge(y_ready, 2 * j)
                V.tensor_tensor_scan(out=l_h[:, :], data0=l_r[:, :], data1=l_i[:, :], initial=0.0,
                                     op0=ALU.mult, op1=ALU.add).then_inc(lru_h, 1)
                dve.wait_ge(lru_h, j + 1)
                dve.wait_ge(ga_read, j + 1)
                V.scalar_tensor_tensor(out=l_h[:, :], in0=g_t[:, :], scalar=0.5, in1=l_h[:, :],
                                       op0=ALU.mult, op1=ALU.mult).then_inc(ya_made, 1)
                dve.wait_ge(ya_made, j + 1)
                V.tensor_scalar(at_j(yy_hi, j), l_h[:, :], 1.0, None, ALU.mult).then_inc(y_hi_ready, 1)

            def front(j, pj):
                dve.wait_ge(product_done, SECT * j + 2)
                dve.wait_ge(eg_ready, j + 1)
                if not is0(j):
                    dve.wait_ge(o_done, j)
                V.tensor_tensor(q_t[:, :], bank[B_Q][:, :], e_g[:, :], ALU.mult).then_inc(qt_ready, 1)
                dve.wait_ge(hp_ready, 2 * j + 2)
                dve.wait_ge(fz_read, j + 1)
                dve.wait_ge(eng_ready, j + 1)
                V.scalar_tensor_tensor(out=f_b[:, :], in0=f_b[:, :], scalar=col(hc_now[pj], C_OMLB),
                                       in1=gcum[:, :], op0=ALU.mult, op1=ALU.mult).then_inc(kt_ready, 1)
                if not is0(j):
                    dve.wait_ge(s_ready, 15 * j)
                V.tensor_copy(dec[:, :], e_g[:, :].rearrange("p (n c) -> p n c", c=CH)[:, :, CH - 1])\
                    .then_inc(dec_ready, 1)
                dve.wait_ge(kt_ready, j + 1)
                dve.wait_ge(dec_ready, j + 1)
                if not is0(j):
                    dve.wait_ge(tkd_done, j)
                V.tensor_tensor(k_d[:, :].rearrange("p (n c) -> p n c", c=CH),
                                f_b[:, :].rearrange("p (n c) -> p n c", c=CH),
                                dec[:, :].unsqueeze(2).to_broadcast([P, NCH, CH]), ALU.mult)\
                    .then_inc(kd_ready, 1)

            def out_b(j, pj):
                dve.wait_ge(rso_ready, j + 1)
                V.scalar_tensor_tensor(out=rs_o[:, :], in0=bank[B_O][:, :], scalar=col(hp_now[pj], C_HG),
                                       in1=rs_o[:, :], op0=ALU.mult, op1=ALU.mult).then_inc(yb_scaled, 1)
                dve.wait_ge(yb_scaled, j + 1)
                dve.wait_ge(sil_ready, j + 1)
                V.tensor_tensor(sil[:, :], rs_o[:, :], sil[:, :], ALU.mult).then_inc(yb_made, 1)
                dve.wait_ge(yb_made, j + 1)
                V.tensor_scalar(at_j(yy_hi, j + KD), sil[:, :], 1.0, None, ALU.mult).then_inc(y_hi_ready, 1)

            def split_y(j):
                dve.wait_ge(y_hi_ready, 2 * j + 1)
                V.tensor_tensor(at_j(yy_lo, j), l_h[:, :], at_j(yy_hi, j).bitcast(F32), ALU.subtract)\
                    .then_inc(y_ready, 1)
                dve.wait_ge(y_hi_ready, 2 * j + 2)
                V.tensor_tensor(at_j(yy_lo, j + KD), sil[:, :], at_j(yy_hi, j + KD).bitcast(F32), ALU.subtract)\
                    .then_inc(y_ready, 1)

            def chain(j, a, b):
                for n in range(a, b):
                    kv = bank[B_KV[n // CPT % 2]][:, n % CPT * P:(n % CPT + 1) * P]
                    if n % CPT == 0:
                        dve.wait_ge(kv_done, 4 * j + n // CPT + 1)
                    if n == 0:
                        if not is0(j):
                            dve.wait_ge(o_done, j)
                        V.tensor_copy(s_all[:, 1, :], kv).then_inc(s_ready, 1)
                        continue
                    dve.wait_ge(s_ready, 15 * j + n)
                    V.scalar_tensor_tensor(out=s_all[:, n + 1, :], in0=s_all[:, n, :], scalar=col(dec, n),
                                           in1=kv, op0=ALU.mult, op1=ALU.add).then_inc(s_ready, 1)

            def head(i, pj, first):
                j = 2 * i + pj
                q, c = 3 * i, SECT * pj
                pp = 1 - pj
                split_at(q, c)
                params(j, pj, is0(i))
                if not first:
                    lru_1(j - 1)
                split_at(q, c + 1)
                scan_g(j)
                if not first:
                    lru_2(j - 1)
                split_at(q, c + 2)
                front(j, pj)
                if not first:
                    lru_3(j - 1)
                    out_b(j - 1, pp)
                split_at(q, c + 3)
                if not first:
                    split_y(j - 1)
                dve.wait_ge(tkd_done, j + 1)
                if not first:
                    dve.wait_ge(kv_done, 4 * j)
                V.tensor_copy(kd_tm[:, :, :].rearrange("p a b -> p (a b)"), bank[B_TR][:, :])\
                    .then_inc(kdtm_ready, 1)
                split_at(q, c + 4)
                dve.wait_ge(consts_made, CONSTS)
                dve.wait_ge(att_done, j + 1)
                if not first:
                    dve.wait_ge(o_done, j)
                V.copy_predicated(out=att[:, :, :], mask=amask[:, :].bitcast(U32).unsqueeze(1)
                                  .to_broadcast([P, NT, P]),
                                  data=bank[B_ATT][:, :].rearrange("p (a b) -> p a b", b=P)).then_inc(att_ready, 1)
                dve.wait_ge(xa_read, j + 1)
                if not first:
                    dve.wait_ge(gate_i, j)
                    dve.wait_ge(ix_ready, j)
                V.tensor_scalar(xc[:, :], xpad[:, 3:3 + T], col(hp_now[pj], 3), col(hp_now[pj], 4),
                                ALU.mult, ALU.add).then_inc(conv_step, 1)
                for t in (2, 1, 0):
                    dve.wait_ge(conv_step, 4 * j + 3 - t)
                    V.scalar_tensor_tensor(out=xc[:, :], in0=xpad[:, t:t + T], scalar=col(hp_now[pj], t),
                                           in1=xc[:, :], op0=ALU.mult, op1=ALU.add).then_inc(conv_step, 1)
                chain(j, 0, 8)
                split_at(q, c + 5)
                dve.wait_ge(ga_sq, j + 1)
                V.tensor_scalar(l_2[:, :], l_2[:, :], GELU_C, 1.0, ALU.mult, ALU.add).then_inc(ga_1, 1)
                dve.wait_ge(ga_1, j + 1)
                V.tensor_tensor(l_2[:, :], bank[B_GA][:, :], l_2[:, :], ALU.mult).then_inc(ga_2, 1)
                chain(j, 8, 15)
                dve.wait_ge(ga_th, j + 1)
                V.scalar_tensor_tensor(out=g_t[:, :], in0=g_t[:, :], scalar=1.0, in1=bank[B_GA][:, :],
                                       op0=ALU.add, op1=ALU.mult).then_inc(ga_read, 1)

            head(0, 0, True)
            head(0, 1, False)
            with dve.Fori(1, HEADS // 2) as i:
                head(i, 0, False)
                head(i, 1, False)

            def merge(m, first):
                q = Q_MERGE + m
                split_at(q, 0)
                if first:
                    lru_1(HEADS - 1)
                    lru_2(HEADS - 1)
                split_at(q, 1)
                if first:
                    lru_3(HEADS - 1)
                    out_b(HEADS - 1, 1)
                    split_y(HEADS - 1)
                split_at(q, 2)
                dve.wait_ge(sig_a, m + 1)
                dve.wait_ge(product_done, 4 * q + 3)
                if not first:
                    dve.wait_ge(mix_ready, m)
                V.tensor_tensor(m_a[:, :], bank[1][:, :], m_ga[:, :], ALU.mult).then_inc(za_read, 1)
                split_at(q, 3)
                dve.wait_ge(sig_b, m + 1)
                dve.wait_ge(product_done, 4 * q + 4)
                V.tensor_tensor(m_b[:, :], bank[4][:, :], m_gb[:, :], ALU.mult).then_inc(zb_read, 1)
                dve.wait_ge(za_read, m + 1)
                dve.wait_ge(zb_read, m + 1)
                V.tensor_tensor(m_a[:, :], m_a[:, :], m_b[:, :], ALU.add).then_inc(mix_sum, 1)
                dve.wait_ge(mix_sum, m + 1)
                V.tensor_scalar(at_j(mix_hi, m), m_a[:, :], 1.0, None, ALU.mult).then_inc(mix_hi_ready, 1)
                dve.wait_ge(mix_hi_ready, m + 1)
                V.tensor_tensor(at_j(mix_lo, m), m_a[:, :], at_j(mix_hi, m).bitcast(F32), ALU.subtract)\
                    .then_inc(mix_ready, 1)

            merge(0, True)
            with dve.Fori(1, KD) as m:
                merge(m, False)

            V.memset(o_acc[:, :], 0.0).then_inc(acc_zero, 1)

            def out_block(it, c):
                q = Q_OUT + it
                m = 4 * it + c
                split_at(q, c)
                dve.wait_ge(o_squared, m + 1)
                if is0(it) and c == 0:
                    dve.wait_ge(acc_zero, 1)
                else:
                    dve.wait_ge(o_summed, m)
                V.tensor_tensor(o_acc[:, :], o_acc[:, :], m_sq[c % 2][:, :], ALU.add).then_inc(o_summed, 1)

            for c in range(RING):
                out_block(0, c)
            with dve.Fori(1, 2) as it:
                for c in range(RING):
                    out_block(it, c)

            dve.wait_ge(rs_ready, 2)
            dve.wait_ge(o_copied, KD)
            dve.wait_ge(x_again, 16)
            for k in range(KD):
                if k >= 1:
                    dve.wait_ge(x1_ready, k)
                V.scalar_tensor_tensor(out=t_tmp[:, :], in0=o_out[:, k, :], scalar=col(pv, O_POST + k),
                                       in1=rs_t[:, :], op0=ALU.mult, op1=ALU.mult).then_inc(osc_ready, 1)
                dve.wait_ge(osc_ready, k + 1)
                V.tensor_tensor(x1[:, k, :], x1[:, k, :], t_tmp[:, :], ALU.add).then_inc(x1_ready, 1)
                dve.wait_ge(g_hi_ready, k + 1)
                V.scalar_tensor_tensor(out=g_lo[:, k, :], in0=x1[:, k, :], scalar=col(pv, O_PREF + k),
                                       in1=g_hi[:, k, :].bitcast(F32), op0=ALU.mult, op1=ALU.subtract)\
                    .then_inc(g_ready2, 1)
            V.memset(u_pad[:, :, 0:2], 0.0).then_inc(pad_zero, 1)

            def pair(it, e, first):
                q = Q_UP + it
                n = 2 * it + e
                if not first:
                    dve.wait_ge(tap0, 2 * n)
                V.tensor_copy(fp_now[e][:, :], pv[:, bass.ds(O_FFN + n * 8, 8)]).then_inc(fp_ready, 1)
                if first:
                    dve.wait_ge(rs_ready, 3)
                    dve.wait_ge(pad_zero, 1)
                for v in range(2):
                    c = 2 * e + v
                    split_at(q, c)
                    dve.wait_ge(product_done, 4 * q + c + 1)
                    V.tensor_tensor(u_pad[:, v, 2:2 + T], bank[c][:, :], rs_2[:, :], ALU.mult).then_inc(up_read, 1)
                    for t, before, after in ((1, tap2, tap1), (0, tap1, tap0)):
                        dve.wait_ge(before, 2 * n + v + 1)
                        V.scalar_tensor_tensor(out=u_c[v][:, :], in0=u_pad[:, v, t:t + T],
                                               scalar=col(fp_now[e], 4 * v + t), in1=u_c[v][:, :],
                                               op0=ALU.mult, op1=ALU.add).then_inc(after, 1)
                dve.wait_ge(gelu_done, n + 1)
                dve.wait_ge(tap0, 2 * n + 2)
                if not first:
                    dve.wait_ge(yf_ready, n)
                V.tensor_tensor(u_y[:, :], u_c[0][:, :], u_c[1][:, :], ALU.mult).then_inc(y_made, 1)
                dve.wait_ge(y_made, n + 1)
                V.tensor_scalar(at_j(yf_hi, n), u_y[:, :], 1.0, None, ALU.mult).then_inc(yf_hi_ready, 1)
                dve.wait_ge(yf_hi_ready, n + 1)
                V.tensor_tensor(at_j(yf_lo, n), u_y[:, :], at_j(yf_hi, n).bitcast(F32), ALU.subtract)\
                    .then_inc(yf_ready, 1)

            pair(0, 0, True)
            pair(0, 1, False)
            with dve.Fori(1, KF // 2) as it:
                pair(it, 0, False)
                pair(it, 1, False)

            with dve.Fori(0, (N_DOWN - LEAD) // RING) as it:
                for c in range(RING):
                    split_at(Q_DOWN + it, c)

            for m in range(KD):
                dve.wait_ge(d_squared, m + 1)
                if m == 0:
                    V.tensor_copy(o_acc[:, :], m_sq[0][:, :]).then_inc(d_summed, 1)
                else:
                    dve.wait_ge(d_summed, m)
                    V.tensor_tensor(o_acc[:, :], o_acc[:, :], m_sq[m % 2][:, :], ALU.add).then_inc(d_summed, 1)
            dve.wait_ge(rs_ready, 4)
            dve.wait_ge(d_copied, KD)
            for m in range(KD):
                V.tensor_tensor(d_out[:, m, :], d_out[:, m, :], rs_t[:, :], ALU.mult).then_inc(d_scaled, 1)
                dve.wait_ge(d_scaled, m + 1)
                V.tensor_tensor(x1[:, m, :], x1[:, m, :], d_out[:, m, :], ALU.add).then_inc(x2_ready, 1)

        @block.tensor
        def _(pe):
            M = nc.tensor.matmul

            def is0(j):
                return isinstance(j, int) and j == 0

            def block3(out, s, b, xh, xl, start, stop):
                M(out, w_hi[s][:, b, :], xh, start=start, stop=False)
                M(out, w_hi[s][:, b, :], xl, start=False, stop=False)
                return M(out, w_lo[s][:, b, :], xh, start=False, stop=stop)

            def product(q, c, out, hi, lo, k0=0, each=None):
                pe.wait_ge(lo_ready, 4 * q + c + 1)
                for k in range(KD):
                    if each is not None:
                        each(k)
                    last = block3(out, c % RING, k, hi[:, k0 + k, :], lo[:, k0 + k, :], k == 0, k == KD - 1)
                last.then_inc(product_done, 1)

            pe.wait_ge(consts_made, CONSTS)
            for k in range(KD):
                pe.wait_ge(x_squared, k + 1)
                last = M(bank[B_TR][:, :], ones[:, :], x_sq[:, k, :], start=(k == 0), stop=(k == KD - 1))
            last.then_inc(ss_done, 1)

            def o_stage(j):
                pe.wait_ge(att_ready, j + 1)
                pe.wait_ge(vtm_ready, j + 1)
                if not is0(j):
                    pe.wait_ge(yb_scaled, j)
                for t in range(NT):
                    last = M(bank[B_O][:, P * t:P * t + P], v_tm[:, t, :], att[:, t, :], start=True, stop=False)
                    pe.wait_ge(s_ready, 15 * j + 4 * t + 3)
                    for n in range(CPT * t, CPT * t + CPT):
                        if n:
                            last = M(bank[B_O][:, CH * n:CH * n + CH], s_all[:, n, :], q_t[:, CH * n:CH * n + CH],
                                     start=False, stop=(n % CPT == CPT - 1))
                last.then_inc(o_done, 1)

            def o_sum(j):
                pe.wait_ge(osq_ready, j + 1)
                pe.wait_ge(i_ready, j + 1)
                M(bank[B_TR][:, :], ones[:, :], o_sq[:, :], start=True, stop=True).then_inc(osum_done, 1)

            def head(i, pj, first):
                j = 2 * i + pj
                q, c = 3 * i, SECT * pj
                each = (lambda k: pe.wait_ge(h_ready, k + 1)) if first else None
                if not first:
                    pe.wait_ge(xa_read, j)
                product(q, c, bank[B_FZ][:, :], h_hi, h_lo, each=each)
                if not first:
                    o_stage(j - 1)
                    pe.wait_ge(ga_read, j)
                product(q, c + 1, bank[B_Q][:, :], h_hi, h_lo)
                if not first:
                    o_sum(j - 1)
                    pe.wait_ge(sil_ready, j)
                product(q, c + 2, bank[B_V][:, :], h_hi, h_lo)
                pe.wait_ge(fz_read, j + 1)
                product(q, c + 3, bank[B_XA][:, :], h_hi, h_lo)
                pe.wait_ge(v_read, j + 1)
                if first:
                    pe.wait_ge(rs_ln, 1)
                else:
                    pe.wait_ge(rso_ln, j)
                for t in range(NT):
                    last = nc.tensor.transpose(bank[B_TR][:, P * t:P * t + P], v_fm[:, P * t:P * t + P], ident[:, :])
                last.then_inc(tv_done, 1)
                pe.wait_ge(kt_ready, j + 1)
                pe.wait_ge(qt_ready, j + 1)
                if not first:
                    pe.wait_ge(r_ready, j)
                for t in range(NT):
                    last = M(bank[B_ATT][:, P * t:P * t + P], f_b[:, P * t:P * t + P], q_t[:, P * t:P * t + P],
                             start=True, stop=True)
                last.then_inc(att_done, 1)
                pe.wait_ge(vtm_ready, j + 1)
                pe.wait_ge(kd_ready, j + 1)
                for t in range(NT):
                    last = nc.tensor.transpose(bank[B_TR][:, P * t:P * t + P], k_d[:, P * t:P * t + P], ident[:, :])
                last.then_inc(tkd_done, 1)
                product(q, c + 4, bank[B_GA][:, :], h_hi, h_lo)

                def increments(t):
                    if t >= 2:
                        pe.wait_ge(s_ready, 15 * j + 4 * (t - 1))
                    elif not first:
                        pe.wait_ge(s_ready, 15 * j)
                    M(bank[B_KV[t % 2]][:, :], kd_tm[:, t, :], v_bd[:, t, :, :].rearrange("p a b -> p (a b)"),
                      start=True, stop=True).then_inc(kv_done, 1)

                pe.wait_ge(kdtm_ready, j + 1)
                pe.wait_ge(vbd_ready, CPT * j + CPT)
                increments(0)
                increments(1)
                product(q, c + 5, bank[B_OG][:, :], h_hi, h_lo)
                increments(2)
                increments(3)
                pe.wait_ge(conv_step, 4 * j + 4)
                pe.wait_ge(att_ready, j + 1)
                pe.wait_ge(lru_landed[pj], 16 * i + 16)
                M(bank[B_ATT][:, :], lru_w[pj][:, 0, :], xc[:, :], start=True, stop=True).then_inc(gate_r, 1)
                pe.wait_ge(kdtm_ready, j + 1)
                M(bank[B_TR][:, :], lru_w[pj][:, 1, :], xc[:, :], start=True, stop=True).then_inc(gate_i, 1)

            head(0, 0, True)
            head(0, 1, False)
            with pe.Fori(1, HEADS // 2) as i:
                head(i, 0, False)
                head(i, 1, False)

            def merge(m, first):
                q = Q_MERGE + m
                if first:
                    pe.wait_ge(xa_read, HEADS)
                else:
                    pe.wait_ge(sig_a, m)
                product(q, 0, bank[0][:, :], h_hi, h_lo)
                if first:
                    o_stage(HEADS - 1)
                    pe.wait_ge(sil_ready, HEADS)
                else:
                    pe.wait_ge(sig_b, m)
                product(q, 1, bank[2][:, :], h_hi, h_lo)
                if first:
                    o_sum(HEADS - 1)
                    pe.wait_ge(ga_read, HEADS)
                    pe.wait_ge(y_ready, 2 * HEADS - 1)
                else:
                    pe.wait_ge(za_read, m)
                product(q, 2, bank[1][:, :], yy_hi, yy_lo)
                if first:
                    pe.wait_ge(y_ready, 2 * HEADS)
                    pe.wait_ge(s_ready, 15 * HEADS)
                else:
                    pe.wait_ge(zb_read, m)
                product(q, 3, bank[4][:, :], yy_hi, yy_lo, k0=KD)

            merge(0, True)
            with pe.Fori(1, KD) as m:
                merge(m, False)

            def out_block(it, c, first):
                q = Q_OUT + it
                if first:
                    if c == 0:
                        pe.wait_ge(za_read, KD)
                        pe.wait_ge(rso_ln, HEADS)
                    each = lambda k: pe.wait_ge(mix_ready, k + 1)
                else:
                    pe.wait_ge(o_copied, 4 * it + c - 3)
                    each = None
                product(q, c, bank[c][:, :], mix_hi, mix_lo, each=each if c == 0 and first else None)

            for c in range(RING):
                out_block(0, c, True)
            with pe.Fori(1, 2) as it:
                for c in range(RING):
                    out_block(it, c, False)
            pe.wait_ge(o_summed, KD)
            M(bank[B_O][:, :], ones[:, :], o_acc[:, :], start=True, stop=True).then_inc(ss_done, 1)

            def up_first(k):
                pe.wait_ge(g_ready2, k + 1)
                pe.wait_ge(x1_sq, k + 1)
                M(bank[B_ATT][:, :], ones[:, :], m_sq[k % 2][:, :], start=(k == 0), stop=(k == KD - 1),
                  ).then_inc(ss_done, 1)

            def up(it, c, first):
                q = Q_UP + it
                if first:
                    pe.wait_ge(o_copied, KD)
                else:
                    pe.wait_ge(up_read, 4 * it + c - 3)
                product(q, c, bank[c][:, :], g_hi, g_lo, each=up_first if first and c == 0 else None)

            for c in range(RING):
                up(0, c, True)
            with pe.Fori(1, KF // 2) as it:
                for c in range(RING):
                    up(it, c, False)

            def down(it, c, first):
                q = Q_DOWN + it
                n = 4 * it + c
                pe.wait_ge(lo_ready, 4 * q + c + 1)
                pe.wait_ge(yf_ready, n + 1)
                if first:
                    yh, yl = yf_hi[:, n, :], yf_lo[:, n, :]
                else:
                    yh = yf_hi[:, bass.ds(n, 1), :].rearrange("p a b -> p (a b)")
                    yl = yf_lo[:, bass.ds(n, 1), :].rearrange("p a b -> p (a b)")
                for m in range(KD):
                    if first and c == 0 and m < RING:
                        pe.wait_ge(up_read, N_UP - 3 + m)
                    last = block3(bank[m][:, :], c, m, yh, yl, bool(first and c == 0), False)
                last.then_inc(product_done, 1)

            for c in range(RING):
                down(0, c, True)
            with pe.Fori(1, KF // RING) as it:
                for c in range(RING):
                    down(it, c, False)
            pe.wait_ge(lo_ready, N_TILES)
            pe.wait_ge(yf_ready, KF)
            rest = KF % RING
            for m in range(KD):
                for c in range(rest):
                    n = KF - rest + c
                    last = block3(bank[m][:, :], c, m, yf_hi[:, n, :], yf_lo[:, n, :], False, c == rest - 1)
                last.then_inc(down_done, 1)
            pe.wait_ge(d_summed, KD)
            pe.wait_ge(d_copied, 1)
            M(bank[0][:, :], ones[:, :], o_acc[:, :], start=True, stop=True).then_inc(ss_done, 1)


_NAMES = ["x", "norm_pre_mix", "w_in", "conv_a_w", "conv_a_b", "lru_wa", "lru_ba", "lru_wx", "lru_bx",
          "lru_lambda", "hg_lb_logits", "hg_norm_g", "w_branch_a", "w_branch_b", "w_out", "norm_post_mix",
          "norm_pre_ffn", "w_up", "conv_f_w", "conv_f_b", "w_down", "norm_post_ffn"]


def _blocks(w):
    n = w.shape[1] // P
    return w.reshape(KD, P, n, P).transpose(2, 1, 0, 3).reshape(n, P, KD * P)


def kernel(**inputs):
    import numpy as np
    import concourse.bacc as bacc
    from concourse.bass_utils import run_bass_kernel_spmd

    a = {n: np.asarray(inputs[n]) for n in _NAMES}
    xT = np.ascontiguousarray(a["x"][0].T.reshape(KD, P, T).transpose(1, 0, 2))
    w_in = _blocks(a["w_in"][0]).reshape(8, KD, P, KD * P)
    heads = w_in[[3, 2, 4, 0, 1, 5]].transpose(1, 0, 2, 3).reshape(N_HEAD, P, KD * P)
    merge = np.stack([w_in[6], w_in[7], _blocks(a["w_branch_a"][0]), _blocks(a["w_branch_b"][0])], 1)
    up = _blocks(a["w_up"][0]).reshape(2, KF, P, KD * P).transpose(1, 0, 2, 3)
    wts = np.concatenate([heads, merge.reshape(N_MERGE, P, KD * P), _blocks(a["w_out"][0]),
                          up.reshape(N_UP, P, KD * P), a["w_down"][0].reshape(N_DOWN, P, KD * P)])
    cols = lambda v: v.reshape(-1, P).T
    per_head = [a["conv_a_w"][0][t] for t in range(4)] + [a["conv_a_b"][0], a["lru_ba"][0], a["lru_bx"][0],
                a["lru_lambda"][0], a["hg_lb_logits"][0], a["hg_lb_logits"][1], a["hg_norm_g"][0]]
    per_up = [a["conv_f_w"][0][t] for t in range(3)] + [a["conv_f_b"][0]]
    ffn = np.stack([cols(v).reshape(P, 2, KF) for v in per_up], 3).transpose(0, 2, 1, 3).reshape(P, -1)
    par = np.concatenate([np.stack([cols(v) for v in per_head], 2).reshape(P, -1),
                          cols(a["norm_pre_mix"][0]), cols(a["norm_post_mix"][0]),
                          cols(a["norm_pre_ffn"][0]), cols(a["norm_post_ffn"][0]), ffn], 1)
    lru = np.stack([a["lru_wa"][0], a["lru_wx"][0]], 2).reshape(HEADS, P, 2 * P)

    nc = bacc.Bacc("TRN2", target_bir_lowering=False, num_devices=1)
    arrays = {"xT": xT, "weights": wts, "params": np.ascontiguousarray(par), "lru_w": np.ascontiguousarray(lru)}
    args = [nc.dram_tensor(n, v.shape, mybir.dt.from_np(v.dtype), kind="ExternalInput").ap()
            for n, v in arrays.items()]
    out = nc.dram_tensor("outT", (P, KD, T), F32, kind="ExternalOutput").ap()
    layer(nc, *args, out)
    r = run_bass_kernel_spmd(nc, [arrays], core_ids=[0])
    y = np.asarray(r.results[0]["outT"])
    return np.ascontiguousarray(y.transpose(2, 1, 0).reshape(1, T, D))
```

```python
from contextlib import ExitStack

import concourse.bass as bass
from concourse import mybir

F32 = mybir.dt.float32
F32R = mybir.dt.float32r
U32 = mybir.dt.uint32
ALU = mybir.AluOpType
ACT = mybir.ActivationFunctionType

P = 128
D = 1024
T = 512
KD = D // P
HEADS = KD
CH = 32
NCH = T // CH
NT = T // P
CPT = P // CH
FF = 2816
KF = FF // P
EPS = 1e-6
RING = 4
LEAD = 2

SECT = 6
N_HEAD = SECT * HEADS
N_MERGE = 4 * KD
N_OUT = KD
N_UP = 2 * KF
N_DOWN = KF
Q_MERGE = N_HEAD // RING
Q_OUT = Q_MERGE + N_MERGE // RING
Q_UP = Q_OUT + N_OUT // RING
Q_DOWN = Q_UP + N_UP // RING
N_TILES = N_HEAD + N_MERGE + N_OUT + N_UP + N_DOWN

HPC = 11
C_BA, C_BX, C_LAM, C_L0, C_L1, C_HG = 5, 6, 7, 8, 9, 10
O_FFN = HEADS * HPC
N_PAR = O_FFN + 4 * 2 * KF
G_PRE, G_POST, G_PREF, G_POSTF = range(4)
HALF = D // 2
C_C8, C_NC8, C_LB, C_OMLB = 0, 1, 2, 3

SET_SIG = "sigmoid_and_others"
SET_EXP = "natural_log_exp_and_others"
GELU_C = 0.044715
GELU_S = 0.7978845608028654


def layer(nc, x, wts, par, lru, gains, out):
    ctx = ExitStack()
    with ctx:
        base = (nc.sbuf_base + 63) // 64 * 64
        top = [base]

        def at(name, shape, dt, offset):
            return nc.alloc_sbuf_tensor_at(name, shape, dt, offset=offset)

        def size(shape):
            n = 4
            for s in shape[1:]:
                n *= s
            return (n + 31) // 32 * 32

        def new(name, shape, dt=F32):
            t = at(name, shape, dt, top[0])
            top[0] += size(shape)
            return t

        def sem(name):
            return ctx.enter_context(nc.semaphore(name))

        w_raw = [new(f"w_raw{s}", [P, KD, P]) for s in range(RING)]
        w_hi = [new(f"w_hi{s}", [P, KD, P], F32R) for s in range(RING)]
        w_lo = [new(f"w_lo{s}", [P, KD, P], F32R) for s in range(RING)]
        pv = new("pv", [P, N_PAR])
        hc = new("hc", [P, HEADS, 4])
        hp_now = [new(f"hp_now{s}", [P, HPC]) for s in range(2)]
        hc_now = [new(f"hc_now{s}", [P, 4]) for s in range(2)]
        fp_now = [new(f"fp_now{s}", [P, 8]) for s in range(2)]
        eps_col = new("eps_col", [P, 2])
        ones = new("ones", [P, P])
        ident = new("ident", [P, P])
        amask = new("amask", [P, P])
        lru_w = [new(f"lru_w{s}", [P, 2, P]) for s in range(2)]
        dq1 = new("dq1", [P, NT, 2])
        dk1 = new("dk1", [P, NT, 2])
        dq2 = new("dq2", [P, NT, CPT])
        dk2 = new("dk2", [P, NT, CPT])
        d_tile = new("d_tile", [P, NT])
        ssq = new("ssq", [P, 16])
        rs_c = new("rs_c", [P, 16])
        sp_t = new("sp_t", [P, 8, HEADS])
        off_h = top[0]
        h_hi = new("h_hi", [P, KD, T], F32R)
        h_lo = new("h_lo", [P, KD, T], F32R)
        g_hi = at("g_hi", [P, KD, T], F32R, off_h)
        g_lo = at("g_lo", [P, KD, T], F32R, off_h + KD * T * 4)
        g_postf = at("g_postf", [P, D], F32, off_h)
        d_g = [at(f"d_g{s}", [P, D], F32, off_h + (1 + s) * D * 4) for s in range(2)]
        junk_d = at("junk_d", [P, D], F32, off_h + 3 * D * 4)
        off_y = top[0]
        yy_hi = new("yy_hi", [P, 2 * KD, T], F32R)
        yy_lo = new("yy_lo", [P, 2 * KD, T], F32R)
        x_in = at("x_in", [P, NT, D], F32, off_y)
        row = D * 4
        g_pre = at("g_pre", [P, D], F32, off_y + 4 * row)
        h_tm = [at(f"h_tm{s}", [P, D], F32, off_y + (5 + s) * row) for s in range(2)]
        junk = at("junk", [P, D], F32, off_y + 7 * row)
        g_post = at("g_post", [P, D], F32, off_y)
        g_pref = at("g_pref", [P, D], F32, off_y + row)
        o_g = [at(f"o_g{s}", [P, D], F32, off_y + (2 + s) * row) for s in range(2)]
        h2_tm = [at(f"h2_tm{s}", [P, D], F32, off_y + (4 + s) * row) for s in range(2)]
        junk_o = at("junk_o", [P, D], F32, off_y + 6 * row)
        yf_hi = at("yf_hi", [P, KF, T], F32R, off_y)
        yf_lo = at("yf_lo", [P, KF, T], F32R, off_y + KF * T * 4)
        off_t = top[0]
        rmask = new("rmask", [P, T])
        f_a = new("f_a", [P, T])
        f_b = new("f_b", [P, T])
        gcum = new("gcum", [P, T])
        e_g = new("e_g", [P, T])
        q_t = new("q_t", [P, T])
        k_d = new("k_d", [P, T])
        q_1 = new("q_1", [P, NT, 2 * CH])
        k_1 = new("k_1", [P, NT, 2 * CH])
        q_2 = new("q_2", [P, NT - 1, P])
        k_2 = new("k_2", [P, NT - 1, P])
        v_fm = new("v_fm", [P, T])
        v_tm = new("v_tm", [P, NT, P])
        kd_tm = new("kd_tm", [P, NT - 1, P])
        att = new("att", [P, NT, P])
        o_sq = v_fm
        rs_o = new("rs_o", [P, T])
        sil = new("sil", [P, T])
        xpad = new("xpad", [P, T + 8])
        xc = new("xc", [P, T])
        l_r = new("l_r", [P, T])
        l_i = new("l_i", [P, T])
        l_th = new("l_th", [P, T])
        l_2 = new("l_2", [P, T])
        l_h = new("l_h", [P, T])
        g_t = new("g_t", [P, T])
        s_all = new("s_all", [P, NT - 1, P])
        mix_hi = at("mix_hi", [P, KD, T], F32R, off_t)
        mix_lo = at("mix_lo", [P, KD, T], F32R, off_t + KD * T * 4)
        x1 = at("x1", [P, NT, D], F32, off_t + 2 * KD * T * 4)
        tmp0 = off_t + 3 * KD * T * 4
        m_a, m_b, m_ga, m_gb = [at(f"m_tmp{s}", [P, T], F32, tmp0 + s * T * 4) for s in range(4)]
        fin0 = off_y + 2 * KF * T * 4
        pads = 2 * (T + 8) * 4
        u_pad = at("u_pad", [P, 2, T + 8], F32, fin0)
        fin1 = fin0 + pads
        assert fin1 + T * 4 <= off_t + 2 * KD * T * 4
        u_c0 = at("u_c0", [P, T], F32, fin1)
        u_c1 = m_b
        u_y = m_gb
        u_c = [u_c0, u_c1]
        top[0] = max(top[0], tmp0 + 4 * T * 4)
        assert top[0] <= nc.sbuf_usable_end, (top[0], nc.sbuf_usable_end)

        bank = [ctx.enter_context(nc.psum_tensor(f"bank{b}", [P, T], F32)) for b in range(8)]
        B_FZ, B_Q, B_V, B_XA, B_GA, B_OG = 0, 1, 2, 0, 1, 2
        B_TR, B_KV, B_ATT2, B_ATT, B_O = 3, 4, 5, 6, 7

        w_landed = [sem(f"w_landed{s}") for s in range(RING)]
        hi_ready = sem("hi_ready")
        lo_ready = sem("lo_ready")
        product_done = sem("product_done")
        x_landed = [sem(f"x_landed{s}") for s in range(4)]
        par_landed = sem("par_landed")
        lru_landed = [sem(f"lru_landed{s}") for s in range(2)]
        consts_made = sem("consts_made")
        setup_v = sem("setup_v")
        setup_a = sem("setup_a")
        g_pre_landed = sem("g_pre_landed")
        x_squared = sem("x_squared")
        x_ln = sem("x_ln")
        x_rs = sem("x_rs")
        h_scaled = sem("h_scaled")
        h_turned = sem("h_turned")
        h_hi_ready = sem("h_hi_ready")
        h_ready = sem("h_ready")
        hp_ready = sem("hp_ready")
        fz_read = sem("fz_read")
        fa_ready = sem("fa_ready")
        logf_ready = sem("logf_ready")
        g_ready = sem("g_ready")
        eg_ready = sem("eg_ready")
        eng_ready = sem("eng_ready")
        dec_steps = sem("dec_steps")
        q1_ready = sem("q1_ready")
        k1_ready = sem("k1_ready")
        q2_ready = sem("q2_ready")
        k2_ready = sem("k2_ready")
        qt_ready = sem("qt_ready")
        kt_ready = sem("kt_ready")
        kd_ready = sem("kd_ready")
        v_read = sem("v_read")
        tv_done = sem("tv_done")
        vtm_ready = sem("vtm_ready")
        tkd_done = sem("tkd_done")
        kdtm_ready = sem("kdtm_ready")
        att_done = sem("att_done")
        att_ready = sem("att_ready")
        att_far_ready = sem("att_far_ready")
        kv_done = sem("kv_done")
        s_ready = sem("s_ready")
        o_done = sem("o_done")
        osq_ready = sem("osq_ready")
        osum_done = sem("osum_done")
        rso_ln = sem("rso_ln")
        rso_ready = sem("rso_ready")
        og_sig = sem("og_sig")
        sil_ready = sem("sil_ready")
        yb_scaled = sem("yb_scaled")
        yb_made = sem("yb_made")
        y_hi_ready = sem("y_hi_ready")
        y_ready = sem("y_ready")
        xa_read = sem("xa_read")
        conv_step = sem("conv_step")
        gate_r = sem("gate_r")
        gate_i = sem("gate_i")
        r_ready = sem("r_ready")
        i_ready = sem("i_ready")
        th_ready = sem("th_ready")
        th_clamped = sem("th_clamped")
        a_ready = sem("a_ready")
        l1_ready = sem("l1_ready")
        l2_ready = sem("l2_ready")
        ix_ready = sem("ix_ready")
        ld_ready = sem("ld_ready")
        w_sqrt = sem("w_sqrt")
        u_ready = sem("u_ready")
        lru_h = sem("lru_h")
        ga_sq = sem("ga_sq")
        ga_1 = sem("ga_1")
        ga_2 = sem("ga_2")
        ga_th = sem("ga_th")
        ga_read = sem("ga_read")
        ya_made = sem("ya_made")
        sig_a = sem("sig_a")
        sig_b = sem("sig_b")
        za_read = sem("za_read")
        zb_read = sem("zb_read")
        mix_sum = sem("mix_sum")
        mix_hi_ready = sem("mix_hi_ready")
        mix_ready = sem("mix_ready")
        x_again = sem("x_again")
        g_post_landed = sem("g_post_landed")
        g_pref_landed = sem("g_pref_landed")
        o_tile = sem("o_tile")
        o_squared = sem("o_squared")
        o_gained = sem("o_gained")
        o_ss = sem("o_ss")
        o_ln = sem("o_ln")
        o_rs = sem("o_rs")
        x1_ready = sem("x1_ready")
        x1_squared = sem("x1_squared")
        x1_ln = sem("x1_ln")
        x1_rs = sem("x1_rs")
        h2_scaled = sem("h2_scaled")
        h2_turned = sem("h2_turned")
        h2_hi_ready = sem("h2_hi_ready")
        h2_ready = sem("h2_ready")
        pad_zero = sem("pad_zero")
        fp_ready = sem("fp_ready")
        pad_ready = sem("pad_ready")
        tap2 = sem("tap2")
        tap1 = sem("tap1")
        tap0 = sem("tap0")
        gelu_done = sem("gelu_done")
        y_made = sem("y_made")
        yf_hi_ready = sem("yf_hi_ready")
        yf_ready = sem("yf_ready")
        g_postf_landed = sem("g_postf_landed")
        d_tile_done = sem("d_tile_done")
        d_squared = sem("d_squared")
        d_gained = sem("d_gained")
        d_ss = sem("d_ss")
        d_ln = sem("d_ln")
        d_rs = sem("d_rs")
        x2_ready = sem("x2_ready")
        stored = sem("stored")

        block = ctx.enter_context(nc.Block())

        def col(t, c):
            return t[:, c:c + 1]

        @block.sync
        def _(sp):
            def tile(q, c, reuse):
                if reuse:
                    sp.wait_ge(lo_ready, 4 * q + c - RING + 1)
                src = wts[4 * q + c] if isinstance(q, int) else \
                    wts[bass.ds(4 * q + c, 1)].rearrange("o p n -> (o p) n")
                sp.dma_start(w_raw[c][:, :, :].rearrange("p a b -> p (a b)"), src).then_inc(w_landed[c], 16)

            sp.dma_start(pv[:, :], par).then_inc(par_landed, 16)
            for t in range(NT):
                sp.dma_start(x_in[:, t, :], x[P * t:P * t + P, :]).then_inc(x_landed[t], 16)
                if t == 0:
                    sp.dma_start(g_pre[:, :], gains[G_PRE:G_PRE + 1, :].to_broadcast([P, D]))\
                        .then_inc(g_pre_landed, 16)
            tile(0, 0, False)
            for c in range(1, RING):
                tile(0, c, False)
            with sp.Fori(1, Q_MERGE + 3) as q:
                for c in range(RING):
                    tile(q, c, True)
            sp.wait_ge(y_ready, 2 * HEADS)
            sp.dma_start(x1[:, :, :], x.rearrange("(t p) d -> p t d", p=P)).then_inc(x_again, 16)
            with sp.Fori(Q_MERGE + 3, N_TILES // RING) as q:
                for c in range(RING):
                    tile(q, c, True)
            for c in range(N_TILES % RING):
                tile(N_TILES // RING, c, True)
            for t in range(NT):
                sp.wait_ge(x2_ready, t + 1)
                sp.dma_start(out[P * t:P * t + P, :], x1[:, t, :]).then_inc(stored, 16)
            sp.wait_ge(stored, 16 * NT)

        CONSTS = 16
        DSTEPS = 9

        @block.gpsimd
        def _(pool):
            nc.gpsimd.memset(eps_col[:, 0:1], EPS).then_inc(consts_made, 1)
            nc.gpsimd.memset(eps_col[:, 1:2], 1.0).then_inc(consts_made, 1)
            nc.gpsimd.memset(ones[:, :], 1.0).then_inc(consts_made, 1)
            nc.gpsimd.memset(ident[:, :], 0.0).then_inc(consts_made, 1)
            nc.gpsimd.memset(amask[:, :], 1.0).then_inc(consts_made, 1)
            nc.gpsimd.memset(rmask[:, :], 1.0).then_inc(consts_made, 1)
            nc.gpsimd.memset(att[:, :, :], 0.0).then_inc(consts_made, 1)
            nc.gpsimd.memset(dq2[:, :, 0:1], 1.0).then_inc(consts_made, 1)
            nc.gpsimd.memset(dk2[:, :, CPT - 1:CPT], 1.0).then_inc(consts_made, 1)
            nc.gpsimd.memset(dq1[:, :, 0:1], 1.0).then_inc(consts_made, 1)
            nc.gpsimd.memset(dk1[:, :, 1:2], 1.0).then_inc(consts_made, 1)
            nc.gpsimd.memset(xpad[:, 0:8], 0.0).then_inc(consts_made, 1)
            pool.wait_ge(consts_made, 12)
            nc.gpsimd.memset(rmask[:, :].rearrange("p (n c) -> p n c", c=CH)[:, :, 0:1], 0.0)\
                .then_inc(consts_made, 1)
            nc.gpsimd.affine_select(out=ident[:, :], in_=ident[:, :], compare_op=ALU.not_equal, fill=1.0,
                                    base=0, pattern=[[-1, P]], channel_multiplier=1).then_inc(consts_made, 1)
            nc.gpsimd.affine_select(out=amask[:, :], in_=amask[:, :], compare_op=ALU.is_ge, fill=0.0,
                                    base=0, pattern=[[1, P]], channel_multiplier=-1).then_inc(consts_made, 1)
            pool.wait_ge(consts_made, 15)
            am = amask[:, :].rearrange("p (b c) -> p b c", c=CH)
            nc.gpsimd.affine_select(out=am, in_=am, compare_op=ALU.is_ge, fill=0.0,
                                    base=0, pattern=[[-CH, CPT], [0, CH]], channel_multiplier=1)\
                .then_inc(consts_made, 1)

            def decays(j, first):
                d = e_g[:, :].rearrange("p (t n c) -> p t n c", n=CPT, c=CH)[:, :, :, CH - 1]
                one = dq2[:, :, 0]

                def times(o, a, b):
                    nc.gpsimd.tensor_tensor(o, a, b, ALU.mult).then_inc(dec_steps, 1)

                pool.wait_ge(eg_ready, j + 1)
                if not first:
                    pool.wait_ge(k2_ready, j)
                    pool.wait_ge(s_ready, 3 * j)
                times(dq1[:, :, 1], d[:, :, 2], one)
                times(dk1[:, :, 0], d[:, :, 1], one)
                times(dq2[:, :, 1], d[:, :, 0], one)
                times(dk2[:, :, 2], d[:, :, 3], one)
                times(dq2[:, :, 2], d[:, :, 0], d[:, :, 1])
                times(dk2[:, :, 1], d[:, :, 2], d[:, :, 3])
                pool.wait_ge(dec_steps, DSTEPS * j + 6)
                times(dq2[:, :, 3], dq2[:, :, 2], d[:, :, 2])
                times(dk2[:, :, 0], dk2[:, :, 1], d[:, :, 1])
                pool.wait_ge(dec_steps, DSTEPS * j + 8)
                times(d_tile[:, :], dq2[:, :, 3], d[:, :, 3])

            pool.wait_ge(consts_made, CONSTS)
            decays(0, True)
            with pool.Fori(1, HEADS) as j:
                decays(j, False)


        @block.scalar
        def _(act):
            A = nc.scalar.activation

            def split_hi(q, c):
                act.wait_ge(w_landed[c % RING], 16 * (q + c // RING + 1))
                if not (isinstance(q, int) and 4 * q + c < RING):
                    act.wait_ge(product_done, 4 * q + c - RING + 1)
                A(w_hi[c % RING][:, :, :], w_raw[c % RING][:, :, :], ACT.Copy).then_inc(hi_ready, 1)

            def split_at(q, c):
                if not (isinstance(q, int) and 4 * q + c + LEAD >= N_TILES):
                    split_hi(q, c + LEAD)

            act.wait_ge(consts_made, CONSTS)
            nc.scalar.preload_act_table_set(SET_EXP)
            act.wait_ge(setup_v, 5)
            A(sp_t[:, 0:3, :], sp_t[:, 0:3, :], ACT.Exp).then_inc(setup_a, 1)
            split_hi(0, 0)

            def turn_hi(dst, turned, hi_done, t):
                for b in range(2):
                    act.wait_ge(turned, 2 * t + b + 1)
                    A(dst[:, 4 * b:4 * b + 4, P * t:P * t + P],
                      bank[2 * t + b][:, :].rearrange("p (a c) -> p a c", c=P), ACT.Copy).then_inc(hi_done, 1)

            def rms(c, ss, ln, rs, n):
                act.wait_ge(ss, n)
                A(col(rs_c, c), col(ssq, c), ACT.Ln, bias=col(eps_col, 0), scale=1.0 / D).then_inc(ln, 1)
                act.wait_ge(ln, (n - 1) % NT + 1)
                A(col(rs_c, c), col(rs_c, c), ACT.Exp, scale=-0.5).then_inc(rs, 1)

            for t in range(NT + 1):
                if t < NT:
                    act.wait_ge(x_landed[t], 16)
                    if t >= 1:
                        act.wait_ge(x_squared, t)
                    A(junk[:, :], x_in[:, t, :], ACT.Square, accum_out=col(ssq, t)).then_inc(x_squared, 1)
                    rms(t, x_squared, x_ln, x_rs, t + 1)
                if t >= 1:
                    turn_hi(h_hi, h_turned, h_hi_ready, t - 1)
            split_hi(0, 1)

            def lru_gates(j, pj):
                act.wait_ge(product_done, SECT * j + 6)
                if not is0(j):
                    act.wait_ge(yb_made, j)
                A(sil[:, :], bank[B_OG][:, :], ACT.Sigmoid).then_inc(og_sig, 1)
                act.wait_ge(gate_r, j + 1)
                if not is0(j):
                    act.wait_ge(lru_h, j)
                A(l_r[:, :], bank[B_ATT][:, :], ACT.Sigmoid, bias=col(hp_now[pj], C_BA)).then_inc(r_ready, 1)
                act.wait_ge(gate_i, j + 1)
                A(l_i[:, :], bank[B_TR][:, :], ACT.Sigmoid, bias=col(hp_now[pj], C_BX)).then_inc(i_ready, 1)
                act.wait_ge(r_ready, j + 1)
                if not is0(j):
                    act.wait_ge(u_ready, j)
                A(l_th[:, :], l_r[:, :], ACT.Tanh, scale=col(hc_now[pj], C_C8)).then_inc(th_ready, 1)

            def is0(j):
                return isinstance(j, int) and j == 0

            def front_sig(j):
                act.wait_ge(product_done, SECT * j + 1)
                if not is0(j):
                    act.wait_ge(att_done, j)
                    act.wait_ge(kd_ready, j)
                A(f_a[:, :], bank[B_FZ][:, :], ACT.Sigmoid).then_inc(fa_ready, 1)
                A(f_b[:, :], bank[B_FZ][:, :], ACT.Sigmoid, scale=-1.0).then_inc(fz_read, 1)

            def front_log(j, pj):
                act.wait_ge(fa_ready, j + 1)
                act.wait_ge(hp_ready, 2 * j + 2)
                A(f_a[:, :], f_a[:, :], ACT.Ln, bias=col(hc_now[pj], C_LB), scale=col(hc_now[pj], C_OMLB))\
                    .then_inc(logf_ready, 1)

            def front_exp(j):
                act.wait_ge(g_ready, j + 1)
                if not is0(j):
                    act.wait_ge(dec_steps, DSTEPS * j)
                    act.wait_ge(kd_ready, j)
                A(e_g[:, :], gcum[:, :], ACT.Exp).then_inc(eg_ready, 1)
                act.wait_ge(eg_ready, j + 1)
                A(gcum[:, :], gcum[:, :], ACT.Exp, scale=-1.0).then_inc(eng_ready, 1)

            def lru_logs(j, pj):
                act.wait_ge(th_ready, j + 1)
                A(l_r[:, :], l_r[:, :], ACT.Exp, scale=col(hc_now[pj], C_NC8)).then_inc(a_ready, 1)
                act.wait_ge(th_clamped, j + 1)
                act.wait_ge(ga_th, j + 1)
                A(l_2[:, :], l_th[:, :], ACT.Ln, bias=col(eps_col, 1)).then_inc(l2_ready, 1)
                act.wait_ge(l2_ready, j + 1)
                A(l_th[:, :], l_th[:, :], ACT.Ln, scale=2.0).then_inc(l1_ready, 1)

            def lru_root(j):
                act.wait_ge(ld_ready, j + 1)
                A(l_th[:, :], l_th[:, :], ACT.Exp, scale=0.5).then_inc(w_sqrt, 1)

            def o_square(j):
                act.wait_ge(o_done, j + 1)
                if not is0(j):
                    act.wait_ge(osum_done, j)
                A(o_sq[:, :], bank[B_O][:, :], ACT.Square).then_inc(osq_ready, 1)

            def o_rms(j):
                act.wait_ge(osum_done, j + 1)
                if not is0(j):
                    act.wait_ge(yb_scaled, j)
                A(rs_o[:, :], bank[B_TR][:, :], ACT.Ln, bias=col(eps_col, 0), scale=1.0 / P).then_inc(rso_ln, 1)
                act.wait_ge(rso_ln, j + 1)
                A(rs_o[:, :], rs_o[:, :], ACT.Exp, scale=-0.5).then_inc(rso_ready, 1)

            def finish_a(j, pj):
                lru_logs(j, pj)
                o_square(j)
                lru_root(j)

            def head(i, pj, first):
                j = 2 * i + pj
                q, c = 3 * i, SECT * pj
                pp = 1 - pj
                split_at(q, c)
                if not first:
                    nc.scalar.preload_act_table_set(SET_SIG)
                    lru_gates(j - 1, pp)
                split_at(q, c + 1)
                if first:
                    nc.scalar.preload_act_table_set(SET_SIG)
                front_sig(j)
                nc.scalar.preload_act_table_set(SET_EXP)
                front_log(j, pj)
                if not first:
                    lru_logs(j - 1, pp)
                front_exp(j)
                if not first:
                    o_square(j - 1)
                    lru_root(j - 1)
                if not is0(i):
                    act.wait_ge(gate_i, j - 1)
                act.dma_start(lru_w[pj][:, :, :].rearrange("p a b -> p (a b)"),
                              lru[bass.ds(j, 1), :, :].rearrange("o p n -> (o p) n")).then_inc(lru_landed[pj], 16)
                split_at(q, c + 2)
                if not first:
                    o_rms(j - 1)
                split_at(q, c + 3)
                act.wait_ge(product_done, SECT * j + 3)
                if not first:
                    act.wait_ge(osum_done, j)
                A(v_fm[:, :], bank[B_V][:, :], ACT.Copy).then_inc(v_read, 1)
                act.wait_ge(tv_done, j + 1)
                if not first:
                    act.wait_ge(o_done, j)
                A(v_tm[:, :, :].rearrange("p a b -> p (a b)"), bank[B_TR][:, :], ACT.Copy).then_inc(vtm_ready, 1)
                split_at(q, c + 4)
                act.wait_ge(product_done, SECT * j + 4)
                if not first:
                    act.wait_ge(conv_step, 4 * j)
                A(xpad[:, 3:3 + T], bank[B_XA][:, :], ACT.Copy).then_inc(xa_read, 1)
                split_at(q, c + 5)
                act.wait_ge(product_done, SECT * j + 5)
                if not first:
                    act.wait_ge(ld_ready, j)
                A(l_2[:, :], bank[B_GA][:, :], ACT.Square).then_inc(ga_sq, 1)
                nc.scalar.preload_act_table_set(SET_SIG)
                act.wait_ge(ga_2, j + 1)
                A(g_t[:, :], l_2[:, :], ACT.Tanh, scale=GELU_S).then_inc(ga_th, 1)

            head(0, 0, True)
            head(0, 1, False)
            with act.Fori(1, HEADS // 2) as i:
                head(i, 0, False)
                head(i, 1, False)

            def merge(m, first):
                q = Q_MERGE + m
                split_at(q, 0)
                if first:
                    lru_gates(HEADS - 1, 1)
                    nc.scalar.preload_act_table_set(SET_EXP)
                    lru_logs(HEADS - 1, 1)
                    o_square(HEADS - 1)
                    lru_root(HEADS - 1)
                split_at(q, 1)
                if first:
                    o_rms(HEADS - 1)
                    act.wait_ge(y_ready, 2 * HEADS)
                    nc.scalar.preload_act_table_set(SET_SIG)
                else:
                    act.wait_ge(mix_sum, m)
                act.wait_ge(product_done, 4 * q + 1)
                A(m_ga[:, :], bank[0][:, :], ACT.Sigmoid).then_inc(sig_a, 1)
                act.wait_ge(product_done, 4 * q + 2)
                A(m_gb[:, :], bank[2][:, :], ACT.Sigmoid).then_inc(sig_b, 1)
                split_at(q, 2)
                split_at(q, 3)

            merge(0, True)
            with act.Fori(1, KD) as m:
                merge(m, False)

            act.wait_ge(product_done, RING * Q_OUT)
            act.dma_start(g_post[:, :], gains[G_POST:G_POST + 1, :].to_broadcast([P, D])).then_inc(g_post_landed, 16)
            act.dma_start(g_pref[:, :], gains[G_PREF:G_PREF + 1, :].to_broadcast([P, D])).then_inc(g_pref_landed, 16)
            nc.scalar.preload_act_table_set(SET_EXP)
            for c in range(N_OUT - LEAD):
                split_at(Q_OUT, c)

            def squares(t, tile_done, squared, junk_buf, c0):
                act.wait_ge(tile_done, t + 1)
                for b in range(2):
                    if t or b:
                        act.wait_ge(squared, 2 * t + b)
                    A(junk_buf[:, 0:HALF], bank[2 * t + b][:, :], ACT.Square, accum_out=col(ssq, c0 + 2 * t + b))\
                        .then_inc(squared, 1)

            for t in range(NT):
                if t >= NT - 1:
                    for c in range(N_OUT - LEAD, N_OUT):
                        split_at(Q_OUT, c)
                squares(t, o_tile, o_squared, junk_o, 4)
                rms(4 + 2 * t, o_ss, o_ln, o_rs, t + 1)
                act.wait_ge(x1_ready, t + 1)
                if t:
                    act.wait_ge(x1_squared, t)
                A(junk_o[:, :], x1[:, t, :], ACT.Square, accum_out=col(ssq, 12 + t)).then_inc(x1_squared, 1)
                rms(12 + t, x1_squared, x1_ln, x1_rs, t + 1)
                turn_hi(g_hi, h2_turned, h2_hi_ready, t)
            nc.scalar.preload_act_table(ACT.Gelu_apprx_tanh)

            def pair(it, e, first):
                q = Q_UP + it
                n = 2 * it + e
                for v in range(2):
                    c = 2 * e + v
                    split_at(q, c)
                    act.wait_ge(product_done, 4 * q + c + 1)
                    act.wait_ge(fp_ready, n + 1)
                    if first:
                        act.wait_ge(pad_zero, 1)
                    else:
                        act.wait_ge(tap0, 2 * n)
                        act.wait_ge(y_made, n)
                    A(u_pad[:, v, 2:2 + T], bank[c][:, :], ACT.Copy).then_inc(pad_ready, 1)
                    A(u_c[v][:, :], bank[c][:, :], ACT.Identity, bias=col(fp_now[e], 4 * v + 3),
                      scale=col(fp_now[e], 4 * v + 2)).then_inc(tap2, 1)
                act.wait_ge(tap0, 2 * n + 1)
                A(u_c[0][:, :], u_c[0][:, :], ACT.Gelu_apprx_tanh).then_inc(gelu_done, 1)

            pair(0, 0, True)
            pair(0, 1, False)
            with act.Fori(1, KF // 2) as it:
                pair(it, 0, False)
                pair(it, 1, False)

            act.wait_ge(product_done, RING * Q_DOWN)
            act.dma_start(g_postf[:, :], gains[G_POSTF:G_POSTF + 1, :].to_broadcast([P, D]))\
                .then_inc(g_postf_landed, 16)
            nc.scalar.preload_act_table_set(SET_EXP)
            with act.Fori(0, (N_DOWN - LEAD) // RING) as it:
                for c in range(RING):
                    split_at(Q_DOWN + it, c)
            for t in range(NT):
                squares(t, d_tile_done, d_squared, junk_d, 4)
                rms(4 + 2 * t, d_ss, d_ln, d_rs, t + 1)

        @block.vector
        def _(dve):
            V = nc.vector

            def is0(j):
                return isinstance(j, int) and j == 0

            def split_lo(q, c):
                s = c % RING
                dve.wait_ge(hi_ready, 4 * q + c + 1)
                V.tensor_tensor(w_lo[s][:, :, :], w_raw[s][:, :, :], w_hi[s][:, :, :].bitcast(F32),
                                ALU.subtract).then_inc(lo_ready, 1)

            def split_at(q, c):
                if not (isinstance(q, int) and 4 * q + c + LEAD >= N_TILES):
                    split_lo(q, c + LEAD)

            def at_j(t, j):
                return t[:, bass.ds(j, 1), :].rearrange("p a b -> p (a b)")

            steps = [0]

            def link(ins):
                steps[0] += 1
                ins.then_inc(setup_v, 1)
                dve.wait_ge(setup_v, steps[0])

            hpv = pv[:, 0:O_FFN].rearrange("p (h c) -> p c h", c=HPC)
            lam, l0, l1 = hpv[:, C_LAM, :], hpv[:, C_L0, :], hpv[:, C_L1, :]
            s = [sp_t[:, a, :] for a in range(8)]
            dve.wait_ge(par_landed, 16)
            link(V.tensor_tensor(s[3], l0, l1, ALU.max))
            link(V.tensor_tensor(s[0], l0, s[3], ALU.subtract))
            link(V.tensor_tensor(s[1], l1, s[3], ALU.subtract))
            link(V.tensor_scalar(s[4], lam, -1.0, None, ALU.mult))
            link(V.tensor_tensor(s[2], lam, s[4], ALU.min))
            dve.wait_ge(setup_a, 1)
            link(V.tensor_tensor(s[3], s[0], s[1], ALU.add))
            link(V.reciprocal(s[3], s[3]))
            link(V.tensor_tensor(hc[:, :, C_LB], s[0], s[3], ALU.mult))
            link(V.tensor_scalar(hc[:, :, C_OMLB], hc[:, :, C_LB], -1.0, 1.0, ALU.mult, ALU.add))
            link(V.tensor_scalar(s[5], s[2], 2.0, None, ALU.add))
            link(V.reciprocal(s[5], s[5]))
            link(V.tensor_tensor(s[5], s[2], s[5], ALU.mult))
            link(V.tensor_tensor(s[6], s[5], s[5], ALU.mult))
            link(V.tensor_scalar(s[7], s[6], 1.0 / 15, None, ALU.mult))
            for odd in (13, 11, 9, 7, 5, 3):
                link(V.scalar_tensor_tensor(out=s[7], in0=s[7], scalar=1.0 / odd, in1=s[6],
                                            op0=ALU.add, op1=ALU.mult))
            link(V.scalar_tensor_tensor(out=s[7], in0=s[7], scalar=1.0, in1=s[5], op0=ALU.add, op1=ALU.mult))
            link(V.tensor_scalar(s[4], s[4], 0.0, 8.0, ALU.max, ALU.mult))
            link(V.scalar_tensor_tensor(out=hc[:, :, C_C8], in0=s[7], scalar=16.0, in1=s[4],
                                        op0=ALU.mult, op1=ALU.add))
            link(V.tensor_scalar(hc[:, :, C_NC8], hc[:, :, C_C8], -1.0, None, ALU.mult))

            def turn_lo(dst_hi, dst_lo, hi_done, done, t):
                for b in range(2):
                    dve.wait_ge(hi_done, 2 * t + b + 1)
                    V.tensor_tensor(dst_lo[:, 4 * b:4 * b + 4, P * t:P * t + P],
                                    bank[2 * t + b][:, :].rearrange("p (a c) -> p a c", c=P),
                                    dst_hi[:, 4 * b:4 * b + 4, P * t:P * t + P].bitcast(F32), ALU.subtract)\
                        .then_inc(done, 1)

            split_lo(0, 0)
            dve.wait_ge(g_pre_landed, 16)
            for t in range(NT + 1):
                if t < NT:
                    dve.wait_ge(x_rs, t + 1)
                    if t >= 2:
                        dve.wait_ge(h_turned, 2 * t - 2)
                    V.scalar_tensor_tensor(out=h_tm[t % 2][:, :], in0=x_in[:, t, :], scalar=col(rs_c, t),
                                           in1=g_pre[:, :], op0=ALU.mult, op1=ALU.mult).then_inc(h_scaled, 1)
                if t >= 1:
                    turn_lo(h_hi, h_lo, h_hi_ready, h_ready, t - 1)
            split_lo(0, 1)

            def params(j, pj, first):
                if not first:
                    dve.wait_ge(y_ready, 2 * j - 2)
                V.tensor_copy(hp_now[pj][:, :], pv[:, bass.ds(j * HPC, HPC)]).then_inc(hp_ready, 1)
                V.tensor_copy(hc_now[pj][:, :], at_j(hc, j)).then_inc(hp_ready, 1)

            def lru_1(j):
                dve.wait_ge(og_sig, j + 1)
                V.tensor_tensor(sil[:, :], bank[B_OG][:, :], sil[:, :], ALU.mult).then_inc(sil_ready, 1)
                dve.wait_ge(th_ready, j + 1)
                V.tensor_scalar(l_th[:, :], l_th[:, :], 2.0 ** -63, None, ALU.max).then_inc(th_clamped, 1)
                dve.wait_ge(i_ready, j + 1)
                V.tensor_tensor(l_i[:, :], l_i[:, :], xc[:, :], ALU.mult).then_inc(ix_ready, 1)

            def scan_g(j):
                dve.wait_ge(logf_ready, j + 1)
                if not is0(j):
                    dve.wait_ge(kt_ready, j)
                V.tensor_tensor_scan(out=gcum[:, :], data0=rmask[:, :], data1=f_a[:, :], initial=0.0,
                                     op0=ALU.mult, op1=ALU.add).then_inc(g_ready, 1)

            def lru_2(j):
                dve.wait_ge(l1_ready, j + 1)
                V.tensor_tensor(l_th[:, :], l_th[:, :], l_2[:, :], ALU.subtract).then_inc(ld_ready, 1)

            def lru_3(j):
                dve.wait_ge(w_sqrt, j + 1)
                dve.wait_ge(ix_ready, j + 1)
                V.tensor_tensor(l_i[:, :], l_i[:, :], l_th[:, :], ALU.mult).then_inc(u_ready, 1)
                dve.wait_ge(u_ready, j + 1)
                dve.wait_ge(a_ready, j + 1)
                if not is0(j):
                    dve.wait_ge(y_ready, 2 * j)
                V.tensor_tensor_scan(out=l_h[:, :], data0=l_r[:, :], data1=l_i[:, :], initial=0.0,
                                     op0=ALU.mult, op1=ALU.add).then_inc(lru_h, 1)
                dve.wait_ge(lru_h, j + 1)
                dve.wait_ge(ga_read, j + 1)
                V.scalar_tensor_tensor(out=l_h[:, :], in0=g_t[:, :], scalar=0.5, in1=l_h[:, :],
                                       op0=ALU.mult, op1=ALU.mult).then_inc(ya_made, 1)
                dve.wait_ge(ya_made, j + 1)
                V.tensor_scalar(at_j(yy_hi, j), l_h[:, :], 1.0, None, ALU.mult).then_inc(y_hi_ready, 1)

            def front(j, pj):
                dve.wait_ge(product_done, SECT * j + 2)
                dve.wait_ge(eg_ready, j + 1)
                if not is0(j):
                    dve.wait_ge(o_done, j)
                V.tensor_tensor(q_t[:, :], bank[B_Q][:, :], e_g[:, :], ALU.mult).then_inc(qt_ready, 1)
                dve.wait_ge(hp_ready, 2 * j + 2)
                dve.wait_ge(fz_read, j + 1)
                dve.wait_ge(eng_ready, j + 1)
                V.scalar_tensor_tensor(out=f_b[:, :], in0=f_b[:, :], scalar=col(hc_now[pj], C_OMLB),
                                       in1=gcum[:, :], op0=ALU.mult, op1=ALU.mult).then_inc(kt_ready, 1)
                dve.wait_ge(kt_ready, j + 1)
                if not is0(j):
                    dve.wait_ge(k2_ready, j)
                    dve.wait_ge(att_done, j)
                chunks = lambda a: a.rearrange("p (n c) -> p n c", c=CH)
                over = lambda a, n: a.unsqueeze(2).to_broadcast([P, n, CH])
                V.tensor_tensor(chunks(k_d[:, :]), chunks(f_b[:, :]), over(chunks(e_g[:, :])[:, :, CH - 1], NCH),
                                ALU.mult).then_inc(kd_ready, 1)
                dve.wait_ge(dec_steps, DSTEPS * j + DSTEPS)
                dve.wait_ge(qt_ready, j + 1)
                dve.wait_ge(kd_ready, j + 1)
                half = lambda a, h: a.rearrange("p (t h n c) -> p t h n c", h=2, n=2, c=CH)[:, :, h, :, :]
                wide = lambda a: a.unsqueeze(3).to_broadcast([P, NT, 2, CH])
                two = lambda a: a.rearrange("p t (n c) -> p t n c", c=CH)
                V.tensor_tensor(two(q_1[:, :, :]), half(q_t[:, :], 1), wide(dq1[:, :, :]), ALU.mult)\
                    .then_inc(q1_ready, 1)
                V.tensor_tensor(two(k_1[:, :, :]), half(k_d[:, :], 0), wide(dk1[:, :, :]), ALU.mult)\
                    .then_inc(k1_ready, 1)
                n3 = NCH - CPT
                flat = lambda a: a.rearrange("p a b -> p (a b)")
                V.tensor_tensor(chunks(flat(q_2[:, :, :])), chunks(q_t[:, P:T]), over(flat(dq2[:, 1:NT, :]), n3),
                                ALU.mult).then_inc(q2_ready, 1)
                if not is0(j):
                    dve.wait_ge(tkd_done, j)
                V.tensor_tensor(chunks(flat(k_2[:, :, :])), chunks(k_d[:, 0:T - P]), over(flat(dk2[:, 0:NT - 1, :]), n3),
                                ALU.mult).then_inc(k2_ready, 1)

            def out_b(j, pj):
                dve.wait_ge(rso_ready, j + 1)
                V.scalar_tensor_tensor(out=rs_o[:, :], in0=bank[B_O][:, :], scalar=col(hp_now[pj], C_HG),
                                       in1=rs_o[:, :], op0=ALU.mult, op1=ALU.mult).then_inc(yb_scaled, 1)
                dve.wait_ge(yb_scaled, j + 1)
                dve.wait_ge(sil_ready, j + 1)
                V.tensor_tensor(sil[:, :], rs_o[:, :], sil[:, :], ALU.mult).then_inc(yb_made, 1)
                dve.wait_ge(yb_made, j + 1)
                V.tensor_scalar(at_j(yy_hi, j + KD), sil[:, :], 1.0, None, ALU.mult).then_inc(y_hi_ready, 1)

            def split_y(j):
                dve.wait_ge(y_hi_ready, 2 * j + 1)
                V.tensor_tensor(at_j(yy_lo, j), l_h[:, :], at_j(yy_hi, j).bitcast(F32), ALU.subtract)\
                    .then_inc(y_ready, 1)
                dve.wait_ge(y_hi_ready, 2 * j + 2)
                V.tensor_tensor(at_j(yy_lo, j + KD), sil[:, :], at_j(yy_hi, j + KD).bitcast(F32), ALU.subtract)\
                    .then_inc(y_ready, 1)

            def chain(j):
                dve.wait_ge(kv_done, j + 1)
                kv = [bank[B_KV][:, P * t:P * t + P] for t in range(NT - 1)]
                if not is0(j):
                    dve.wait_ge(o_done, j)
                V.tensor_copy(s_all[:, 0, :], kv[0]).then_inc(s_ready, 1)
                for t in range(1, NT - 1):
                    dve.wait_ge(s_ready, 3 * j + t)
                    V.scalar_tensor_tensor(out=s_all[:, t, :], in0=s_all[:, t - 1, :], scalar=col(d_tile, t),
                                           in1=kv[t], op0=ALU.mult, op1=ALU.add).then_inc(s_ready, 1)

            def head(i, pj, first):
                j = 2 * i + pj
                q, c = 3 * i, SECT * pj
                pp = 1 - pj
                split_at(q, c)
                params(j, pj, is0(i))
                if not first:
                    lru_1(j - 1)
                split_at(q, c + 1)
                scan_g(j)
                if not first:
                    lru_2(j - 1)
                split_at(q, c + 2)
                front(j, pj)
                if not first:
                    lru_3(j - 1)
                    out_b(j - 1, pp)
                split_at(q, c + 3)
                if not first:
                    split_y(j - 1)
                dve.wait_ge(tkd_done, j + 1)
                if not first:
                    dve.wait_ge(kv_done, j)
                V.tensor_copy(kd_tm[:, :, :].rearrange("p a b -> p (a b)"), bank[B_TR][:, 0:T - P])\
                    .then_inc(kdtm_ready, 1)
                split_at(q, c + 4)
                dve.wait_ge(consts_made, CONSTS)
                dve.wait_ge(att_done, j + 1)
                if not first:
                    dve.wait_ge(o_done, j)
                V.copy_predicated(out=att[:, :, :], mask=amask[:, :].bitcast(U32).unsqueeze(1)
                                  .to_broadcast([P, NT, P]),
                                  data=bank[B_ATT][:, :].rearrange("p (a b) -> p a b", b=P)).then_inc(att_ready, 1)
                far = bank[B_ATT2][:, :].rearrange("p (l t c) -> p l t c", l=2, t=NT)
                dve.wait_ge(att_ready, j + 1)
                for b in (0, 2):
                    V.tensor_copy(att[CH * b:CH * b + CH, :, CH * (b + 1):CH * (b + 2)],
                                  far[CH * b:CH * b + CH, 0, :, CH * (b // 2):CH * (b // 2) + CH])\
                        .then_inc(att_far_ready, 1)
                V.tensor_copy(att[0:2 * CH, :, 2 * CH:P], far[0:2 * CH, 1, :, :]).then_inc(att_far_ready, 1)
                dve.wait_ge(xa_read, j + 1)
                if not first:
                    dve.wait_ge(gate_i, j)
                    dve.wait_ge(ix_ready, j)
                V.tensor_scalar(xc[:, :], xpad[:, 3:3 + T], col(hp_now[pj], 3), col(hp_now[pj], 4),
                                ALU.mult, ALU.add).then_inc(conv_step, 1)
                for t in (2, 1, 0):
                    dve.wait_ge(conv_step, 4 * j + 3 - t)
                    V.scalar_tensor_tensor(out=xc[:, :], in0=xpad[:, t:t + T], scalar=col(hp_now[pj], t),
                                           in1=xc[:, :], op0=ALU.mult, op1=ALU.add).then_inc(conv_step, 1)
                split_at(q, c + 5)
                dve.wait_ge(ga_sq, j + 1)
                V.tensor_scalar(l_2[:, :], l_2[:, :], GELU_C, 1.0, ALU.mult, ALU.add).then_inc(ga_1, 1)
                dve.wait_ge(ga_1, j + 1)
                V.tensor_tensor(l_2[:, :], bank[B_GA][:, :], l_2[:, :], ALU.mult).then_inc(ga_2, 1)
                chain(j)
                dve.wait_ge(ga_th, j + 1)
                V.scalar_tensor_tensor(out=g_t[:, :], in0=g_t[:, :], scalar=1.0, in1=bank[B_GA][:, :],
                                       op0=ALU.add, op1=ALU.mult).then_inc(ga_read, 1)

            head(0, 0, True)
            head(0, 1, False)
            with dve.Fori(1, HEADS // 2) as i:
                head(i, 0, False)
                head(i, 1, False)

            def merge(m, first):
                q = Q_MERGE + m
                split_at(q, 0)
                if first:
                    lru_1(HEADS - 1)
                    lru_2(HEADS - 1)
                split_at(q, 1)
                if first:
                    lru_3(HEADS - 1)
                    out_b(HEADS - 1, 1)
                    split_y(HEADS - 1)
                split_at(q, 2)
                dve.wait_ge(sig_a, m + 1)
                dve.wait_ge(product_done, 4 * q + 3)
                if not first:
                    dve.wait_ge(mix_ready, m)
                V.tensor_tensor(m_a[:, :], bank[1][:, :], m_ga[:, :], ALU.mult).then_inc(za_read, 1)
                split_at(q, 3)
                dve.wait_ge(sig_b, m + 1)
                dve.wait_ge(product_done, 4 * q + 4)
                V.tensor_tensor(m_b[:, :], bank[4][:, :], m_gb[:, :], ALU.mult).then_inc(zb_read, 1)
                dve.wait_ge(za_read, m + 1)
                dve.wait_ge(zb_read, m + 1)
                V.tensor_tensor(m_a[:, :], m_a[:, :], m_b[:, :], ALU.add).then_inc(mix_sum, 1)
                dve.wait_ge(mix_sum, m + 1)
                V.tensor_scalar(at_j(mix_hi, m), m_a[:, :], 1.0, None, ALU.mult).then_inc(mix_hi_ready, 1)
                dve.wait_ge(mix_hi_ready, m + 1)
                V.tensor_tensor(at_j(mix_lo, m), m_a[:, :], at_j(mix_hi, m).bitcast(F32), ALU.subtract)\
                    .then_inc(mix_ready, 1)

            merge(0, True)
            with dve.Fori(1, KD) as m:
                merge(m, False)

            for c in range(N_OUT - LEAD):
                split_at(Q_OUT, c)

            def gained(t, squared, landed, g, dst, done, ss_done, scaled):
                dve.wait_ge(landed, 16)
                for b in range(2):
                    dve.wait_ge(squared, 2 * t + b + 1)
                    if t >= 2:
                        dve.wait_ge(scaled, t - 1)
                    V.tensor_tensor(dst[t % 2][:, HALF * b:HALF * b + HALF], bank[2 * t + b][:, :],
                                    g[:, HALF * b:HALF * b + HALF], ALU.mult).then_inc(done, 1)
                V.tensor_tensor(col(ssq, 4 + 2 * t), col(ssq, 4 + 2 * t), col(ssq, 5 + 2 * t), ALU.add)\
                    .then_inc(ss_done, 1)

            dve.wait_ge(x_again, 16)
            dve.wait_ge(g_pref_landed, 16)
            for t in range(NT):
                if t >= NT - 1:
                    for c in range(N_OUT - LEAD, N_OUT):
                        split_at(Q_OUT, c)
                gained(t, o_squared, g_post_landed, g_post, o_g, o_gained, o_ss, x1_ready)
                dve.wait_ge(o_gained, 2 * t + 2)
                dve.wait_ge(o_rs, t + 1)
                V.scalar_tensor_tensor(out=x1[:, t, :], in0=o_g[t % 2][:, :], scalar=col(rs_c, 4 + 2 * t),
                                       in1=x1[:, t, :], op0=ALU.mult, op1=ALU.add).then_inc(x1_ready, 1)
                dve.wait_ge(x1_ready, t + 1)
                dve.wait_ge(x1_rs, t + 1)
                if t >= 2:
                    dve.wait_ge(h2_turned, 2 * t - 2)
                V.scalar_tensor_tensor(out=h2_tm[t % 2][:, :], in0=x1[:, t, :], scalar=col(rs_c, 12 + t),
                                       in1=g_pref[:, :], op0=ALU.mult, op1=ALU.mult).then_inc(h2_scaled, 1)
                turn_lo(g_hi, g_lo, h2_hi_ready, h2_ready, t)
            V.memset(u_pad[:, :, 0:2], 0.0).then_inc(pad_zero, 1)

            def pair(it, e, first):
                q = Q_UP + it
                n = 2 * it + e
                if not first:
                    dve.wait_ge(tap0, 2 * n)
                V.tensor_copy(fp_now[e][:, :], pv[:, bass.ds(O_FFN + n * 8, 8)]).then_inc(fp_ready, 1)
                for v in range(2):
                    c = 2 * e + v
                    split_at(q, c)
                    dve.wait_ge(pad_ready, 2 * n + v + 1)
                    for t, before, after in ((1, tap2, tap1), (0, tap1, tap0)):
                        dve.wait_ge(before, 2 * n + v + 1)
                        V.scalar_tensor_tensor(out=u_c[v][:, :], in0=u_pad[:, v, t:t + T],
                                               scalar=col(fp_now[e], 4 * v + t), in1=u_c[v][:, :],
                                               op0=ALU.mult, op1=ALU.add).then_inc(after, 1)
                dve.wait_ge(gelu_done, n + 1)
                dve.wait_ge(tap0, 2 * n + 2)
                if not first:
                    dve.wait_ge(yf_ready, n)
                V.tensor_tensor(u_y[:, :], u_c[0][:, :], u_c[1][:, :], ALU.mult).then_inc(y_made, 1)
                dve.wait_ge(y_made, n + 1)
                V.tensor_scalar(at_j(yf_hi, n), u_y[:, :], 1.0, None, ALU.mult).then_inc(yf_hi_ready, 1)
                dve.wait_ge(yf_hi_ready, n + 1)
                V.tensor_tensor(at_j(yf_lo, n), u_y[:, :], at_j(yf_hi, n).bitcast(F32), ALU.subtract)\
                    .then_inc(yf_ready, 1)

            pair(0, 0, True)
            pair(0, 1, False)
            with dve.Fori(1, KF // 2) as it:
                pair(it, 0, False)
                pair(it, 1, False)

            with dve.Fori(0, (N_DOWN - LEAD) // RING) as it:
                for c in range(RING):
                    split_at(Q_DOWN + it, c)

            for t in range(NT):
                gained(t, d_squared, g_postf_landed, g_postf, d_g, d_gained, d_ss, x2_ready)
                dve.wait_ge(d_gained, 2 * t + 2)
                dve.wait_ge(d_rs, t + 1)
                V.scalar_tensor_tensor(out=x1[:, t, :], in0=d_g[t % 2][:, :], scalar=col(rs_c, 4 + 2 * t),
                                       in1=x1[:, t, :], op0=ALU.mult, op1=ALU.add).then_inc(x2_ready, 1)

        @block.tensor
        def _(pe):
            M = nc.tensor.matmul

            def is0(j):
                return isinstance(j, int) and j == 0

            def block3(out, s, b, xh, xl, start, stop):
                M(out, w_hi[s][:, b, :], xh, start=start, stop=False)
                M(out, w_hi[s][:, b, :], xl, start=False, stop=False)
                return M(out, w_lo[s][:, b, :], xh, start=False, stop=stop)

            def product(q, c, out, hi, lo, k0=0, each=None):
                pe.wait_ge(lo_ready, 4 * q + c + 1)
                for k in range(KD):
                    if each is not None:
                        each(k)
                    last = block3(out, c % RING, k, hi[:, k0 + k, :], lo[:, k0 + k, :], k == 0, k == KD - 1)
                last.then_inc(product_done, 1)

            def turn(src, scaled, turned, t):
                pe.wait_ge(scaled, t + 1)
                for b in range(2):
                    for k in range(4):
                        last = nc.tensor.transpose(bank[2 * t + b][:, P * k:P * k + P],
                                                   src[:, P * (4 * b + k):P * (4 * b + k) + P], ident[:, :])
                    last.then_inc(turned, 1)

            pe.wait_ge(consts_made, CONSTS)
            for t in range(NT):
                turn(h_tm[t % 2], h_scaled, h_turned, t)

            def o_stage(j):
                pe.wait_ge(att_ready, j + 1)
                pe.wait_ge(att_far_ready, 3 * j + 3)
                pe.wait_ge(vtm_ready, j + 1)
                pe.wait_ge(q2_ready, j + 1)
                pe.wait_ge(s_ready, 3 * j + 3)
                if not is0(j):
                    pe.wait_ge(yb_scaled, j)
                for t in range(NT):
                    last = M(bank[B_O][:, P * t:P * t + P], v_tm[:, t, :], att[:, t, :], start=True, stop=(t == 0))
                    if t:
                        last = M(bank[B_O][:, P * t:P * t + P], s_all[:, t - 1, :], q_2[:, t - 1, :],
                                 start=False, stop=True)
                last.then_inc(o_done, 1)

            def o_sum(j):
                pe.wait_ge(osq_ready, j + 1)
                pe.wait_ge(i_ready, j + 1)
                M(bank[B_TR][:, :], ones[:, :], o_sq[:, :], start=True, stop=True).then_inc(osum_done, 1)

            def head(i, pj, first):
                j = 2 * i + pj
                q, c = 3 * i, SECT * pj
                if first:
                    pe.wait_ge(h_ready, 2 * NT)
                else:
                    pe.wait_ge(xa_read, j)
                product(q, c, bank[B_FZ][:, :], h_hi, h_lo)
                if not first:
                    o_stage(j - 1)
                    pe.wait_ge(ga_read, j)
                product(q, c + 1, bank[B_Q][:, :], h_hi, h_lo)
                if not first:
                    o_sum(j - 1)
                    pe.wait_ge(sil_ready, j)
                product(q, c + 2, bank[B_V][:, :], h_hi, h_lo)
                pe.wait_ge(fz_read, j + 1)
                product(q, c + 3, bank[B_XA][:, :], h_hi, h_lo)
                pe.wait_ge(v_read, j + 1)
                if not first:
                    pe.wait_ge(rso_ln, j)
                for t in range(NT):
                    last = nc.tensor.transpose(bank[B_TR][:, P * t:P * t + P], v_fm[:, P * t:P * t + P], ident[:, :])
                last.then_inc(tv_done, 1)
                pe.wait_ge(kt_ready, j + 1)
                pe.wait_ge(qt_ready, j + 1)
                if not first:
                    pe.wait_ge(r_ready, j)
                for t in range(NT):
                    last = M(bank[B_ATT][:, P * t:P * t + P], f_b[:, P * t:P * t + P], q_t[:, P * t:P * t + P],
                             start=True, stop=True)
                pe.wait_ge(kd_ready, j + 1)
                if not first:
                    pe.wait_ge(att_far_ready, 3 * j)
                far = bank[B_ATT2][:, :].rearrange("p (l t c) -> p l t c", l=2, t=NT)
                odd = q_t[:, :].rearrange("p (t n e c) -> p t n e c", n=2, e=2, c=CH)
                for t in range(NT):
                    M(far[:, 0, t, :].rearrange("p (n c) -> p n c", c=CH), k_d[:, P * t:P * t + P],
                      odd[:, t, :, 1, :], start=True, stop=True)
                pe.wait_ge(q1_ready, j + 1)
                pe.wait_ge(k1_ready, j + 1)
                for t in range(NT):
                    last = M(far[0:2 * CH, 1, t, :], k_1[:, t, :], q_1[:, t, :], start=True, stop=True)
                last.then_inc(att_done, 1)
                pe.wait_ge(vtm_ready, j + 1)
                pe.wait_ge(k2_ready, j + 1)
                for t in range(NT - 1):
                    last = nc.tensor.transpose(bank[B_TR][:, P * t:P * t + P], k_2[:, t, :], ident[:, :])
                last.then_inc(tkd_done, 1)
                product(q, c + 4, bank[B_GA][:, :], h_hi, h_lo)
                pe.wait_ge(kdtm_ready, j + 1)
                if not first:
                    pe.wait_ge(s_ready, 3 * j)
                for t in range(NT - 1):
                    last = M(bank[B_KV][:, P * t:P * t + P], kd_tm[:, t, :], v_tm[:, t, :], start=True, stop=True)
                last.then_inc(kv_done, 1)
                product(q, c + 5, bank[B_OG][:, :], h_hi, h_lo)
                pe.wait_ge(conv_step, 4 * j + 4)
                pe.wait_ge(att_ready, j + 1)
                pe.wait_ge(lru_landed[pj], 16 * i + 16)
                M(bank[B_ATT][:, :], lru_w[pj][:, 0, :], xc[:, :], start=True, stop=True).then_inc(gate_r, 1)
                pe.wait_ge(kdtm_ready, j + 1)
                M(bank[B_TR][:, :], lru_w[pj][:, 1, :], xc[:, :], start=True, stop=True).then_inc(gate_i, 1)

            head(0, 0, True)
            head(0, 1, False)
            with pe.Fori(1, HEADS // 2) as i:
                head(i, 0, False)
                head(i, 1, False)

            def merge(m, first):
                q = Q_MERGE + m
                if first:
                    pe.wait_ge(xa_read, HEADS)
                else:
                    pe.wait_ge(sig_a, m)
                product(q, 0, bank[0][:, :], h_hi, h_lo)
                if first:
                    o_stage(HEADS - 1)
                    pe.wait_ge(sil_ready, HEADS)
                else:
                    pe.wait_ge(sig_b, m)
                product(q, 1, bank[2][:, :], h_hi, h_lo)
                if first:
                    o_sum(HEADS - 1)
                    pe.wait_ge(ga_read, HEADS)
                    pe.wait_ge(y_ready, 2 * HEADS - 1)
                else:
                    pe.wait_ge(za_read, m)
                product(q, 2, bank[1][:, :], yy_hi, yy_lo)
                if first:
                    pe.wait_ge(y_ready, 2 * HEADS)
                    pe.wait_ge(s_ready, 3 * HEADS)
                else:
                    pe.wait_ge(zb_read, m)
                product(q, 3, bank[4][:, :], yy_hi, yy_lo, k0=KD)

            merge(0, True)
            with pe.Fori(1, KD) as m:
                merge(m, False)

            def token_major(q0, n_k, yh, yl, y_sem, tile_done):
                def step(k, t):
                    s = k % RING
                    toks = slice(P * t, P * t + P)
                    for x, ws in ((yh, (w_hi, w_lo)), (yl, (w_hi,))):
                        for w in ws:
                            for b in range(2):
                                last = M(bank[2 * t + b][:, :], x[:, k, toks], w[s][:, 4 * b:4 * b + 4, :]
                                         .rearrange("p a c -> p (a c)"), start=(k == 0 and w is w_hi and x is yh),
                                         stop=(k == n_k - 1 and x is yl))
                    return last

                def landed(k):
                    pe.wait_ge(lo_ready, RING * q0 + k + 1)
                    pe.wait_ge(y_sem, k + 1)

                for k in range(n_k - RING):
                    landed(k)
                    for t in range(NT):
                        last = step(k, t)
                    last.then_inc(product_done, 1)
                for t in range(NT):
                    for k in range(n_k - RING, n_k):
                        if t == 0:
                            landed(k)
                        last = step(k, t)
                        if t == NT - 1 and k < n_k - 1:
                            last.then_inc(product_done, 1)
                    last.then_inc(tile_done, 1)
                pe.wait_ge(tile_done, NT)
                pe.sem_inc(product_done, 1)

            pe.wait_ge(mix_sum, KD)
            pe.wait_ge(yb_scaled, HEADS)
            token_major(Q_OUT, N_OUT, mix_hi, mix_lo, mix_ready, o_tile)
            for t in range(NT):
                pe.wait_ge(o_gained, 2 * t + 2)
                turn(h2_tm[t % 2], h2_scaled, h2_turned, t)

            def up(it, c, first):
                q = Q_UP + it
                if first:
                    pe.wait_ge(h2_ready, 2 * NT)
                else:
                    pe.wait_ge(tap2, 4 * it + c - 3)
                product(q, c, bank[c][:, :], g_hi, g_lo)

            for c in range(RING):
                up(0, c, True)
            with pe.Fori(1, KF // 2) as it:
                for c in range(RING):
                    up(it, c, False)

            pe.wait_ge(tap2, N_UP)
            token_major(Q_DOWN, N_DOWN, yf_hi, yf_lo, yf_ready, d_tile_done)


_NAMES = ["x", "norm_pre_mix", "w_in", "conv_a_w", "conv_a_b", "lru_wa", "lru_ba", "lru_wx", "lru_bx",
          "lru_lambda", "hg_lb_logits", "hg_norm_g", "w_branch_a", "w_branch_b", "w_out", "norm_post_mix",
          "norm_pre_ffn", "w_up", "conv_f_w", "conv_f_b", "w_down", "norm_post_ffn"]


def _blocks(w):
    n = w.shape[1] // P
    return w.reshape(KD, P, n, P).transpose(2, 1, 0, 3).reshape(n, P, KD * P)


def kernel(**inputs):
    import numpy as np
    import concourse.bacc as bacc
    from concourse.bass_utils import run_bass_kernel_spmd

    a = {n: np.asarray(inputs[n]) for n in _NAMES}
    w_in = _blocks(a["w_in"][0]).reshape(8, KD, P, KD * P)
    heads = w_in[[3, 2, 4, 0, 1, 5]].transpose(1, 0, 2, 3).reshape(N_HEAD, P, KD * P)
    merge = np.stack([w_in[6], w_in[7], _blocks(a["w_branch_a"][0]), _blocks(a["w_branch_b"][0])], 1)
    up = _blocks(a["w_up"][0]).reshape(2, KF, P, KD * P).transpose(1, 0, 2, 3)
    wts = np.concatenate([heads, merge.reshape(N_MERGE, P, KD * P), a["w_out"][0].reshape(N_OUT, P, D),
                          up.reshape(N_UP, P, KD * P), a["w_down"][0].reshape(N_DOWN, P, KD * P)])
    cols = lambda v: v.reshape(-1, P).T
    per_head = [a["conv_a_w"][0][t] for t in range(4)] + [a["conv_a_b"][0], a["lru_ba"][0], a["lru_bx"][0],
                a["lru_lambda"][0], a["hg_lb_logits"][0], a["hg_lb_logits"][1], a["hg_norm_g"][0]]
    per_up = [a["conv_f_w"][0][t] for t in range(3)] + [a["conv_f_b"][0]]
    ffn = np.stack([cols(v).reshape(P, 2, KF) for v in per_up], 3).transpose(0, 2, 1, 3).reshape(P, -1)
    par = np.concatenate([np.stack([cols(v) for v in per_head], 2).reshape(P, -1), ffn], 1)
    gains = np.stack([a[n][0] for n in ("norm_pre_mix", "norm_post_mix", "norm_pre_ffn", "norm_post_ffn")])
    lru = np.stack([a["lru_wa"][0], a["lru_wx"][0]], 2).reshape(HEADS, P, 2 * P)

    nc = bacc.Bacc("TRN2", target_bir_lowering=False, num_devices=1)
    arrays = {"x": a["x"][0], "weights": wts, "params": np.ascontiguousarray(par),
              "lru_w": np.ascontiguousarray(lru), "gains": gains}
    arrays = {f"{n}_dram": np.ascontiguousarray(v) for n, v in arrays.items()}
    args = [nc.dram_tensor(n, v.shape, mybir.dt.from_np(v.dtype), kind="ExternalInput").ap()
            for n, v in arrays.items()]
    out = nc.dram_tensor("out_dram", (T, D), F32, kind="ExternalOutput").ap()
    layer(nc, *args, out)
    r = run_bass_kernel_spmd(nc, [arrays], core_ids=[0])
    return np.asarray(r.results[0]["out_dram"]).reshape(1, T, D)
```

```python
from contextlib import ExitStack

import concourse.bass as bass
from concourse import mybir

F32 = mybir.dt.float32
F32R = mybir.dt.float32r
U32 = mybir.dt.uint32
ALU = mybir.AluOpType
ACT = mybir.ActivationFunctionType

P = 128
D = 1024
T = 512
KD = D // P
HEADS = KD
CH = 32
NCH = T // CH
NT = T // P
CPT = P // CH
FF = 2816
KF = FF // P
EPS = 1e-6
RING = 4
LEAD = 2
EARLY = 3

SECT = 6
N_HEAD = SECT * HEADS
N_MERGE = 4 * KD
N_OUT = KD
N_UP = 2 * KF
N_DOWN = KF
Q_MERGE = N_HEAD // RING
Q_OUT = Q_MERGE + N_MERGE // RING
Q_UP = Q_OUT + N_OUT // RING
Q_DOWN = Q_UP + N_UP // RING
N_TILES = N_HEAD + N_MERGE + N_OUT + N_UP + N_DOWN

HPC = 11
C_BA, C_BX, C_LAM, C_L0, C_L1, C_HG = 5, 6, 7, 8, 9, 10
O_FFN = HEADS * HPC
N_PAR = O_FFN + 4 * 2 * KF
G_PRE, G_POST, G_PREF, G_POSTF = range(4)
HALF = D // 2
HALF_T = T // 2
C_C8, C_NC8, C_LB, C_OMLB = 0, 1, 2, 3

SET_SIG = "sigmoid_and_others"
SET_EXP = "natural_log_exp_and_others"
GELU_C = 0.044715
GELU_S = 0.7978845608028654


def layer(nc, x, wts, par, lru, gains, out):
    ctx = ExitStack()
    with ctx:
        base = (nc.sbuf_base + 63) // 64 * 64
        top = [base]

        def at(name, shape, dt, offset):
            return nc.alloc_sbuf_tensor_at(name, shape, dt, offset=offset)

        def size(shape):
            n = 4
            for s in shape[1:]:
                n *= s
            return (n + 31) // 32 * 32

        def new(name, shape, dt=F32):
            t = at(name, shape, dt, top[0])
            top[0] += size(shape)
            return t

        def sem(name):
            return ctx.enter_context(nc.semaphore(name))

        w_raw = [new(f"w_raw{s}", [P, KD, P]) for s in range(RING)]
        w_hi = [new(f"w_hi{s}", [P, KD, P], F32R) for s in range(RING)]
        w_lo = [new(f"w_lo{s}", [P, KD, P], F32R) for s in range(RING)]
        pv = new("pv", [P, N_PAR])
        hc = new("hc", [P, HEADS, 4])
        hp_now = [new(f"hp_now{s}", [P, HPC]) for s in range(2)]
        hc_now = [new(f"hc_now{s}", [P, 4]) for s in range(2)]
        fp_now = [new(f"fp_now{s}", [P, 8]) for s in range(2)]
        eps_col = new("eps_col", [P, 2])
        ones_r = new("ones_r", [P, P], F32R)
        ident = new("ident", [P, P])
        amask = new("amask", [P, P])
        lru_w = [new(f"lru_w{s}", [P, 2, P]) for s in range(2)]
        lru_hi = new("lru_hi", [P, 2, P], F32R)
        lru_lo = new("lru_lo", [P, 2, P], F32R)
        dq1 = new("dq1", [P, NT, 2])
        dk1 = new("dk1", [P, NT, 2])
        dq2 = new("dq2", [P, NT, CPT])
        dk2 = new("dk2", [P, NT, CPT])
        d_tile = new("d_tile", [P, NT])
        ssq = new("ssq", [P, 16])
        rs_c = new("rs_c", [P, 16])
        sp_t = new("sp_t", [P, 8, HEADS])
        off_h = top[0]
        h_hi = new("h_hi", [P, KD, T], F32R)
        h_lo = new("h_lo", [P, KD, T], F32R)
        g_hi = at("g_hi", [P, KD, T], F32R, off_h)
        g_lo = at("g_lo", [P, KD, T], F32R, off_h + KD * T * 4)
        g_postf = at("g_postf", [P, D], F32, off_h)
        d_g = [at(f"d_g{s}", [P, D], F32, off_h + (1 + s) * D * 4) for s in range(2)]
        junk_d = at("junk_d", [P, D], F32, off_h + 3 * D * 4)
        off_y = top[0]
        yy_hi = new("yy_hi", [P, 2 * KD, T], F32R)
        yy_lo = new("yy_lo", [P, 2 * KD, T], F32R)
        x_in = at("x_in", [P, NT, D], F32, off_y)
        row = D * 4
        g_pre = at("g_pre", [P, D], F32, off_y + 4 * row)
        h_tm = [at(f"h_tm{s}", [P, D], F32, off_y + (5 + s) * row) for s in range(2)]
        junk = at("junk", [P, D], F32, off_y + 7 * row)
        g_post = at("g_post", [P, D], F32, off_y)
        g_pref = at("g_pref", [P, D], F32, off_y + row)
        o_g = [at(f"o_g{s}", [P, D], F32, off_y + (2 + s) * row) for s in range(2)]
        h2_tm = [at(f"h2_tm{s}", [P, D], F32, off_y + (4 + s) * row) for s in range(2)]
        junk_o = at("junk_o", [P, D], F32, off_y + 6 * row)
        yf_hi = at("yf_hi", [P, KF, T], F32R, off_y)
        yf_lo = at("yf_lo", [P, KF, T], F32R, off_y + KF * T * 4)
        off_t = top[0]
        rmask = new("rmask", [P, T])
        f_a = new("f_a", [P, T])
        f_b = new("f_b", [P, T])
        gcum = new("gcum", [P, T])
        e_g = new("e_g", [P, T])
        q_t = new("q_t", [P, T])
        k_d = new("k_d", [P, T])
        q_1 = new("q_1", [P, NT, 2 * CH])
        k_1 = new("k_1", [P, NT, 2 * CH])
        q_2 = new("q_2", [P, NT - 1, P])
        k_2 = new("k_2", [P, NT - 1, P])
        v_fm = new("v_fm", [P, T])
        v_tm = new("v_tm", [P, NT, P])
        kd_tm = new("kd_tm", [P, NT - 1, P])
        att = new("att", [P, NT, P])
        o_sq = v_fm
        rs_o = new("rs_o", [P, T])
        sil = new("sil", [P, T])
        xpad = new("xpad", [P, T + 8])
        xc = new("xc", [P, T])
        l_r = new("l_r", [P, T])
        l_i = new("l_i", [P, T])
        l_th = new("l_th", [P, T])
        l_2 = new("l_2", [P, T])
        l_h = new("l_h", [P, T])
        g_t = new("g_t", [P, T])
        ones = g_t[:, 0:P]
        part_hi = new("part_hi", [P, T], F32R)
        part_lo = new("part_lo", [P, T], F32R)
        s_all = new("s_all", [P, NT - 1, P])
        mix_hi = at("mix_hi", [P, KD, T], F32R, off_t)
        mix_lo = at("mix_lo", [P, KD, T], F32R, off_t + KD * T * 4)
        x1 = at("x1", [P, NT, D], F32, off_t + 2 * KD * T * 4)
        tmp0 = off_t + 3 * KD * T * 4
        m_a, m_b, m_ga, m_gb = [at(f"m_tmp{s}", [P, T], F32, tmp0 + s * T * 4) for s in range(4)]
        fin0 = off_y + 2 * KF * T * 4
        pads = 2 * (T + 8) * 4
        u_pad = at("u_pad", [P, 2, T + 8], F32, fin0)
        fin1 = fin0 + pads
        assert fin1 + T * 4 <= off_t + 2 * KD * T * 4
        u_c0 = at("u_c0", [P, T], F32, fin1)
        u_c1 = m_b
        u_y = m_gb
        u_c = [u_c0, u_c1]
        top[0] = max(top[0], tmp0 + 4 * T * 4)
        assert top[0] <= nc.sbuf_usable_end, (top[0], nc.sbuf_usable_end)

        bank = [ctx.enter_context(nc.psum_tensor(f"bank{b}", [P, T], F32)) for b in range(8)]
        B_FZ, B_Q, B_V, B_XA, B_GA, B_OG = 0, 1, 2, 0, 1, 2
        B_TR, B_KV, B_ATT2, B_ATT, B_O = 3, 4, 5, 6, 7

        w_landed = [sem(f"w_landed{s}") for s in range(RING)]
        hi_ready = sem("hi_ready")
        lo_ready = sem("lo_ready")
        product_done = sem("product_done")
        x_landed = [sem(f"x_landed{s}") for s in range(4)]
        par_landed = sem("par_landed")
        lru_landed = [sem(f"lru_landed{s}") for s in range(2)]
        consts_made = sem("consts_made")
        ones_split = sem("ones_split")
        setup_v = sem("setup_v")
        setup_a = sem("setup_a")
        g_pre_landed = sem("g_pre_landed")
        x_squared = sem("x_squared")
        x_ln = sem("x_ln")
        x_rs = sem("x_rs")
        h_scaled = sem("h_scaled")
        h_turned = sem("h_turned")
        h_hi_ready = sem("h_hi_ready")
        h_ready = sem("h_ready")
        hp_ready = sem("hp_ready")
        fz_read = sem("fz_read")
        fa_ready = sem("fa_ready")
        logf_ready = sem("logf_ready")
        g_ready = sem("g_ready")
        eg_ready = sem("eg_ready")
        eng_ready = sem("eng_ready")
        dec_steps = sem("dec_steps")
        q1_ready = sem("q1_ready")
        k1_ready = sem("k1_ready")
        q2_ready = sem("q2_ready")
        k2_ready = sem("k2_ready")
        qt_ready = sem("qt_ready")
        kt_ready = sem("kt_ready")
        kd_ready = sem("kd_ready")
        v_read = sem("v_read")
        tv_done = sem("tv_done")
        vtm_ready = sem("vtm_ready")
        tkd_done = sem("tkd_done")
        kdtm_ready = sem("kdtm_ready")
        att_done = sem("att_done")
        att_ready = sem("att_ready")
        att_far_ready = sem("att_far_ready")
        kv_done = sem("kv_done")
        s_ready = sem("s_ready")
        o_done = sem("o_done")
        osq_ready = sem("osq_ready")
        osq_hi = sem("osq_hi")
        osq_lo = sem("osq_lo")
        osum_done = sem("osum_done")
        rso_ln = sem("rso_ln")
        rso_ready = sem("rso_ready")
        og_sig = sem("og_sig")
        sil_ready = sem("sil_ready")
        yb_scaled = sem("yb_scaled")
        yb_made = sem("yb_made")
        y_hi_ready = sem("y_hi_ready")
        y_ready = sem("y_ready")
        xa_read = sem("xa_read")
        conv_step = sem("conv_step")
        gate_hi = sem("gate_hi")
        gate_lo = sem("gate_lo")
        gate_r = sem("gate_r")
        gate_i = sem("gate_i")
        r_ready = sem("r_ready")
        i_ready = sem("i_ready")
        th_ready = sem("th_ready")
        th_clamped = sem("th_clamped")
        a_ready = sem("a_ready")
        l1_ready = sem("l1_ready")
        l2_ready = sem("l2_ready")
        ix_ready = sem("ix_ready")
        ld_ready = sem("ld_ready")
        w_sqrt = sem("w_sqrt")
        u_ready = sem("u_ready")
        lru_h = sem("lru_h")
        ga_sq = sem("ga_sq")
        ga_1 = sem("ga_1")
        ga_2 = sem("ga_2")
        ga_th = sem("ga_th")
        ga_read = sem("ga_read")
        ya_made = sem("ya_made")
        sig_a = sem("sig_a")
        sig_b = sem("sig_b")
        za_read = sem("za_read")
        zb_read = sem("zb_read")
        mix_sum = sem("mix_sum")
        mix_hi_ready = sem("mix_hi_ready")
        mix_ready = sem("mix_ready")
        x_again = sem("x_again")
        g_post_landed = sem("g_post_landed")
        g_pref_landed = sem("g_pref_landed")
        o_tile = sem("o_tile")
        o_squared = sem("o_squared")
        o_gained = sem("o_gained")
        o_ss = sem("o_ss")
        o_ln = sem("o_ln")
        o_rs = sem("o_rs")
        x1_ready = sem("x1_ready")
        x1_squared = sem("x1_squared")
        x1_ln = sem("x1_ln")
        x1_rs = sem("x1_rs")
        h2_scaled = sem("h2_scaled")
        h2_turned = sem("h2_turned")
        h2_hi_ready = sem("h2_hi_ready")
        h2_ready = sem("h2_ready")
        pad_zero = sem("pad_zero")
        fp_ready = sem("fp_ready")
        pad_ready = sem("pad_ready")
        tap2 = sem("tap2")
        tap1 = sem("tap1")
        tap0 = sem("tap0")
        gelu_done = sem("gelu_done")
        y_made = sem("y_made")
        yf_hi_ready = sem("yf_hi_ready")
        yf_ready = sem("yf_ready")
        g_postf_landed = sem("g_postf_landed")
        d_tile_done = sem("d_tile_done")
        d_squared = sem("d_squared")
        d_gained = sem("d_gained")
        d_ss = sem("d_ss")
        d_ln = sem("d_ln")
        d_rs = sem("d_rs")
        x2_ready = sem("x2_ready")
        stored = sem("stored")

        block = ctx.enter_context(nc.Block())

        def col(t, c):
            return t[:, c:c + 1]

        @block.sync
        def _(sp):
            def tile(q, c, reuse):
                if reuse:
                    sp.wait_ge(lo_ready, 4 * q + c - RING + 1)
                src = wts[4 * q + c] if isinstance(q, int) else \
                    wts[bass.ds(4 * q + c, 1)].rearrange("o p n -> (o p) n")
                sp.dma_start(w_raw[c][:, :, :].rearrange("p a b -> p (a b)"), src).then_inc(w_landed[c], 16)

            sp.dma_start(pv[:, :], par).then_inc(par_landed, 16)
            for t in range(NT):
                sp.dma_start(x_in[:, t, :], x[P * t:P * t + P, :]).then_inc(x_landed[t], 16)
                if t == 0:
                    sp.dma_start(g_pre[:, :], gains[G_PRE:G_PRE + 1, :].to_broadcast([P, D]))\
                        .then_inc(g_pre_landed, 16)
                if t:
                    tile(0, t - 1, False)
            tile(0, RING - 1, False)
            with sp.Fori(1, Q_MERGE + 3) as q:
                for c in range(RING):
                    tile(q, c, True)
            sp.wait_ge(y_ready, 2 * HEADS)
            sp.dma_start(x1[:, :, :], x.rearrange("(t p) d -> p t d", p=P)).then_inc(x_again, 16)
            with sp.Fori(Q_MERGE + 3, N_TILES // RING) as q:
                for c in range(RING):
                    tile(q, c, True)
            for c in range(N_TILES % RING):
                tile(N_TILES // RING, c, True)
            for t in range(NT):
                for b in range(2):
                    sp.wait_ge(x2_ready, 2 * t + b + 1)
                    cols = slice(HALF * b, HALF * b + HALF)
                    sp.dma_start(out[P * t:P * t + P, cols], x1[:, t, cols]).then_inc(stored, 16)
            sp.wait_ge(stored, 2 * 16 * NT)

        CONSTS = 16
        DSTEPS = 9

        @block.gpsimd
        def _(pool):
            nc.gpsimd.memset(eps_col[:, 0:1], EPS).then_inc(consts_made, 1)
            nc.gpsimd.memset(eps_col[:, 1:2], 1.0).then_inc(consts_made, 1)
            nc.gpsimd.memset(ones, 1.0).then_inc(consts_made, 1)
            nc.gpsimd.memset(ident[:, :], 0.0).then_inc(consts_made, 1)
            nc.gpsimd.memset(amask[:, :], 1.0).then_inc(consts_made, 1)
            nc.gpsimd.memset(rmask[:, :], 1.0).then_inc(consts_made, 1)
            nc.gpsimd.memset(att[:, :, :], 0.0).then_inc(consts_made, 1)
            nc.gpsimd.memset(dq2[:, :, 0:1], 1.0).then_inc(consts_made, 1)
            nc.gpsimd.memset(dk2[:, :, CPT - 1:CPT], 1.0).then_inc(consts_made, 1)
            nc.gpsimd.memset(dq1[:, :, 0:1], 1.0).then_inc(consts_made, 1)
            nc.gpsimd.memset(dk1[:, :, 1:2], 1.0).then_inc(consts_made, 1)
            nc.gpsimd.memset(xpad[:, 0:8], 0.0).then_inc(consts_made, 1)
            pool.wait_ge(consts_made, 12)
            nc.gpsimd.memset(rmask[:, :].rearrange("p (n c) -> p n c", c=CH)[:, :, 0:1], 0.0)\
                .then_inc(consts_made, 1)
            nc.gpsimd.affine_select(out=ident[:, :], in_=ident[:, :], compare_op=ALU.not_equal, fill=1.0,
                                    base=0, pattern=[[-1, P]], channel_multiplier=1).then_inc(consts_made, 1)
            nc.gpsimd.affine_select(out=amask[:, :], in_=amask[:, :], compare_op=ALU.is_ge, fill=0.0,
                                    base=0, pattern=[[1, P]], channel_multiplier=-1).then_inc(consts_made, 1)
            pool.wait_ge(consts_made, 15)
            am = amask[:, :].rearrange("p (b c) -> p b c", c=CH)
            nc.gpsimd.affine_select(out=am, in_=am, compare_op=ALU.is_ge, fill=0.0,
                                    base=0, pattern=[[-CH, CPT], [0, CH]], channel_multiplier=1)\
                .then_inc(consts_made, 1)

            def decays(j, first):
                d = e_g[:, :].rearrange("p (t n c) -> p t n c", n=CPT, c=CH)[:, :, :, CH - 1]
                one = dq2[:, :, 0]

                def times(o, a, b):
                    nc.gpsimd.tensor_tensor(o, a, b, ALU.mult).then_inc(dec_steps, 1)

                pool.wait_ge(eg_ready, j + 1)
                if not first:
                    pool.wait_ge(k2_ready, j)
                    pool.wait_ge(s_ready, 3 * j)
                times(dq1[:, :, 1], d[:, :, 2], one)
                times(dk1[:, :, 0], d[:, :, 1], one)
                times(dq2[:, :, 1], d[:, :, 0], one)
                times(dk2[:, :, 2], d[:, :, 3], one)
                times(dq2[:, :, 2], d[:, :, 0], d[:, :, 1])
                times(dk2[:, :, 1], d[:, :, 2], d[:, :, 3])
                pool.wait_ge(dec_steps, DSTEPS * j + 6)
                times(dq2[:, :, 3], dq2[:, :, 2], d[:, :, 2])
                times(dk2[:, :, 0], dk2[:, :, 1], d[:, :, 1])
                pool.wait_ge(dec_steps, DSTEPS * j + 8)
                times(d_tile[:, :], dq2[:, :, 3], d[:, :, 3])

            def split_lo(n):
                s = n % RING
                pool.wait_ge(hi_ready, n + 1)
                nc.gpsimd.tensor_tensor(w_lo[s][:, :, :], w_raw[s][:, :, :], w_hi[s][:, :, :].bitcast(F32),
                                        ALU.subtract).then_inc(lo_ready, 1)

            pool.wait_ge(consts_made, CONSTS)
            for n in range(EARLY):
                split_lo(n)
            decays(0, True)
            with pool.Fori(1, HEADS) as j:
                decays(j, False)
            pool.wait_ge(lo_ready, RING * Q_UP)
            for n in range(RING * Q_UP, RING * Q_UP + EARLY):
                split_lo(n)

        @block.scalar
        def _(act):
            A = nc.scalar.activation

            def split_hi(q, c):
                act.wait_ge(w_landed[c % RING], 16 * (q + c // RING + 1))
                if not (isinstance(q, int) and 4 * q + c < RING):
                    act.wait_ge(product_done, 4 * q + c - RING + 1)
                A(w_hi[c % RING][:, :, :], w_raw[c % RING][:, :, :], ACT.Copy).then_inc(hi_ready, 1)

            def split_at(q, c):
                if not (isinstance(q, int) and 4 * q + c + LEAD >= N_TILES):
                    split_hi(q, c + LEAD)

            nc.scalar.preload_act_table_set(SET_EXP)
            act.wait_ge(consts_made, CONSTS)
            A(ones_r[:, :], ones, ACT.Copy).then_inc(ones_split, 1)
            act.wait_ge(setup_v, 5)
            A(sp_t[:, 0:3, :], sp_t[:, 0:3, :], ACT.Exp).then_inc(setup_a, 1)

            def turn_hi(dst, turned, hi_done, t):
                for b in range(2):
                    act.wait_ge(turned, 2 * t + b + 1)
                    A(dst[:, 4 * b:4 * b + 4, P * t:P * t + P],
                      bank[2 * t + b][:, :].rearrange("p (a c) -> p a c", c=P), ACT.Copy).then_inc(hi_done, 1)

            def rms(c, ss, ln, rs, n):
                act.wait_ge(ss, n)
                A(col(rs_c, c), col(ssq, c), ACT.Ln, bias=col(eps_col, 0), scale=1.0 / D).then_inc(ln, 1)
                act.wait_ge(ln, (n - 1) % NT + 1)
                A(col(rs_c, c), col(rs_c, c), ACT.Exp, scale=-0.5).then_inc(rs, 1)

            def x_rms(t):
                act.wait_ge(x_landed[t], 16)
                if t:
                    act.wait_ge(x_squared, t)
                A(junk[:, :], x_in[:, t, :], ACT.Square, accum_out=col(ssq, t)).then_inc(x_squared, 1)
                rms(t, x_squared, x_ln, x_rs, t + 1)

            x_rms(0)
            x_rms(1)
            turn_hi(h_hi, h_turned, h_hi_ready, 0)
            split_hi(0, 0)
            turn_hi(h_hi, h_turned, h_hi_ready, 1)
            x_rms(2)
            split_hi(0, 1)
            x_rms(3)
            split_hi(0, 2)
            turn_hi(h_hi, h_turned, h_hi_ready, 2)
            turn_hi(h_hi, h_turned, h_hi_ready, 3)

            def lru_gates(j, pj):
                act.wait_ge(product_done, SECT * j + 6)
                if not is0(j):
                    act.wait_ge(yb_made, j)
                A(sil[:, :], bank[B_OG][:, :], ACT.Sigmoid).then_inc(og_sig, 1)
                act.wait_ge(gate_r, j + 1)
                if not is0(j):
                    act.wait_ge(lru_h, j)
                A(l_r[:, :], bank[B_ATT][:, :], ACT.Sigmoid, bias=col(hp_now[pj], C_BA)).then_inc(r_ready, 1)
                act.wait_ge(gate_i, j + 1)
                A(l_i[:, :], bank[B_TR][:, :], ACT.Sigmoid, bias=col(hp_now[pj], C_BX)).then_inc(i_ready, 1)
                act.wait_ge(r_ready, j + 1)
                if not is0(j):
                    act.wait_ge(u_ready, j)
                A(l_th[:, :], l_r[:, :], ACT.Tanh, scale=col(hc_now[pj], C_C8)).then_inc(th_ready, 1)

            def is0(j):
                return isinstance(j, int) and j == 0

            def front_sig(j):
                act.wait_ge(product_done, SECT * j + 1)
                if not is0(j):
                    act.wait_ge(att_done, j)
                    act.wait_ge(kd_ready, j)
                A(f_a[:, :], bank[B_FZ][:, :], ACT.Sigmoid).then_inc(fa_ready, 1)
                A(f_b[:, :], bank[B_FZ][:, :], ACT.Sigmoid, scale=-1.0).then_inc(fz_read, 1)

            def front_log(j, pj):
                act.wait_ge(fa_ready, j + 1)
                act.wait_ge(hp_ready, 2 * j + 2)
                A(f_a[:, :], f_a[:, :], ACT.Ln, bias=col(hc_now[pj], C_LB), scale=col(hc_now[pj], C_OMLB))\
                    .then_inc(logf_ready, 1)

            def front_exp(j):
                act.wait_ge(g_ready, j + 1)
                if not is0(j):
                    act.wait_ge(dec_steps, DSTEPS * j)
                    act.wait_ge(kd_ready, j)
                A(e_g[:, :], gcum[:, :], ACT.Exp).then_inc(eg_ready, 1)
                act.wait_ge(eg_ready, j + 1)
                A(gcum[:, :], gcum[:, :], ACT.Exp, scale=-1.0).then_inc(eng_ready, 1)

            def lru_logs(j, pj):
                act.wait_ge(th_ready, j + 1)
                A(l_r[:, :], l_r[:, :], ACT.Exp, scale=col(hc_now[pj], C_NC8)).then_inc(a_ready, 1)
                act.wait_ge(th_clamped, j + 1)
                act.wait_ge(ga_th, j + 1)
                A(l_2[:, :], l_th[:, :], ACT.Ln, bias=col(eps_col, 1)).then_inc(l2_ready, 1)
                act.wait_ge(l2_ready, j + 1)
                A(l_th[:, :], l_th[:, :], ACT.Ln, scale=2.0).then_inc(l1_ready, 1)

            def lru_root(j):
                act.wait_ge(ld_ready, j + 1)
                A(l_th[:, :], l_th[:, :], ACT.Exp, scale=0.5).then_inc(w_sqrt, 1)

            def o_square(j):
                act.wait_ge(o_done, j + 1)
                if not is0(j):
                    act.wait_ge(osum_done, j)
                A(o_sq[:, :], bank[B_O][:, :], ACT.Square).then_inc(osq_ready, 1)
                act.wait_ge(osq_ready, j + 1)
                act.wait_ge(gate_i, j + 1)
                A(part_hi[:, :], o_sq[:, :], ACT.Copy).then_inc(osq_hi, 1)

            def o_rms(j):
                act.wait_ge(osum_done, j + 1)
                if not is0(j):
                    act.wait_ge(yb_scaled, j)
                A(rs_o[:, :], bank[B_TR][:, :], ACT.Ln, bias=col(eps_col, 0), scale=1.0 / P).then_inc(rso_ln, 1)
                act.wait_ge(rso_ln, j + 1)
                A(rs_o[:, :], rs_o[:, :], ACT.Exp, scale=-0.5).then_inc(rso_ready, 1)

            def finish_a(j, pj):
                lru_logs(j, pj)
                o_square(j)
                lru_root(j)

            def head(i, pj, first):
                j = 2 * i + pj
                q, c = 3 * i, SECT * pj
                pp = 1 - pj
                if not first:
                    split_at(q, c)
                    nc.scalar.preload_act_table_set(SET_SIG)
                    lru_gates(j - 1, pp)
                split_at(q, c + 1)
                if first:
                    nc.scalar.preload_act_table_set(SET_SIG)
                front_sig(j)
                nc.scalar.preload_act_table_set(SET_EXP)
                front_log(j, pj)
                if not first:
                    lru_logs(j - 1, pp)
                front_exp(j)
                if not first:
                    o_square(j - 1)
                    lru_root(j - 1)
                if not is0(i):
                    act.wait_ge(gate_i, j - 1)
                act.dma_start(lru_w[pj][:, :, :].rearrange("p a b -> p (a b)"),
                              lru[bass.ds(j, 1), :, :].rearrange("o p n -> (o p) n")).then_inc(lru_landed[pj], 16)
                split_at(q, c + 2)
                split_at(q, c + 3)
                if not first:
                    o_rms(j - 1)
                act.wait_ge(product_done, SECT * j + 3)
                if not first:
                    act.wait_ge(osum_done, j)
                A(v_fm[:, :], bank[B_V][:, :], ACT.Copy).then_inc(v_read, 1)
                act.wait_ge(tv_done, j + 1)
                if not first:
                    act.wait_ge(o_done, j)
                A(v_tm[:, :, :].rearrange("p a b -> p (a b)"), bank[B_TR][:, :], ACT.Copy).then_inc(vtm_ready, 1)
                split_at(q, c + 4)
                act.wait_ge(product_done, SECT * j + 4)
                if not first:
                    act.wait_ge(conv_step, 4 * j)
                A(xpad[:, 3:3 + T], bank[B_XA][:, :], ACT.Copy).then_inc(xa_read, 1)
                split_at(q, c + 5)
                act.wait_ge(product_done, SECT * j + 5)
                if not first:
                    act.wait_ge(ld_ready, j)
                A(l_2[:, :], bank[B_GA][:, :], ACT.Square).then_inc(ga_sq, 1)
                act.wait_ge(lru_landed[pj], 16 * i + 16)
                if not first:
                    act.wait_ge(osum_done, j)
                A(lru_hi[:, :, :], lru_w[pj][:, :, :], ACT.Copy).then_inc(gate_hi, 1)
                act.wait_ge(conv_step, 4 * j + 4)
                A(part_hi[:, :], xc[:, :], ACT.Copy).then_inc(gate_hi, 1)
                nc.scalar.preload_act_table_set(SET_SIG)
                act.wait_ge(ga_2, j + 1)
                A(g_t[:, :], l_2[:, :], ACT.Tanh, scale=GELU_S).then_inc(ga_th, 1)

            head(0, 0, True)
            head(0, 1, False)
            with act.Fori(1, HEADS // 2) as i:
                head(i, 0, False)
                head(i, 1, False)

            def gates(m, done_a, done_b, bank_a, bank_b):
                act.wait_ge(product_done, done_a)
                A(m_ga[:, :], bank[bank_a][:, :], ACT.Sigmoid).then_inc(sig_a, 1)
                act.wait_ge(product_done, done_b)
                A(m_gb[:, :], bank[bank_b][:, :], ACT.Sigmoid).then_inc(sig_b, 1)

            q = Q_MERGE
            split_at(q, 0)
            lru_gates(HEADS - 1, 1)
            nc.scalar.preload_act_table_set(SET_EXP)
            lru_logs(HEADS - 1, 1)
            o_square(HEADS - 1)
            lru_root(HEADS - 1)
            split_at(q, 1)
            split_at(q, 2)
            o_rms(HEADS - 1)
            split_at(q, 3)
            nc.scalar.preload_act_table_set(SET_SIG)
            act.wait_ge(y_ready, 2 * HEADS)
            gates(0, 4 * q + 1, 4 * q + 2, 0, 2)
            split_at(q + 1, 0)
            split_at(q + 1, 1)
            act.wait_ge(mix_sum, 1)
            gates(1, 4 * q + 3, 4 * q + 4, B_ATT2, B_ATT)
            split_at(q + 1, 2)
            split_at(q + 1, 3)
            with act.Fori(2, KD) as m:
                q = Q_MERGE + m
                split_at(q, 0)
                split_at(q, 1)
                act.wait_ge(mix_sum, m)
                gates(m, 4 * q + 1, 4 * q + 2, 0, 2)
                split_at(q, 2)
                split_at(q, 3)

            act.wait_ge(product_done, RING * Q_OUT)
            act.dma_start(g_post[:, :], gains[G_POST:G_POST + 1, :].to_broadcast([P, D])).then_inc(g_post_landed, 16)
            act.dma_start(g_pref[:, :], gains[G_PREF:G_PREF + 1, :].to_broadcast([P, D])).then_inc(g_pref_landed, 16)
            nc.scalar.preload_act_table_set(SET_EXP)
            for c in range(N_OUT - LEAD):
                split_at(Q_OUT, c)

            def square(t, b, tile_done, squared, junk_buf, c0):
                act.wait_ge(tile_done, 2 * t + b + 1)
                if t or b:
                    act.wait_ge(squared, 2 * t + b)
                A(junk_buf[:, 0:HALF], bank[2 * t + b][:, :], ACT.Square, accum_out=col(ssq, c0 + 2 * t + b))\
                    .then_inc(squared, 1)

            def rms_half(c, squared, half, t):
                act.wait_ge(squared, 2 * t + 1)
                A(col(ssq, c), col(ssq, c), ACT.Identity, bias=col(eps_col, 0), scale=1.0 / D).then_inc(half, 1)

            def rms_whole(c, squared, half, ln, rs, t):
                act.wait_ge(squared, 2 * t + 2)
                act.wait_ge(half, t + 1)
                A(col(rs_c, c), col(ssq, c + 1), ACT.Ln, bias=col(ssq, c), scale=1.0 / D).then_inc(ln, 1)
                act.wait_ge(ln, t + 1)
                A(col(rs_c, c), col(rs_c, c), ACT.Exp, scale=-0.5).then_inc(rs, 1)

            for t in range(NT):
                if t == NT - 1:
                    split_hi(Q_UP, 1)
                square(t, 0, o_tile, o_squared, junk_o, 4)
                rms_half(4 + 2 * t, o_squared, o_ss, t)
                square(t, 1, o_tile, o_squared, junk_o, 4)
                rms_whole(4 + 2 * t, o_squared, o_ss, o_ln, o_rs, t)
                if t == NT - 2:
                    split_hi(Q_UP, 0)
                elif t == NT - 1:
                    split_hi(Q_UP, 2)
                if t:
                    turn_hi(g_hi, h2_turned, h2_hi_ready, t - 1)
                act.wait_ge(x1_ready, t + 1)
                if t:
                    act.wait_ge(x1_squared, t)
                A(junk_o[:, :], x1[:, t, :], ACT.Square, accum_out=col(ssq, 12 + t)).then_inc(x1_squared, 1)
                rms(12 + t, x1_squared, x1_ln, x1_rs, t + 1)
            turn_hi(g_hi, h2_turned, h2_hi_ready, NT - 1)
            nc.scalar.preload_act_table(ACT.Gelu_apprx_tanh)

            def pair(it, e, first):
                q = Q_UP + it
                n = 2 * it + e
                for v in range(2):
                    c = 2 * e + v
                    if not (first and c + LEAD < EARLY):
                        split_at(q, c)
                    act.wait_ge(product_done, 4 * q + c + 1)
                    act.wait_ge(fp_ready, n + 1)
                    if first:
                        act.wait_ge(pad_zero, 1)
                    else:
                        act.wait_ge(tap0, 2 * n)
                        act.wait_ge(y_made, n)
                    A(u_pad[:, v, 2:2 + T], bank[c][:, :], ACT.Copy).then_inc(pad_ready, 1)
                    A(u_c[v][:, :], bank[c][:, :], ACT.Identity, bias=col(fp_now[e], 4 * v + 3),
                      scale=col(fp_now[e], 4 * v + 2)).then_inc(tap2, 1)
                act.wait_ge(tap0, 2 * n + 1)
                A(u_c[0][:, :], u_c[0][:, :], ACT.Gelu_apprx_tanh).then_inc(gelu_done, 1)

            pair(0, 0, True)
            pair(0, 1, False)
            with act.Fori(1, KF // 2) as it:
                pair(it, 0, False)
                pair(it, 1, False)

            act.wait_ge(product_done, RING * Q_DOWN)
            act.dma_start(g_postf[:, :], gains[G_POSTF:G_POSTF + 1, :].to_broadcast([P, D]))\
                .then_inc(g_postf_landed, 16)
            nc.scalar.preload_act_table_set(SET_EXP)
            with act.Fori(0, (N_DOWN - LEAD) // RING) as it:
                for c in range(RING):
                    split_at(Q_DOWN + it, c)
            for t in range(NT):
                square(t, 0, d_tile_done, d_squared, junk_d, 4)
                rms_half(4 + 2 * t, d_squared, d_ss, t)
                square(t, 1, d_tile_done, d_squared, junk_d, 4)
                rms_whole(4 + 2 * t, d_squared, d_ss, d_ln, d_rs, t)

        @block.vector
        def _(dve):
            V = nc.vector

            def is0(j):
                return isinstance(j, int) and j == 0

            def split_lo(q, c):
                s = c % RING
                dve.wait_ge(hi_ready, 4 * q + c + 1)
                V.tensor_tensor(w_lo[s][:, :, :], w_raw[s][:, :, :], w_hi[s][:, :, :].bitcast(F32),
                                ALU.subtract).then_inc(lo_ready, 1)

            def split_at(q, c):
                if not (isinstance(q, int) and 4 * q + c + LEAD >= N_TILES):
                    split_lo(q, c + LEAD)

            def at_j(t, j):
                return t[:, bass.ds(j, 1), :].rearrange("p a b -> p (a b)")

            steps = [0]

            def link(ins):
                steps[0] += 1
                ins.then_inc(setup_v, 1)
                dve.wait_ge(setup_v, steps[0])

            hpv = pv[:, 0:O_FFN].rearrange("p (h c) -> p c h", c=HPC)
            lam, l0, l1 = hpv[:, C_LAM, :], hpv[:, C_L0, :], hpv[:, C_L1, :]
            s = [sp_t[:, a, :] for a in range(8)]
            dve.wait_ge(par_landed, 16)
            link(V.tensor_tensor(s[3], l0, l1, ALU.max))
            link(V.tensor_tensor(s[0], l0, s[3], ALU.subtract))
            link(V.tensor_tensor(s[1], l1, s[3], ALU.subtract))
            link(V.tensor_scalar(s[4], lam, -1.0, None, ALU.mult))
            link(V.tensor_tensor(s[2], lam, s[4], ALU.min))
            dve.wait_ge(setup_a, 1)
            link(V.tensor_tensor(s[3], s[0], s[1], ALU.add))
            link(V.reciprocal(s[3], s[3]))
            link(V.tensor_tensor(hc[:, :, C_LB], s[0], s[3], ALU.mult))
            link(V.tensor_scalar(hc[:, :, C_OMLB], hc[:, :, C_LB], -1.0, 1.0, ALU.mult, ALU.add))

            def softplus():
                link(V.tensor_scalar(s[5], s[2], 2.0, None, ALU.add))
                link(V.reciprocal(s[5], s[5]))
                link(V.tensor_tensor(s[5], s[2], s[5], ALU.mult))
                link(V.tensor_tensor(s[6], s[5], s[5], ALU.mult))
                link(V.tensor_scalar(s[7], s[6], 1.0 / 15, None, ALU.mult))
                for odd in (13, 11, 9, 7, 5, 3):
                    link(V.scalar_tensor_tensor(out=s[7], in0=s[7], scalar=1.0 / odd, in1=s[6],
                                                op0=ALU.add, op1=ALU.mult))
                link(V.scalar_tensor_tensor(out=s[7], in0=s[7], scalar=1.0, in1=s[5], op0=ALU.add, op1=ALU.mult))
                link(V.tensor_scalar(s[4], s[4], 0.0, 8.0, ALU.max, ALU.mult))
                link(V.scalar_tensor_tensor(out=hc[:, :, C_C8], in0=s[7], scalar=16.0, in1=s[4],
                                            op0=ALU.mult, op1=ALU.add))
                link(V.tensor_scalar(hc[:, :, C_NC8], hc[:, :, C_C8], -1.0, None, ALU.mult))

            def turn_lo(dst_hi, dst_lo, hi_done, done, t):
                for b in range(2):
                    dve.wait_ge(hi_done, 2 * t + b + 1)
                    V.tensor_tensor(dst_lo[:, 4 * b:4 * b + 4, P * t:P * t + P],
                                    bank[2 * t + b][:, :].rearrange("p (a c) -> p a c", c=P),
                                    dst_hi[:, 4 * b:4 * b + 4, P * t:P * t + P].bitcast(F32), ALU.subtract)\
                        .then_inc(done, 1)

            def h_scale(t):
                dve.wait_ge(x_rs, t + 1)
                if t >= 2:
                    dve.wait_ge(h_turned, 2 * t - 2)
                V.scalar_tensor_tensor(out=h_tm[t % 2][:, :], in0=x_in[:, t, :], scalar=col(rs_c, t),
                                       in1=g_pre[:, :], op0=ALU.mult, op1=ALU.mult).then_inc(h_scaled, 1)

            dve.wait_ge(g_pre_landed, 16)
            h_scale(0)
            h_scale(1)
            turn_lo(h_hi, h_lo, h_hi_ready, h_ready, 0)
            turn_lo(h_hi, h_lo, h_hi_ready, h_ready, 1)
            h_scale(2)
            softplus()
            h_scale(3)
            turn_lo(h_hi, h_lo, h_hi_ready, h_ready, 2)
            turn_lo(h_hi, h_lo, h_hi_ready, h_ready, 3)

            def params(j, pj, first):
                if not first:
                    dve.wait_ge(y_ready, 2 * j - 2)
                V.tensor_copy(hp_now[pj][:, :], pv[:, bass.ds(j * HPC, HPC)]).then_inc(hp_ready, 1)
                V.tensor_copy(hc_now[pj][:, :], at_j(hc, j)).then_inc(hp_ready, 1)

            def lru_1(j):
                dve.wait_ge(og_sig, j + 1)
                V.tensor_tensor(sil[:, :], bank[B_OG][:, :], sil[:, :], ALU.mult).then_inc(sil_ready, 1)
                dve.wait_ge(th_ready, j + 1)
                V.tensor_scalar(l_th[:, :], l_th[:, :], 2.0 ** -63, None, ALU.max).then_inc(th_clamped, 1)
                dve.wait_ge(i_ready, j + 1)
                V.tensor_tensor(l_i[:, :], l_i[:, :], xc[:, :], ALU.mult).then_inc(ix_ready, 1)

            def scan_g(j):
                dve.wait_ge(logf_ready, j + 1)
                if not is0(j):
                    dve.wait_ge(kt_ready, j)
                V.tensor_tensor_scan(out=gcum[:, :], data0=rmask[:, :], data1=f_a[:, :], initial=0.0,
                                     op0=ALU.mult, op1=ALU.add).then_inc(g_ready, 1)

            def osq_split(j):
                dve.wait_ge(osq_hi, j + 1)
                V.tensor_tensor(part_lo[:, :], o_sq[:, :], part_hi[:, :].bitcast(F32), ALU.subtract)\
                    .then_inc(osq_lo, 1)

            def gate_split(j, pj):
                dve.wait_ge(gate_hi, 2 * j + 1)
                V.tensor_tensor(lru_lo[:, :, :], lru_w[pj][:, :, :], lru_hi[:, :, :].bitcast(F32), ALU.subtract)\
                    .then_inc(gate_lo, 1)
                dve.wait_ge(gate_hi, 2 * j + 2)
                V.tensor_tensor(part_lo[:, :], xc[:, :], part_hi[:, :].bitcast(F32), ALU.subtract)\
                    .then_inc(gate_lo, 1)

            def lru_2(j):
                dve.wait_ge(l1_ready, j + 1)
                V.tensor_tensor(l_th[:, :], l_th[:, :], l_2[:, :], ALU.subtract).then_inc(ld_ready, 1)

            def lru_3(j):
                dve.wait_ge(w_sqrt, j + 1)
                dve.wait_ge(ix_ready, j + 1)
                V.tensor_tensor(l_i[:, :], l_i[:, :], l_th[:, :], ALU.mult).then_inc(u_ready, 1)
                dve.wait_ge(u_ready, j + 1)
                dve.wait_ge(a_ready, j + 1)
                if not is0(j):
                    dve.wait_ge(y_ready, 2 * j)
                V.tensor_tensor_scan(out=l_h[:, :], data0=l_r[:, :], data1=l_i[:, :], initial=0.0,
                                     op0=ALU.mult, op1=ALU.add).then_inc(lru_h, 1)
                dve.wait_ge(lru_h, j + 1)
                dve.wait_ge(ga_read, j + 1)
                V.scalar_tensor_tensor(out=l_h[:, :], in0=g_t[:, :], scalar=0.5, in1=l_h[:, :],
                                       op0=ALU.mult, op1=ALU.mult).then_inc(ya_made, 1)
                dve.wait_ge(ya_made, j + 1)
                V.tensor_scalar(at_j(yy_hi, j), l_h[:, :], 1.0, None, ALU.mult).then_inc(y_hi_ready, 1)

            def front(j, pj):
                dve.wait_ge(product_done, SECT * j + 2)
                dve.wait_ge(eg_ready, j + 1)
                if not is0(j):
                    dve.wait_ge(o_done, j)
                V.tensor_tensor(q_t[:, :], bank[B_Q][:, :], e_g[:, :], ALU.mult).then_inc(qt_ready, 1)
                dve.wait_ge(hp_ready, 2 * j + 2)
                dve.wait_ge(fz_read, j + 1)
                dve.wait_ge(eng_ready, j + 1)
                V.scalar_tensor_tensor(out=f_b[:, :], in0=f_b[:, :], scalar=col(hc_now[pj], C_OMLB),
                                       in1=gcum[:, :], op0=ALU.mult, op1=ALU.mult).then_inc(kt_ready, 1)
                dve.wait_ge(kt_ready, j + 1)
                if not is0(j):
                    dve.wait_ge(k2_ready, j)
                    dve.wait_ge(att_done, j)
                chunks = lambda a: a.rearrange("p (n c) -> p n c", c=CH)
                over = lambda a, n: a.unsqueeze(2).to_broadcast([P, n, CH])
                V.tensor_tensor(chunks(k_d[:, :]), chunks(f_b[:, :]), over(chunks(e_g[:, :])[:, :, CH - 1], NCH),
                                ALU.mult).then_inc(kd_ready, 1)
                dve.wait_ge(dec_steps, DSTEPS * j + DSTEPS)
                dve.wait_ge(qt_ready, j + 1)
                dve.wait_ge(kd_ready, j + 1)
                half = lambda a, h: a.rearrange("p (t h n c) -> p t h n c", h=2, n=2, c=CH)[:, :, h, :, :]
                wide = lambda a: a.unsqueeze(3).to_broadcast([P, NT, 2, CH])
                two = lambda a: a.rearrange("p t (n c) -> p t n c", c=CH)
                V.tensor_tensor(two(q_1[:, :, :]), half(q_t[:, :], 1), wide(dq1[:, :, :]), ALU.mult)\
                    .then_inc(q1_ready, 1)
                V.tensor_tensor(two(k_1[:, :, :]), half(k_d[:, :], 0), wide(dk1[:, :, :]), ALU.mult)\
                    .then_inc(k1_ready, 1)
                n3 = NCH - CPT
                flat = lambda a: a.rearrange("p a b -> p (a b)")
                V.tensor_tensor(chunks(flat(q_2[:, :, :])), chunks(q_t[:, P:T]), over(flat(dq2[:, 1:NT, :]), n3),
                                ALU.mult).then_inc(q2_ready, 1)
                if not is0(j):
                    dve.wait_ge(tkd_done, j)
                V.tensor_tensor(chunks(flat(k_2[:, :, :])), chunks(k_d[:, 0:T - P]),
                                over(flat(dk2[:, 0:NT - 1, :]), n3), ALU.mult).then_inc(k2_ready, 1)

            def out_b(j, pj):
                dve.wait_ge(rso_ready, j + 1)
                V.scalar_tensor_tensor(out=rs_o[:, :], in0=bank[B_O][:, :], scalar=col(hp_now[pj], C_HG),
                                       in1=rs_o[:, :], op0=ALU.mult, op1=ALU.mult).then_inc(yb_scaled, 1)
                dve.wait_ge(yb_scaled, j + 1)
                dve.wait_ge(sil_ready, j + 1)
                V.tensor_tensor(sil[:, :], rs_o[:, :], sil[:, :], ALU.mult).then_inc(yb_made, 1)
                dve.wait_ge(yb_made, j + 1)
                V.tensor_scalar(at_j(yy_hi, j + KD), sil[:, :], 1.0, None, ALU.mult).then_inc(y_hi_ready, 1)

            def split_y(j):
                dve.wait_ge(y_hi_ready, 2 * j + 1)
                V.tensor_tensor(at_j(yy_lo, j), l_h[:, :], at_j(yy_hi, j).bitcast(F32), ALU.subtract)\
                    .then_inc(y_ready, 1)
                dve.wait_ge(y_hi_ready, 2 * j + 2)
                V.tensor_tensor(at_j(yy_lo, j + KD), sil[:, :], at_j(yy_hi, j + KD).bitcast(F32), ALU.subtract)\
                    .then_inc(y_ready, 1)

            def chain(j):
                dve.wait_ge(kv_done, j + 1)
                kv = [bank[B_KV][:, P * t:P * t + P] for t in range(NT - 1)]
                if not is0(j):
                    dve.wait_ge(o_done, j)
                V.tensor_copy(s_all[:, 0, :], kv[0]).then_inc(s_ready, 1)
                for t in range(1, NT - 1):
                    dve.wait_ge(s_ready, 3 * j + t)
                    V.scalar_tensor_tensor(out=s_all[:, t, :], in0=s_all[:, t - 1, :], scalar=col(d_tile, t),
                                           in1=kv[t], op0=ALU.mult, op1=ALU.add).then_inc(s_ready, 1)

            def head(i, pj, first):
                j = 2 * i + pj
                q, c = 3 * i, SECT * pj
                pp = 1 - pj
                if not first:
                    split_at(q, c)
                params(j, pj, is0(i))
                if not first:
                    lru_1(j - 1)
                split_at(q, c + 1)
                scan_g(j)
                if not first:
                    lru_2(j - 1)
                split_at(q, c + 2)
                if not first:
                    osq_split(j - 1)
                front(j, pj)
                if not first:
                    lru_3(j - 1)
                split_at(q, c + 3)
                if not first:
                    out_b(j - 1, pp)
                    split_y(j - 1)
                dve.wait_ge(tkd_done, j + 1)
                if not first:
                    dve.wait_ge(kv_done, j)
                V.tensor_copy(kd_tm[:, :, :].rearrange("p a b -> p (a b)"), bank[B_TR][:, 0:T - P])\
                    .then_inc(kdtm_ready, 1)
                split_at(q, c + 4)
                dve.wait_ge(consts_made, CONSTS)
                dve.wait_ge(att_done, j + 1)
                if not first:
                    dve.wait_ge(o_done, j)
                V.copy_predicated(out=att[:, :, :], mask=amask[:, :].bitcast(U32).unsqueeze(1)
                                  .to_broadcast([P, NT, P]),
                                  data=bank[B_ATT][:, :].rearrange("p (a b) -> p a b", b=P)).then_inc(att_ready, 1)
                far = bank[B_ATT2][:, :].rearrange("p (l t c) -> p l t c", l=2, t=NT)
                dve.wait_ge(att_ready, j + 1)
                for b in (0, 2):
                    V.tensor_copy(att[CH * b:CH * b + CH, :, CH * (b + 1):CH * (b + 2)],
                                  far[CH * b:CH * b + CH, 0, :, CH * (b // 2):CH * (b // 2) + CH])\
                        .then_inc(att_far_ready, 1)
                V.tensor_copy(att[0:2 * CH, :, 2 * CH:P], far[0:2 * CH, 1, :, :]).then_inc(att_far_ready, 1)
                dve.wait_ge(xa_read, j + 1)
                if not first:
                    dve.wait_ge(gate_i, j)
                    dve.wait_ge(ix_ready, j)
                V.tensor_scalar(xc[:, :], xpad[:, 3:3 + T], col(hp_now[pj], 3), col(hp_now[pj], 4),
                                ALU.mult, ALU.add).then_inc(conv_step, 1)
                for t in (2, 1, 0):
                    dve.wait_ge(conv_step, 4 * j + 3 - t)
                    V.scalar_tensor_tensor(out=xc[:, :], in0=xpad[:, t:t + T], scalar=col(hp_now[pj], t),
                                           in1=xc[:, :], op0=ALU.mult, op1=ALU.add).then_inc(conv_step, 1)
                split_at(q, c + 5)
                dve.wait_ge(ga_sq, j + 1)
                V.tensor_scalar(l_2[:, :], l_2[:, :], GELU_C, 1.0, ALU.mult, ALU.add).then_inc(ga_1, 1)
                dve.wait_ge(ga_1, j + 1)
                V.tensor_tensor(l_2[:, :], bank[B_GA][:, :], l_2[:, :], ALU.mult).then_inc(ga_2, 1)
                gate_split(j, pj)
                chain(j)
                dve.wait_ge(ga_th, j + 1)
                V.scalar_tensor_tensor(out=g_t[:, :], in0=g_t[:, :], scalar=1.0, in1=bank[B_GA][:, :],
                                       op0=ALU.add, op1=ALU.mult).then_inc(ga_read, 1)

            dve.wait_ge(lo_ready, EARLY)
            head(0, 0, True)
            head(0, 1, False)
            with dve.Fori(1, HEADS // 2) as i:
                head(i, 0, False)
                head(i, 1, False)

            def mix(m, done_a, done_b, first, between):
                dve.wait_ge(sig_a, m + 1)
                dve.wait_ge(product_done, done_a)
                if not first:
                    dve.wait_ge(mix_ready, m)
                V.tensor_tensor(m_a[:, :], bank[1][:, :], m_ga[:, :], ALU.mult).then_inc(za_read, 1)
                between()
                dve.wait_ge(sig_b, m + 1)
                dve.wait_ge(product_done, done_b)
                V.tensor_tensor(m_b[:, :], bank[4][:, :], m_gb[:, :], ALU.mult).then_inc(zb_read, 1)
                dve.wait_ge(za_read, m + 1)
                dve.wait_ge(zb_read, m + 1)
                V.tensor_tensor(m_a[:, :], m_a[:, :], m_b[:, :], ALU.add).then_inc(mix_sum, 1)
                dve.wait_ge(mix_sum, m + 1)
                V.tensor_scalar(at_j(mix_hi, m), m_a[:, :], 1.0, None, ALU.mult).then_inc(mix_hi_ready, 1)
                dve.wait_ge(mix_hi_ready, m + 1)
                V.tensor_tensor(at_j(mix_lo, m), m_a[:, :], at_j(mix_hi, m).bitcast(F32), ALU.subtract)\
                    .then_inc(mix_ready, 1)

            q = Q_MERGE
            split_at(q, 0)
            lru_1(HEADS - 1)
            lru_2(HEADS - 1)
            split_at(q, 1)
            osq_split(HEADS - 1)
            lru_3(HEADS - 1)
            split_at(q, 2)
            out_b(HEADS - 1, 1)
            split_y(HEADS - 1)
            split_at(q, 3)
            split_at(q + 1, 0)
            mix(0, 4 * q + 5, 4 * q + 6, True, lambda: split_at(q + 1, 1))
            mix(1, 4 * q + 7, 4 * q + 8, False, lambda: split_at(q + 1, 2))
            split_at(q + 1, 3)
            with dve.Fori(2, KD) as m:
                q = Q_MERGE + m
                for c in range(RING - 1):
                    split_at(q, c)
                mix(m, 4 * q + 3, 4 * q + 4, False, lambda: split_at(q, RING - 1))

            for c in range(N_OUT - LEAD):
                split_at(Q_OUT, c)

            def gained(t, squared, landed, g, dst, done, scaled, scales=1):
                dve.wait_ge(landed, 16)
                for b in range(2):
                    dve.wait_ge(squared, 2 * t + b + 1)
                    if t >= 2:
                        dve.wait_ge(scaled, scales * (t - 1))
                    V.tensor_tensor(dst[t % 2][:, HALF * b:HALF * b + HALF], bank[2 * t + b][:, :],
                                    g[:, HALF * b:HALF * b + HALF], ALU.mult).then_inc(done, 1)

            def h2_scale(t):
                dve.wait_ge(x1_ready, t + 1)
                dve.wait_ge(x1_rs, t + 1)
                if t >= 2:
                    dve.wait_ge(h2_turned, 2 * t - 2)
                V.scalar_tensor_tensor(out=h2_tm[t % 2][:, :], in0=x1[:, t, :], scalar=col(rs_c, 12 + t),
                                       in1=g_pref[:, :], op0=ALU.mult, op1=ALU.mult).then_inc(h2_scaled, 1)

            dve.wait_ge(x_again, 16)
            dve.wait_ge(g_pref_landed, 16)
            for t in range(NT):
                gained(t, o_squared, g_post_landed, g_post, o_g, o_gained, x1_ready)
                dve.wait_ge(o_gained, 2 * t + 2)
                dve.wait_ge(o_rs, t + 1)
                V.scalar_tensor_tensor(out=x1[:, t, :], in0=o_g[t % 2][:, :], scalar=col(rs_c, 4 + 2 * t),
                                       in1=x1[:, t, :], op0=ALU.mult, op1=ALU.add).then_inc(x1_ready, 1)
                if t:
                    turn_lo(g_hi, g_lo, h2_hi_ready, h2_ready, t - 1)
                h2_scale(t)
            turn_lo(g_hi, g_lo, h2_hi_ready, h2_ready, NT - 1)
            dve.wait_ge(lo_ready, RING * Q_UP + EARLY)
            V.memset(u_pad[:, :, 0:2], 0.0).then_inc(pad_zero, 1)

            def pair(it, e, first):
                q = Q_UP + it
                n = 2 * it + e
                if not first:
                    dve.wait_ge(tap0, 2 * n)
                V.tensor_copy(fp_now[e][:, :], pv[:, bass.ds(O_FFN + n * 8, 8)]).then_inc(fp_ready, 1)
                for v in range(2):
                    c = 2 * e + v
                    if not (first and c + LEAD < EARLY):
                        split_at(q, c)
                    dve.wait_ge(pad_ready, 2 * n + v + 1)
                    for t, before, after in ((1, tap2, tap1), (0, tap1, tap0)):
                        dve.wait_ge(before, 2 * n + v + 1)
                        V.scalar_tensor_tensor(out=u_c[v][:, :], in0=u_pad[:, v, t:t + T],
                                               scalar=col(fp_now[e], 4 * v + t), in1=u_c[v][:, :],
                                               op0=ALU.mult, op1=ALU.add).then_inc(after, 1)
                dve.wait_ge(gelu_done, n + 1)
                dve.wait_ge(tap0, 2 * n + 2)
                if not first:
                    dve.wait_ge(yf_ready, n)
                V.tensor_tensor(u_y[:, :], u_c[0][:, :], u_c[1][:, :], ALU.mult).then_inc(y_made, 1)
                dve.wait_ge(y_made, n + 1)
                V.tensor_scalar(at_j(yf_hi, n), u_y[:, :], 1.0, None, ALU.mult).then_inc(yf_hi_ready, 1)
                dve.wait_ge(yf_hi_ready, n + 1)
                V.tensor_tensor(at_j(yf_lo, n), u_y[:, :], at_j(yf_hi, n).bitcast(F32), ALU.subtract)\
                    .then_inc(yf_ready, 1)

            pair(0, 0, True)
            pair(0, 1, False)
            with dve.Fori(1, KF // 2) as it:
                pair(it, 0, False)
                pair(it, 1, False)

            with dve.Fori(0, (N_DOWN - LEAD) // RING) as it:
                for c in range(RING):
                    split_at(Q_DOWN + it, c)

            for t in range(NT):
                gained(t, d_squared, g_postf_landed, g_postf, d_g, d_gained, x2_ready, 2)
                dve.wait_ge(d_gained, 2 * t + 2)
                dve.wait_ge(d_rs, t + 1)
                for b in range(2):
                    cols = slice(HALF * b, HALF * b + HALF)
                    V.scalar_tensor_tensor(out=x1[:, t, cols], in0=d_g[t % 2][:, cols], scalar=col(rs_c, 4 + 2 * t),
                                           in1=x1[:, t, cols], op0=ALU.mult, op1=ALU.add).then_inc(x2_ready, 1)

        @block.tensor
        def _(pe):
            M = nc.tensor.matmul

            def is0(j):
                return isinstance(j, int) and j == 0

            def block3(out, s, b, xh, xl, start, stop):
                M(out, w_hi[s][:, b, :], xh, start=start, stop=False)
                M(out, w_hi[s][:, b, :], xl, start=False, stop=False)
                return M(out, w_lo[s][:, b, :], xh, start=False, stop=stop)

            def blocks(c, out, hi, lo, k0=0, toks=slice(0, T), midway=None):
                for k in range(KD):
                    if midway is not None and k == KD // 2:
                        midway()
                    last = block3(out[:, toks], c % RING, k, hi[:, k0 + k, toks], lo[:, k0 + k, toks],
                                  k == 0, k == KD - 1)
                return last

            def product(q, c, out, hi, lo, k0=0):
                pe.wait_ge(lo_ready, 4 * q + c + 1)
                blocks(c, out, hi, lo, k0).then_inc(product_done, 1)

            def turn(src, scaled, turned, t):
                pe.wait_ge(scaled, t + 1)
                for b in range(2):
                    for k in range(4):
                        last = nc.tensor.transpose(bank[2 * t + b][:, P * k:P * k + P],
                                                   src[:, P * (4 * b + k):P * (4 * b + k) + P], ident[:, :])
                    last.then_inc(turned, 1)

            def in_halves(q, outs, hi, lo, ready, turned_tile, third_early):
                pe.wait_ge(ready, NT)
                for c in range(EARLY):
                    pe.wait_ge(lo_ready, 4 * q + c + 1)
                    early = third_early and c == 0
                    blocks(c, outs[c], hi, lo, toks=slice(0, HALF_T),
                           midway=(lambda: turned_tile(NT - 2)) if early else None)
                    if c < 2 and not early:
                        turned_tile(NT - 2 + c)
                pe.wait_ge(ready, 2 * NT)
                for c in range(EARLY):
                    blocks(c, outs[c], hi, lo, toks=slice(HALF_T, T)).then_inc(product_done, 1)

            pe.wait_ge(consts_made, CONSTS)
            def keep_warm(n):
                for _ in range(n):
                    M(bank[7][:, 0:P], ident[:, :], ident[:, :], start=True, stop=True)

            keep_warm(10)
            pe.wait_ge(ones_split, 1)
            turn(h_tm[0], h_scaled, h_turned, 0)
            keep_warm(8)
            turn(h_tm[1], h_scaled, h_turned, 1)
            keep_warm(8)
            in_halves(0, [bank[b] for b in (B_FZ, B_Q, B_V)], h_hi, h_lo, h_ready,
                      lambda t: turn(h_tm[t % 2], h_scaled, h_turned, t), False)

            def o_stage(j):
                pe.wait_ge(att_ready, j + 1)
                pe.wait_ge(att_far_ready, 3 * j + 3)
                pe.wait_ge(vtm_ready, j + 1)
                pe.wait_ge(q2_ready, j + 1)
                pe.wait_ge(s_ready, 3 * j + 3)
                if not is0(j):
                    pe.wait_ge(yb_scaled, j)
                for t in range(NT):
                    last = M(bank[B_O][:, P * t:P * t + P], v_tm[:, t, :], att[:, t, :], start=True, stop=(t == 0))
                    if t:
                        last = M(bank[B_O][:, P * t:P * t + P], s_all[:, t - 1, :], q_2[:, t - 1, :],
                                 start=False, stop=True)
                last.then_inc(o_done, 1)

            def o_sum(j):
                pe.wait_ge(osq_lo, j + 1)
                pe.wait_ge(i_ready, j + 1)
                M(bank[B_TR][:, :], ones_r[:, :], part_hi[:, :], start=True, stop=False)
                M(bank[B_TR][:, :], ones_r[:, :], part_lo[:, :], start=False, stop=True).then_inc(osum_done, 1)

            def gate(b, g):
                M(bank[b][:, :], lru_hi[:, g, :], part_hi[:, :], start=True, stop=False)
                M(bank[b][:, :], lru_hi[:, g, :], part_lo[:, :], start=False, stop=False)
                return M(bank[b][:, :], lru_lo[:, g, :], part_hi[:, :], start=False, stop=True)

            def head(i, pj, first):
                j = 2 * i + pj
                q, c = 3 * i, SECT * pj
                if not first:
                    pe.wait_ge(xa_read, j)
                    product(q, c, bank[B_FZ][:, :], h_hi, h_lo)
                    o_stage(j - 1)
                    pe.wait_ge(ga_read, j)
                    product(q, c + 1, bank[B_Q][:, :], h_hi, h_lo)
                    pe.wait_ge(sil_ready, j)
                    product(q, c + 2, bank[B_V][:, :], h_hi, h_lo)
                    o_sum(j - 1)
                pe.wait_ge(fz_read, j + 1)
                product(q, c + 3, bank[B_XA][:, :], h_hi, h_lo)
                pe.wait_ge(v_read, j + 1)
                if not first:
                    pe.wait_ge(rso_ln, j)
                for t in range(NT):
                    last = nc.tensor.transpose(bank[B_TR][:, P * t:P * t + P], v_fm[:, P * t:P * t + P], ident[:, :])
                last.then_inc(tv_done, 1)
                pe.wait_ge(kt_ready, j + 1)
                pe.wait_ge(qt_ready, j + 1)
                if not first:
                    pe.wait_ge(r_ready, j)
                for t in range(NT):
                    last = M(bank[B_ATT][:, P * t:P * t + P], f_b[:, P * t:P * t + P], q_t[:, P * t:P * t + P],
                             start=True, stop=True)
                pe.wait_ge(kd_ready, j + 1)
                if not first:
                    pe.wait_ge(att_far_ready, 3 * j)
                far = bank[B_ATT2][:, :].rearrange("p (l t c) -> p l t c", l=2, t=NT)
                odd = q_t[:, :].rearrange("p (t n e c) -> p t n e c", n=2, e=2, c=CH)
                for t in range(NT):
                    M(far[:, 0, t, :].rearrange("p (n c) -> p n c", c=CH), k_d[:, P * t:P * t + P],
                      odd[:, t, :, 1, :], start=True, stop=True)
                pe.wait_ge(q1_ready, j + 1)
                pe.wait_ge(k1_ready, j + 1)
                for t in range(NT):
                    last = M(far[0:2 * CH, 1, t, :], k_1[:, t, :], q_1[:, t, :], start=True, stop=True)
                last.then_inc(att_done, 1)
                pe.wait_ge(vtm_ready, j + 1)
                pe.wait_ge(k2_ready, j + 1)
                for t in range(NT - 1):
                    last = nc.tensor.transpose(bank[B_TR][:, P * t:P * t + P], k_2[:, t, :], ident[:, :])
                last.then_inc(tkd_done, 1)
                product(q, c + 4, bank[B_GA][:, :], h_hi, h_lo)
                pe.wait_ge(kdtm_ready, j + 1)
                if not first:
                    pe.wait_ge(s_ready, 3 * j)
                for t in range(NT - 1):
                    last = M(bank[B_KV][:, P * t:P * t + P], kd_tm[:, t, :], v_tm[:, t, :], start=True, stop=True)
                last.then_inc(kv_done, 1)
                product(q, c + 5, bank[B_OG][:, :], h_hi, h_lo)
                pe.wait_ge(gate_lo, 2 * j + 2)
                pe.wait_ge(att_ready, j + 1)
                gate(B_ATT, 0).then_inc(gate_r, 1)
                pe.wait_ge(kdtm_ready, j + 1)
                gate(B_TR, 1).then_inc(gate_i, 1)

            head(0, 0, True)
            head(0, 1, False)
            with pe.Fori(1, HEADS // 2) as i:
                head(i, 0, False)
                head(i, 1, False)

            q = Q_MERGE
            pe.wait_ge(xa_read, HEADS)
            product(q, 0, bank[0][:, :], h_hi, h_lo)
            o_stage(HEADS - 1)
            pe.wait_ge(sil_ready, HEADS)
            product(q, 1, bank[2][:, :], h_hi, h_lo)
            pe.wait_ge(att_far_ready, 3 * HEADS)
            product(q, 2, bank[B_ATT2][:, :], h_hi, h_lo)
            o_sum(HEADS - 1)
            pe.wait_ge(r_ready, HEADS)
            product(q, 3, bank[B_ATT][:, :], h_hi, h_lo)
            pe.wait_ge(ga_read, HEADS)
            pe.wait_ge(y_ready, 2 * HEADS - 1)
            product(q + 1, 0, bank[1][:, :], yy_hi, yy_lo)
            pe.wait_ge(y_ready, 2 * HEADS)
            pe.wait_ge(s_ready, 3 * HEADS)
            product(q + 1, 1, bank[4][:, :], yy_hi, yy_lo, k0=KD)
            pe.wait_ge(za_read, 1)
            product(q + 1, 2, bank[1][:, :], yy_hi, yy_lo)
            pe.wait_ge(zb_read, 1)
            product(q + 1, 3, bank[4][:, :], yy_hi, yy_lo, k0=KD)
            with pe.Fori(2, KD) as m:
                q = Q_MERGE + m
                pe.wait_ge(sig_a, m)
                product(q, 0, bank[0][:, :], h_hi, h_lo)
                pe.wait_ge(sig_b, m)
                product(q, 1, bank[2][:, :], h_hi, h_lo)
                pe.wait_ge(za_read, m)
                product(q, 2, bank[1][:, :], yy_hi, yy_lo)
                pe.wait_ge(zb_read, m)
                product(q, 3, bank[4][:, :], yy_hi, yy_lo, k0=KD)

            def token_major(q0, n_k, yh, yl, y_sem, tile_done, banks_free, in_tile):
                def step(k, t, halves):
                    s = k % RING
                    toks = slice(P * t, P * t + P)
                    for x, ws in ((yh, (w_hi, w_lo)), (yl, (w_hi,))):
                        for w in ws:
                            for b in halves:
                                last = M(bank[2 * t + b][:, :], x[:, k, toks], w[s][:, 4 * b:4 * b + 4, :]
                                         .rearrange("p a c -> p (a c)"), start=(k == 0 and w is w_hi and x is yh),
                                         stop=(k == n_k - 1 and x is yl))
                    return last

                def landed(k):
                    pe.wait_ge(lo_ready, RING * q0 + k + 1)
                    pe.wait_ge(y_sem, k + 1)

                for k in range(n_k - RING):
                    landed(k)
                    for t in range(NT):
                        if k == 0:
                            banks_free(t)
                        last = step(k, t, (0, 1))
                    last.then_inc(product_done, 1)
                for t in range(NT):
                    k = n_k - RING
                    if t == 0:
                        landed(k)
                    last = step(k, t, (0, 1))
                    if t == NT - 1:
                        last.then_inc(product_done, 1)
                    for b in range(2):
                        for k in range(n_k - RING + 1, n_k):
                            if t == 0 and b == 0:
                                landed(k)
                            last = step(k, t, (b,))
                            if t == NT - 1 and b == 1 and k < n_k - 1:
                                last.then_inc(product_done, 1)
                            if b == 0 and k == n_k - RING + 1:
                                in_tile(t)
                        last.then_inc(tile_done, 1)
                    if t == NT - 1:
                        pe.wait_ge(tile_done, 2 * NT)
                        pe.sem_inc(product_done, 1)

            def merge_banks(t):
                if t == 0:
                    pe.wait_ge(sig_a, KD)
                    pe.wait_ge(za_read, KD)
                elif t == 1:
                    pe.wait_ge(sig_b, KD)
                elif t == 2:
                    pe.wait_ge(zb_read, KD)
                else:
                    pe.wait_ge(yb_scaled, HEADS)

            def turn_h2(t):
                pe.wait_ge(o_gained, 2 * t + 2)
                turn(h2_tm[t % 2], h2_scaled, h2_turned, t)

            token_major(Q_OUT, N_OUT, mix_hi, mix_lo, mix_ready, o_tile, merge_banks,
                        lambda t: turn_h2(t - 2) if t >= 2 else None)

            in_halves(Q_UP, bank, g_hi, g_lo, h2_ready, turn_h2, True)
            for c in range(EARLY, RING):
                product(Q_UP, c, bank[c][:, :], g_hi, g_lo)
            with pe.Fori(1, KF // 2) as it:
                for c in range(RING):
                    pe.wait_ge(tap2, 4 * it + c - 3)
                    product(Q_UP + it, c, bank[c][:, :], g_hi, g_lo)

            token_major(Q_DOWN, N_DOWN, yf_hi, yf_lo, yf_ready, d_tile_done,
                        lambda t: pe.wait_ge(tap2, min(N_UP, N_UP - 2 + 2 * t)), lambda t: None)


_NAMES = ["x", "norm_pre_mix", "w_in", "conv_a_w", "conv_a_b", "lru_wa", "lru_ba", "lru_wx", "lru_bx",
          "lru_lambda", "hg_lb_logits", "hg_norm_g", "w_branch_a", "w_branch_b", "w_out", "norm_post_mix",
          "norm_pre_ffn", "w_up", "conv_f_w", "conv_f_b", "w_down", "norm_post_ffn"]


def _blocks(w):
    n = w.shape[1] // P
    return w.reshape(KD, P, n, P).transpose(2, 1, 0, 3).reshape(n, P, KD * P)


def kernel(**inputs):
    import numpy as np
    import concourse.bacc as bacc
    from concourse.bass_utils import run_bass_kernel_spmd

    a = {n: np.asarray(inputs[n]) for n in _NAMES}
    w_in = _blocks(a["w_in"][0]).reshape(8, KD, P, KD * P)
    heads = w_in[[3, 2, 4, 0, 1, 5]].transpose(1, 0, 2, 3).reshape(N_HEAD, P, KD * P)
    merge = np.stack([w_in[6], w_in[7], _blocks(a["w_branch_a"][0]), _blocks(a["w_branch_b"][0])], 1)
    merge[0:2] = merge[0:2].reshape(2, 2, 2, P, KD * P).transpose(1, 0, 2, 3, 4).reshape(2, 4, P, KD * P)
    up = _blocks(a["w_up"][0]).reshape(2, KF, P, KD * P).transpose(1, 0, 2, 3)
    wts = np.concatenate([heads, merge.reshape(N_MERGE, P, KD * P), a["w_out"][0].reshape(N_OUT, P, D),
                          up.reshape(N_UP, P, KD * P), a["w_down"][0].reshape(N_DOWN, P, KD * P)])
    cols = lambda v: v.reshape(-1, P).T
    per_head = [a["conv_a_w"][0][t] for t in range(4)] + [a["conv_a_b"][0], a["lru_ba"][0], a["lru_bx"][0],
                a["lru_lambda"][0], a["hg_lb_logits"][0], a["hg_lb_logits"][1], a["hg_norm_g"][0]]
    per_up = [a["conv_f_w"][0][t] for t in range(3)] + [a["conv_f_b"][0]]
    ffn = np.stack([cols(v).reshape(P, 2, KF) for v in per_up], 3).transpose(0, 2, 1, 3).reshape(P, -1)
    par = np.concatenate([np.stack([cols(v) for v in per_head], 2).reshape(P, -1), ffn], 1)
    gains = np.stack([a[n][0] for n in ("norm_pre_mix", "norm_post_mix", "norm_pre_ffn", "norm_post_ffn")])
    lru = np.stack([a["lru_wa"][0], a["lru_wx"][0]], 2).reshape(HEADS, P, 2 * P)

    nc = bacc.Bacc("TRN2", target_bir_lowering=False, num_devices=1)
    arrays = {"x": a["x"][0], "weights": wts, "params": np.ascontiguousarray(par),
              "lru_w": np.ascontiguousarray(lru), "gains": gains}
    arrays = {f"{n}_dram": np.ascontiguousarray(v) for n, v in arrays.items()}
    args = [nc.dram_tensor(n, v.shape, mybir.dt.from_np(v.dtype), kind="ExternalInput").ap()
            for n, v in arrays.items()]
    out = nc.dram_tensor("out_dram", (T, D), F32, kind="ExternalOutput").ap()
    layer(nc, *args, out)
    r = run_bass_kernel_spmd(nc, [arrays], core_ids=[0])
    return np.asarray(r.results[0]["out_dram"]).reshape(1, T, D)
```
